# Optimizing a Trainium2 kernel written in Bass

```python
import math
import jax, jax.numpy as jnp
from jax import lax
import numpy as np

D_MODEL = 1024
BATCH = 1
SEQ = 512
DEPTH = 2
DEC_BATCH = 8
DEC_SEQ = 1
PAST_LEN = 4096
PAGE_SIZE = 128

N_ATT_LAYERS = (DEPTH + 1) // 2
N_CONV_LAYERS = DEPTH // 2
ATT_WIDTH = D_MODEL // 2
N_ATT_HEADS = 4
ATT_HD = ATT_WIDTH // (2 * N_ATT_HEADS)
Q_BLOCK = 128
N_BUCKETS = 32
MAX_DISTANCE = 128
RG_WIDTH = D_MODEL // 2
RG_BLOCKS = 8
RG_BD = RG_WIDTH // RG_BLOCKS
RG_CONV = 4
RG_C = 8.0
SC_WIDTH = D_MODEL
SC_CONV = 3
N_KEYS = 128
N_EXPERTS = N_KEYS * N_KEYS
PEER_HEADS = 8
PEER_KDIM = 256
PEER_TOPK = 16
PEER_BLOCK = 256
EPS = 1e-6
SPLIT_A = (ATT_WIDTH, 2 * ATT_WIDTH, 3 * ATT_WIDTH, 3 * ATT_WIDTH + RG_WIDTH)
IN_A_WIDTH = 3 * ATT_WIDTH + 2 * RG_WIDTH

kernel_name = "hybrid_diffattn_rglru_shortconv_peer_step"

def lambda_init(layer):
    return 0.8 - 0.6 * math.exp(-0.3 * layer)

def rmsnorm(x, g):
    xf = x.astype(jnp.float32)
    y = xf * lax.rsqrt(jnp.mean(xf * xf, axis=-1, keepdims=True) + EPS)
    return (y * g.astype(jnp.float32)).astype(x.dtype)

def t5_bucket(dist):
    max_exact = N_BUCKETS // 2
    n = jnp.maximum(dist, 0)
    nf = jnp.maximum(n, 1).astype(jnp.float32)
    far = max_exact + (jnp.log(nf / max_exact) / math.log(MAX_DISTANCE / max_exact)
                       * (N_BUCKETS - max_exact)).astype(jnp.int32)
    return jnp.where(n < max_exact, n, jnp.minimum(far, N_BUCKETS - 1))

def rel_bias_for(rel_bias, dist):
    return jnp.moveaxis(rel_bias[t5_bucket(dist)], -1, 0).astype(jnp.float32)

def diff_lambda(lq1, lk1, lq2, lk2, lam_init):
    f32 = jnp.float32
    return (jnp.exp(jnp.sum(lq1.astype(f32) * lk1.astype(f32)))
            - jnp.exp(jnp.sum(lq2.astype(f32) * lk2.astype(f32))) + lam_init)

def diff_weights(logits, lam):
    p = jax.nn.softmax(logits, axis=-1)
    return p[:, :, 0] - lam * p[:, :, 1]

def diff_attn_prompt(q, k, v, rel_bias, lam):
    b, s = q.shape[0], q.shape[1]
    nblk = s // Q_BLOCK
    scale = ATT_HD ** -0.5
    qb = jnp.moveaxis(q.reshape(b, nblk, Q_BLOCK, N_ATT_HEADS, 2, ATT_HD), 1, 0)
    kpos = jnp.arange(s, dtype=jnp.int32)

    def block(args):
        qi, i = args
        qpos = i * Q_BLOCK + jnp.arange(Q_BLOCK, dtype=jnp.int32)
        dist = qpos[:, None] - kpos[None, :]
        logits = jnp.einsum('bqhcd,bkhcd->bhcqk', qi, k).astype(jnp.float32) * scale
        logits = logits + rel_bias_for(rel_bias, dist)[None, :, None]
        logits = jnp.where(dist >= 0, logits, -jnp.inf)
        w = diff_weights(logits, lam).astype(v.dtype)
        return jnp.einsum('bhqk,bkhe->bqhe', w, v)

    out = lax.map(block, (qb, jnp.arange(nblk, dtype=jnp.int32)))
    return jnp.moveaxis(out, 0, 1).reshape(b, s, N_ATT_HEADS, 2 * ATT_HD)

def diff_attn_sample(q, k_new, v_new, k_past, v_past, rel_bias, lam):
    t, p = q.shape[1], k_past.shape[1]
    scale = ATT_HD ** -0.5
    qpos = p + jnp.arange(t, dtype=jnp.int32)
    dist_past = qpos[:, None] - jnp.arange(p, dtype=jnp.int32)[None, :]
    dist_new = qpos[:, None] - qpos[None, :]
    lp = (jnp.einsum('bqhcd,bkhcd->bhcqk', q, k_past).astype(jnp.float32) * scale
          + rel_bias_for(rel_bias, dist_past)[None, :, None])
    ln = (jnp.einsum('bqhcd,bkhcd->bhcqk', q, k_new).astype(jnp.float32) * scale
          + rel_bias_for(rel_bias, dist_new)[None, :, None])
    ln = jnp.where(dist_new >= 0, ln, -jnp.inf)
    w = diff_weights(jnp.concatenate([lp, ln], axis=-1), lam).astype(v_new.dtype)
    return (jnp.einsum('bhqk,bkhe->bqhe', w[..., :p], v_past)
            + jnp.einsum('bhqk,bkhe->bqhe', w[..., p:], v_new))

def causal_dwconv(x, buf, w, b=None):
    width, t = w.shape[0], x.shape[1]
    xp = jnp.concatenate([buf.astype(x.dtype), x], axis=1)
    y = xp[:, 0:t] * w[0]
    for i in range(1, width):
        y = y + xp[:, i:i + t] * w[i]
    if b is not None:
        y = y + b
    return y, xp[:, t:]

def rglru(xc, h0, wa, ba, wi, bi, lam):
    f32 = jnp.float32
    b, t, _ = xc.shape
    xf = xc.astype(f32)
    xb = xf.reshape(b, t, RG_BLOCKS, RG_BD)
    r = jax.nn.sigmoid(jnp.einsum('btnd,nde->btne', xb, wa.astype(f32)).reshape(b, t, RG_WIDTH) + ba.astype(f32))
    i = jax.nn.sigmoid(jnp.einsum('btnd,nde->btne', xb, wi.astype(f32)).reshape(b, t, RG_WIDTH) + bi.astype(f32))
    log_a = -RG_C * r * jax.nn.softplus(-lam.astype(f32))
    a = jnp.exp(log_a)
    u = jnp.sqrt(-jnp.expm1(2.0 * log_a)) * (i * xf)
    u = u.at[:, 0].add(a[:, 0] * h0.astype(f32))

    def combine(c1, c2):
        return c1[0] * c2[0], c2[0] * c1[1] + c2[1]

    _, h = lax.associative_scan(combine, (a, u), axis=1)
    return h.astype(xc.dtype), h[:, -1].astype(xc.dtype)

def peer(x, w_q, sub_keys, u_tab, v_tab):
    shp = x.shape
    xf = x.reshape(-1, D_MODEL)
    n_tok = xf.shape[0]
    blk = min(PEER_BLOCK, n_tok)
    nblk = -(-n_tok // blk)
    xf = jnp.pad(xf, ((0, nblk * blk - n_tok), (0, 0)))

    def one(xb):
        q = (xb @ w_q).reshape(blk, PEER_HEADS, 2, PEER_KDIM // 2)
        s = jnp.einsum('thcd,hcnd->thcn', q, sub_keys).astype(jnp.float32)
        s1, i1 = lax.top_k(s[:, :, 0], PEER_TOPK)
        s2, i2 = lax.top_k(s[:, :, 1], PEER_TOPK)
        cand = (s1[..., :, None] + s2[..., None, :]).reshape(blk, PEER_HEADS, PEER_TOPK * PEER_TOPK)
        sc, ci = lax.top_k(cand, PEER_TOPK)
        e1 = jnp.take_along_axis(i1, ci // PEER_TOPK, axis=-1)
        e2 = jnp.take_along_axis(i2, ci % PEER_TOPK, axis=-1)
        eidx = e1 * N_KEYS + e2
        g = jax.nn.softmax(sc, axis=-1)
        act = jax.nn.gelu(jnp.einsum('td,thkd->thk', xb, u_tab[eidx]).astype(jnp.float32))
        coef = (g * act).astype(xb.dtype)
        return jnp.einsum('thk,thkd->td', coef, v_tab[eidx])

    y = lax.map(one, xf.reshape(nblk, blk, D_MODEL))
    return y.reshape(-1, D_MODEL)[:n_tok].reshape(shp)

def setup_inputs(seed: int = 0) -> dict:
    key = jax.random.key(seed)
    ks = iter(jax.random.split(key, 48))
    f32 = jnp.float32

    def nrm(shape, scale):
        return jax.random.normal(next(ks), shape, f32) * scale

    def gain(shape):
        return 1.0 + nrm(shape, 0.05)

    n_pages = PAST_LEN // PAGE_SIZE
    n_used = DEC_BATCH * n_pages
    n_phys = n_used + (n_used + 3) // 4
    perm = jax.random.permutation(next(ks), n_phys).astype(jnp.int32)
    page_table = perm[:n_used].reshape(DEC_BATCH, n_pages)
    a_c = jax.random.uniform(next(ks), (N_ATT_LAYERS, RG_WIDTH), f32, 0.9, 0.999)
    s = a_c ** (1.0 / RG_C)
    rg_lambda = jnp.log(s) - jnp.log1p(-s)
    kv_shape = (N_ATT_LAYERS, n_phys, PAGE_SIZE, N_ATT_HEADS, 2 * ATT_HD)
    return {
        "x_prompt": nrm((BATCH, SEQ, D_MODEL), 1.0),
        "x_sample": nrm((DEC_BATCH, DEC_SEQ, D_MODEL), 1.0),
        "cache_k": nrm(kv_shape, 1.0),
        "cache_v": nrm(kv_shape, 1.0),
        "page_table": page_table,
        "state_rglru_h": nrm((N_ATT_LAYERS, DEC_BATCH, RG_WIDTH), 0.5),
        "state_rglru_conv": nrm((N_ATT_LAYERS, DEC_BATCH, RG_CONV - 1, RG_WIDTH), 1.0),
        "state_sconv": nrm((N_CONV_LAYERS, DEC_BATCH, SC_CONV - 1, SC_WIDTH), 1.0),
        "rel_bias": nrm((N_BUCKETS, N_ATT_HEADS), 0.5),
        "norm_mix": gain((DEPTH, D_MODEL)),
        "norm_ffn": gain((DEPTH, D_MODEL)),
        "norm_final": gain((D_MODEL,)),
        "w_in_a": nrm((N_ATT_LAYERS, D_MODEL, IN_A_WIDTH), D_MODEL ** -0.5),
        "w_out_a": nrm((N_ATT_LAYERS, ATT_WIDTH + RG_WIDTH, D_MODEL), (ATT_WIDTH + RG_WIDTH) ** -0.5),
        "lambda_q1": nrm((N_ATT_LAYERS, ATT_HD), 0.1),
        "lambda_k1": nrm((N_ATT_LAYERS, ATT_HD), 0.1),
        "lambda_q2": nrm((N_ATT_LAYERS, ATT_HD), 0.1),
        "lambda_k2": nrm((N_ATT_LAYERS, ATT_HD), 0.1),
        "subln_g": gain((N_ATT_LAYERS, 2 * ATT_HD)),
        "rg_conv_w": nrm((N_ATT_LAYERS, RG_CONV, RG_WIDTH), RG_CONV ** -0.5),
        "rg_conv_b": nrm((N_ATT_LAYERS, RG_WIDTH), 0.02),
        "rg_wa": nrm((N_ATT_LAYERS, RG_BLOCKS, RG_BD, RG_BD), RG_BD ** -0.5),
        "rg_ba": nrm((N_ATT_LAYERS, RG_WIDTH), 0.1),
        "rg_wi": nrm((N_ATT_LAYERS, RG_BLOCKS, RG_BD, RG_BD), RG_BD ** -0.5),
        "rg_bi": nrm((N_ATT_LAYERS, RG_WIDTH), 0.1),
        "rg_lambda": rg_lambda,
        "w_in_c": nrm((N_CONV_LAYERS, D_MODEL, 3 * SC_WIDTH), D_MODEL ** -0.5),
        "sc_conv_w": nrm((N_CONV_LAYERS, SC_CONV, SC_WIDTH), SC_CONV ** -0.5),
        "w_out_c": nrm((N_CONV_LAYERS, SC_WIDTH, D_MODEL), SC_WIDTH ** -0.5),
        "peer_wq": nrm((DEPTH, D_MODEL, PEER_HEADS * PEER_KDIM), D_MODEL ** -0.5),
        "peer_keys": nrm((DEPTH, PEER_HEADS, 2, N_KEYS, PEER_KDIM // 2), (PEER_KDIM // 2) ** -0.5),
        "peer_u": nrm((DEPTH, N_EXPERTS, D_MODEL), D_MODEL ** -0.5),
        "peer_v": nrm((DEPTH, N_EXPERTS, D_MODEL), 0.5 / math.sqrt(PEER_HEADS)),
    }

def reference(x_prompt, x_sample, cache_k, cache_v, page_table, state_rglru_h, state_rglru_conv, state_sconv,
              rel_bias, norm_mix, norm_ffn, norm_final,
              w_in_a, w_out_a, lambda_q1, lambda_k1, lambda_q2, lambda_k2, subln_g,
              rg_conv_w, rg_conv_b, rg_wa, rg_ba, rg_wi, rg_bi, rg_lambda,
              w_in_c, sc_conv_w, w_out_c,
              peer_wq, peer_keys, peer_u, peer_v):

    def run(x, is_sample):
        nb, t = x.shape[0], x.shape[1]
        ks, vs, hs, rbufs, sbufs = [], [], [], [], []
        for l in range(DEPTH):
            j = l // 2
            h = rmsnorm(x, norm_mix[l])
            if l % 2 == 0:
                z = h @ w_in_a[j]
                q, k, v, xr, gr = jnp.split(z, SPLIT_A, axis=-1)
                q = q.reshape(nb, t, N_ATT_HEADS, 2, ATT_HD)
                k = k.reshape(nb, t, N_ATT_HEADS, 2, ATT_HD)
                v = v.reshape(nb, t, N_ATT_HEADS, 2 * ATT_HD)
                lam = diff_lambda(lambda_q1[j], lambda_k1[j], lambda_q2[j], lambda_k2[j], lambda_init(l))
                if is_sample:
                    k_past = cache_k[j, page_table].reshape(nb, -1, N_ATT_HEADS, 2, ATT_HD)
                    v_past = cache_v[j, page_table].reshape(nb, -1, N_ATT_HEADS, 2 * ATT_HD)
                    o = diff_attn_sample(q, k, v, k_past, v_past, rel_bias, lam)
                    buf0 = state_rglru_conv[j]
                    h0 = state_rglru_h[j]
                else:
                    o = diff_attn_prompt(q, k, v, rel_bias, lam)
                    buf0 = jnp.zeros((nb, RG_CONV - 1, RG_WIDTH), x.dtype)
                    h0 = jnp.zeros((nb, RG_WIDTH), x.dtype)
                o = rmsnorm(o, subln_g[j]) * (1.0 - lambda_init(l))
                xc, rbuf = causal_dwconv(xr, buf0, rg_conv_w[j], rg_conv_b[j])
                hr, h_last = rglru(xc, h0, rg_wa[j], rg_ba[j], rg_wi[j], rg_bi[j], rg_lambda[j])
                rg = hr * jax.nn.gelu(gr)
                mix = jnp.concatenate([o.reshape(nb, t, ATT_WIDTH), rg], axis=-1) @ w_out_a[j]
                ks.append(k.reshape(nb, t, N_ATT_HEADS, 2 * ATT_HD))
                vs.append(v)
                hs.append(h_last)
                rbufs.append(rbuf)
            else:
                z = h @ w_in_c[j]
                bg, cg, xs = jnp.split(z, 3, axis=-1)
                if is_sample:
                    buf0 = state_sconv[j]
                else:
                    buf0 = jnp.zeros((nb, SC_CONV - 1, SC_WIDTH), x.dtype)
                cv, sbuf = causal_dwconv(cg * xs, buf0, sc_conv_w[j])
                mix = (bg * cv) @ w_out_c[j]
                sbufs.append(sbuf)
            x = x + mix
            x = x + peer(rmsnorm(x, norm_ffn[l]), peer_wq[l], peer_keys[l], peer_u[l], peer_v[l])
        return (rmsnorm(x, norm_final), jnp.stack(ks), jnp.stack(vs), jnp.stack(hs),
                jnp.stack(rbufs), jnp.stack(sbufs))

    y_prompt, k_prompt, v_prompt, h_prompt, rgconv_prompt, sconv_prompt = run(x_prompt, False)
    y_sample, k_sample, v_sample, h_sample, rgconv_sample, sconv_sample = run(x_sample, True)
    return (y_prompt, y_sample, k_prompt, v_prompt, k_sample, v_sample, h_prompt, h_sample,
            rgconv_prompt, rgconv_sample, sconv_prompt, sconv_sample)


_drawn_inputs = setup_inputs


def setup_inputs(seed=0):
    import zlib

    import numpy as np

    out = dict(_drawn_inputs(seed))
    spreads = {}
    factors = {}
    for name, (base, spread) in spreads.items():
        noise = np.random.default_rng([zlib.crc32(name.encode()), seed]).standard_normal(out[name].shape)
        drawn = base * np.exp(spread * noise) if base else spread * noise
        out[name] = __import__('jax').numpy.asarray(drawn.astype(out[name].dtype))
    for name, factor in factors.items():
        out[name] = (out[name] * factor).astype(out[name].dtype)
    return out
```

```python
import math
from contextlib import ExitStack

import concourse.bass as bass
import numpy as np
from concourse import mybir

F32 = mybir.dt.float32
I32 = mybir.dt.int32
U32 = mybir.dt.uint32
ALU = mybir.AluOpType
ACT = mybir.ActivationFunctionType
AX = mybir.AxisListType

P = 128
D = 1024
KD = D // P
SEQ = 512
TILES = SEQ // P
DEC = 8
TOK = SEQ + DEC
HALF = TOK // 2
HEADS = 4
HD = 64
AW = 512
PAST = 4096
PAGES = PAST // P
NPHYS = 320
RB = 4
RGC = 4
SCC = 3
BUCKETS = 32
PH = 8
TOPK = 16
NKEY = 128
NEXP = NKEY * NKEY
HC = 2 * PH
SEL = PH * TOPK
EPS = 1e-6
LOW = -3.0e38
MASK = -1.0e30
LAM0 = 0.8 - 0.6 * math.exp(0.0)
BLK = 512
PG = 4
PSLOTS = 4
GSLOTS = 8
GBODY = 2 * GSLOTS
LAST = SEL // GBODY

PRM = dict(conv_w=0, conv_b=16, ba=20, bi=24, lam=28, subln=32, sconv=33)
NPRM = 33 + KD * SCC


def bucket(dist):
    exact = BUCKETS // 2
    n = np.maximum(dist, 0)
    nf = np.maximum(n, 1).astype(np.float32)
    far = exact + (np.log(nf / np.float32(exact)) / np.float32(math.log(128 / exact))
                   * np.float32(BUCKETS - exact)).astype(np.int32)
    return np.where(n < exact, n, np.minimum(far, BUCKETS - 1))


def shape_constants():
    w = 2 * SEQ
    j = np.arange(SEQ + P - 1)
    oh = np.zeros((BUCKETS + 1, SEQ + P - 1), np.float32)
    dist = SEQ - 1 - j
    ok = dist >= 0
    oh[bucket(dist)[ok], j[ok]] = 1.0
    oh[BUCKETS, ~ok] = 1.0
    back = PAST - np.arange(PAST)
    b = bucket(back)
    assert (b[:-P] == BUCKETS - 1).all()
    ohd = np.zeros((BUCKETS, 2, P), np.float32)
    ohd[BUCKETS - 1, 0, :] = 1.0
    ohd[b[-P:], 1, np.arange(P)] = 1.0
    ident = np.eye(P, dtype=np.float32)
    sel = np.zeros((DEC, DEC, P), np.float32)
    for i in range(DEC):
        sel[i, i] = 1.0
    part = np.arange(P)
    rep = (part[None, :] // TOPK == np.arange(DEC)[:, None]).astype(np.float32)
    small = np.zeros((P, 16 + 16 + DEC), np.float32)
    small[:, 0:16] = np.arange(16)
    small[:, 16:32] = part[:, None] % TOPK == np.arange(16)[None, :]
    small[:, 32:32 + DEC] = part[:, None] // TOPK == np.arange(DEC)[None, :]
    return {"c_oh": oh, "c_ohd": ohd, "c_ident": ident, "c_sel": sel, "c_rep": rep, "c_small": small}


class Chain:

    def __init__(self, eng, sem):
        self.eng, self.sem, self.n = eng, sem, 0

    def __call__(self, ins):
        self.n += 1
        ins.then_inc(self.sem, 1)
        self.eng.wait_ge(self.sem, self.n)

    def clear(self):
        self.eng.sem_clear(self.sem)
        self.n = 0


def wait_apart(eng, go, sem, value):
    eng.wait_ge(sem, value)
    eng.sem_inc(go, 1)


def rows(t):
    return P if t < TILES else DEC


def cols(t):
    return slice(t * P, t * P + rows(t))


def build(nc, ins, outs):
    with ExitStack() as ctx:
        program(nc, ins, outs, ctx)


def program(nc, ins, outs, ctx):
    def sb(name, shape, dt=F32):
        return ctx.enter_context(nc.sbuf_tensor(name, shape, dt))

    def sem(name):
        return ctx.enter_context(nc.semaphore(name))

    xs = sb("xs", [P, TILES + 1, D])
    hn = sb("hn", [P, TILES + 1, D])
    hT = sb("hT", [P, KD, TOK])
    wr = sb("wr", [P, 2, KD, BLK])
    gain = sb("gain", [P, D])
    junk = sb("junk", [P, D])
    ident = sb("ident", [P, P])
    ones = sb("ones", [P, P])
    selb = sb("selb", [DEC, DEC, P])
    rep = sb("rep", [DEC, P])
    small = sb("small", [P, 16 + 16 + DEC])
    prm = sb("prm", [P, NPRM])
    lamv = sb("lamv", [P, 4, HD])
    h0s = sb("h0s", [P, RB, DEC])
    st = sb("st", [P, 64])
    kq = sb("kq", [P, 160])
    AREA = 26400
    area = sb("area", [P, AREA])

    def at(off, *shape):
        n = math.prod(shape)
        assert off + n <= AREA, (off, shape)
        v = area[:, off:off + n]
        if len(shape) == 2:
            v = v.rearrange("p (a b) -> p a b", a=shape[0])
        elif len(shape) == 3:
            v = v.rearrange("p (a b c) -> p a b c", a=shape[0], b=shape[1])
        return v

    cat = hT
    z = at(0, TILES + 1, 3 * AW)
    qT = at(7680, HEADS, SEQ)
    kT = at(9728, HEADS, SEQ)
    xp = at(11776, RB, SEQ + RGC - 1)
    xd = at(13836, RB, DEC, RGC)
    grT = at(13964, RB, TOK)
    s = at(16044, DEC, PAGES + 1, 8)
    pages = at(18156, PSLOTS, PG, AW)
    qb = hn[:, 0:TILES, :].rearrange("p t c -> p (t c)").rearrange("p (b c) -> p b c", b=DEC)
    bias = at(18156, HEADS, SEQ)
    lg = at(20204, 2, SEQ)
    wt = at(21228, SEQ)
    pT = at(21740, SEQ)
    sq = at(22252, SEQ)
    rs = at(22764, SEQ)
    wide = at(23276, SEQ + P - 1)
    ohs = area[0:BUCKETS + 1, 23920:23920 + SEQ + P - 1]
    rbx = area[0:BUCKETS + 1, 24600:24600 + HEADS]
    rbw = area[0:BUCKETS + 1, 24620:24620 + P]
    bd = hn[:, TILES, 0:2 * 8].rearrange("p (a b) -> p a b", a=2)
    ohd = hn[0:BUCKETS, TILES, 128:128 + 2 * P].rearrange("p (a b) -> p a b", a=2)
    rbs = hn[0:BUCKETS, TILES, 400:404]
    rb0 = hn[0:DEC, TILES, 408:412]
    snew = hn[0:DEC, TILES, 512:1024]
    sn8 = hn[0:DEC, TILES, 416:424]
    sdg = hn[0:DEC, TILES, 432:496]
    xc = at(0, RB, TOK)
    gr_ = at(2080, RB, TOK)
    gi_ = at(4160, RB, TOK)
    ua = at(6240, RB, TOK)
    ub = at(8320, RB, TOK)
    hs = at(18156, RB, TOK)
    gg = at(20236, RB, TOK)
    wab = at(22316, 2, RB, P)
    cgT = at(0, KD, TOK)
    cxp = at(4160, KD, SEQ + SCC - 1)
    cxd = at(8272, KD, DEC, SCC)
    bgT = at(8464, KD, TOK)
    cvT = at(12624, KD, TOK)
    pq = at(0, HC, TOK)
    keys = at(8320, HC, NKEY)
    sc = at(10368, HC, NKEY)
    sc2 = at(12416, 256)
    v16 = at(12672, HC, TOPK)
    i16 = area[:, 12928:13184].bitcast(U32).rearrange("p (a b) -> p a b", a=HC)
    i16f = at(13184, HC, TOPK)
    cand = at(13440, PH, 256)
    s16 = at(15488, PH, TOPK)
    c16 = area[:, 15616:15744].bitcast(U32)
    chi = area[:, 15744:15872].bitcast(U32)
    clo = area[:, 15872:16000].bitcast(U32)
    hif = at(16000, SEL)
    lof = at(16128, SEL)
    e1f = at(16256, SEL)
    e2f = at(16384, 2, SEL)
    gsum = at(16640, PH)
    eix = area[:, 16768:16768 + TILES * SEL].bitcast(I32).rearrange("p (a b) -> p a b", a=TILES)
    gt = at(17280, TILES, SEL)
    dots = at(17792, SEL)
    coef = at(17920, SEL)
    d16 = at(18048, GBODY)
    ixs = area[:, 18064:18064 + 2 * GSLOTS].bitcast(I32)
    ring = at(18080, GSLOTS, D)
    xrep = at(10368, D)
    dsel = at(11400, 2, PH, TOPK)
    dex = at(11660, 2 * PH)
    dix = area[:, 11680:11688].bitcast(I32)
    ddot = at(11690, PH)
    dcf = at(11700, PH)
    dw = at(11720, PH, DEC)

    ps = [ctx.enter_context(nc.psum_tensor(f"ps{i}", [P, 512], F32)) for i in range(8)]

    go = sem("go")
    consts = sem("consts")
    xland = sem("xland")
    gland = sem("gland")
    gused = sem("gused")
    normed = sem("normed")
    dve_s, act_s, pool_s = sem("dve_s"), sem("act_s"), sem("pool_s")
    wland = [sem("wland0"), sem("wland1")]
    wused = sem("wused")
    aready, afree = sem("aready"), sem("afree")
    vready, vfree = sem("vready"), sem("vfree")
    stored = sem("stored")
    mixin = sem("mixin")
    rgst = sem("rgst")
    tpost = sem("tpost")
    kfree = sem("kfree")
    kland = [sem(f"kland{i}") for i in range(PSLOTS)]
    kdone = sem("kdone")
    pt_ = sem("pt_")
    toepl = sem("toepl")
    attn = sem("attn")
    asm_ = sem("asm_")
    acts = sem("acts")
    scored = sem("scored")
    scfree = sem("scfree")
    chosen = sem("chosen")
    expd = sem("expd")
    rland = [sem(f"rland{i}") for i in range(GSLOTS)]
    rfree = sem("rfree")
    dexs = sem("dexs")
    keyl = sem("keyl")
    dotd = sem("dotd")
    geld = sem("geld")
    decs = sem("decs")
    repd = sem("repd")
    peerd = sem("peerd")
    sconst = sem("sconst")
    meansq, rstd, dnorm = sem("meansq"), sem("rstd"), sem("dnorm")
    headq, headd = sem("headq"), sem("headd")
    lamq, lamd, hland = sem("lamq"), sem("lamd"), sem("hland")

    block = ctx.enter_context(nc.Block())

    W_ORDER = [("w_in_a", j) for j in range(5)] + [("w_out_a", j) for j in range(2)] + \
              [("wq0", j) for j in range(4)] + [("w_in_c", j) for j in (2, 3, 4, 5, 0, 1)] + \
              [("w_out_c", j) for j in range(2)] + [("wq1", j) for j in range(4)]

    A_QB = 2 * (TILES + 1) + 3 * (TILES + 1) + 2 * 2 * RB + 2 * TILES + DEC + 1
    A_PEER = 2 * (TILES + 1) + 2 * HC + 4 * (TILES + 1) + 2
    A_CG = A_QB + 2 * HEADS + 2 * HEADS * TILES + 4 * RB + A_PEER + 2 * (TILES + 1) + 2 * KD
    A_BG = A_CG + 2 * KD

    n_stores = [0]

    @block.sync
    def _(sp):
        for c, v in (("c_ident", ident[:, :]), ("c_sel", selb[:, :, :]), ("c_rep", rep[:, :]),
                     ("c_small", small[:, :]), ("prm", prm[:, :])):
            sp.dma_start(v, ins[c]).then_inc(consts, 16)
        for i, n in enumerate(("lambda_q1", "lambda_k1", "lambda_q2", "lambda_k2")):
            sp.dma_start(lamv[:, i, :], ins[n].broadcast_to([P, HD])).then_inc(consts, 16)
        sp.dma_start(h0s[:, :, :], ins["h0"]).then_inc(hland, 16)
        sp.dma_start(xd[:, :, :, 0:RGC - 1], ins["rgbuf"]).then_inc(hland, 16)
        x3 = ins["x_prompt"].rearrange("(t p) d -> p t d", p=P)
        sp.dma_start(xs[:, 0:TILES, :], x3).then_inc(xland, 16)
        sp.dma_start(xs[0:DEC, TILES, :], ins["x_sample"]).then_inc(xland, 16)

        nblk = [0]

        def weight(k=1):
            for _ in range(k):
                n = nblk[0]
                name, j = W_ORDER[n]
                if n >= 2:
                    sp.wait_ge(wused, n - 1)
                sp.dma_start(wr[:, n % 2, :, :], ins[name][j]).then_inc(wland[n % 2], 16)
                nblk[0] += 1

        weight(5)

        def page_loop(cache, g0):
            with sp.Fori(0, DEC) as b:
                for g in range(PAGES // PG):
                    wait_apart(sp, go, kfree, b * (PAGES // PG) + (g0 + g + 1))
                    for i in range(PG):
                        page = sp.value_load(ins["page_table"][0:1, bass.ds(b * PAGES + g * PG + i, 1)],
                                             min_val=0, max_val=NPHYS - 1)
                        sp.dma_start(pages[:, g % PSLOTS, i, :],
                                     cache[bass.ds(page * P, P), :]).then_inc(kland[g % PSLOTS], 16)

        page_loop(ins["cache_k"], 0)
        page_loop(ins["cache_v"], DEC * (PAGES // PG))

        for h in range(HEADS):
            sp.wait_ge(toepl, h + 1)
            sp.dma_start(ins["skew"][h], wide).then_inc(stored, 16)
            n_stores[0] += 1
            sp.wait_ge(stored, 16 * n_stores[0])
            n = SEQ + P - 1
            src = bass.AP(ins["skew"].tensor, h * P * n + P - 1, [[n - 1, P], [1, SEQ]])
            sp.dma_start(bias[:, h, :], src).then_inc(pt_, 16)
            sp.wait_ge(pt_, 16 * (h + 1))

        weight(2)
        weight(4)
        weight(6)
        weight(2)
        weight(4)
        assert nblk[0] == len(W_ORDER)
        y3 = outs["y_prompt"].rearrange("(t p) d -> p t d", p=P)
        for t in range(TILES + 1):
            sp.wait_ge(normed, 4 * (TILES + 1) + t + 1)
            dst = y3[:, t, :] if t < TILES else outs["y_sample"]
            sp.dma_start(dst, hn[0:rows(t), t, :]).then_inc(stored, 16)
            n_stores[0] += 1
        sp.wait_ge(stored, 16 * (n_stores[0]))
        sp.wait_ge(sconst, 16 * 10)

    @block.gpsimd
    def _(pool):
        pool.memset(ones[:, :], 1.0).then_inc(go, 1)
        pool.wait_ge(go, 1)
        def gathers(l, what, tile_ix, g0):
            tab = ins[what + str(l)]
            with pool.Fori(0, LAST) as i:
                pool.sem_clear(pool_s)
                for half in range(2):
                    o = half * GSLOTS
                    pool.tensor_copy(ixs[:, o:o + GSLOTS], tile_ix[:, bass.ds(i * GBODY + o, GSLOTS)])\
                        .then_inc(pool_s, 1)
                    for r in range(GSLOTS):
                        wait_apart(pool, go, rfree, i * GBODY + (g0 + o + r + 1))
                        pool.wait_ge(pool_s, half + 1)
                        pool.indirect_dma_start(ring[:, r, :], None, tab,
                                                bass.IndirectOffsetOnAxis(ap=ixs[:, o + r:o + r + 1], axis=0))\
                            .then_inc(rland[r], 16)

        for l in range(2):
            base = l * (TILES * 2 * SEL + 2 * PH)
            for t in range(TILES):
                pool.wait_ge(chosen, l * (TILES + 2) + t + 1)
                gathers(l, "peer_u", eix[:, t, :], base + t * 2 * SEL)
                gathers(l, "peer_v", eix[:, t, :], base + t * 2 * SEL + SEL)
            g0 = base + TILES * 2 * SEL
            pool.wait_ge(chosen, l * (TILES + 2) + TILES + 2)
            for n, what in enumerate(("peer_u", "peer_v")):
                for h in range(PH):
                    pool.wait_ge(rfree, g0 + n * PH + h + 1)
                    pool.indirect_dma_start(ring[:, h, :], None, ins[what + str(l)],
                                            bass.IndirectOffsetOnAxis(ap=dix[:, h:h + 1], axis=0))\
                        .then_inc(rland[h], 16)

    @block.tensor
    def _(pe):
        na, nv, nb = [0], [0], [0]

        def abank():
            g = na[0]
            na[0] += 1
            if g >= 4:
                pe.wait_ge(afree, g - 3)
            return ps[g % 4]

        def vbank():
            g = nv[0]
            nv[0] += 1
            if g >= 4:
                pe.wait_ge(vfree, g - 3)
            return ps[4 + g % 4]

        def wblock():
            n = nb[0]
            nb[0] += 1
            pe.wait_ge(wland[n % 2], 16 * (n // 2 + 1))
            return wr[:, n % 2, :, :]

        def transposes(norm):
            for t in range(TILES + 1):
                r = rows(t)
                pe.wait_ge(normed, norm * (TILES + 1) + t + 1)
                for k0 in range(0, KD, 4):
                    b = abank()
                    for k in range(4):
                        m = pe.transpose(b[:, k * P:k * P + r], hn[0:r, t, (k0 + k) * P:(k0 + k + 1) * P],
                                         ident[0:r, 0:r])
                    m.then_inc(aready, 1)

        def natural(bank_of, ready, lhs):
            w = wblock()
            for t in range(TILES + 1):
                b = bank_of()
                for k in range(KD):
                    m = pe.matmul(b[0:rows(t), :], lhs[:, k, cols(t)], w[:, k, :], start=(k == 0), stop=(k == KD - 1))
                m.then_inc(ready, 1)
            pe.wait_ge(ready, (na if bank_of is abank else nv)[0])
            pe.sem_inc(wused, 1)

        def tlayout(bank_of, ready, counter):
            w = wblock()
            for c in range(BLK // P):
                for half in range(2):
                    b = bank_of()
                    for k in range(KD):
                        m = pe.matmul(b[:, 0:HALF], w[:, k, c * P:(c + 1) * P], hT[:, k, half * HALF:(half + 1) * HALF],
                                      start=(k == 0), stop=(k == KD - 1))
                    m.then_inc(ready, 1)
            pe.wait_ge(ready, counter[0])
            pe.sem_inc(wused, 1)

        pe.wait_ge(consts, 16 * 9)
        pe.wait_ge(go, 1)
        transposes(0)
        pe.wait_ge(afree, na[0])
        for _ in range(3):
            natural(abank, aready, hT)
        for _ in range(2):
            tlayout(abank, aready, na)
        pe.wait_ge(afree, na[0])
        for t in range(TILES):
            for part in range(2):
                b = abank()
                for h in range(HEADS):
                    m = pe.transpose(b[:, h * P:(h + 1) * P], z[:, t, part * AW + h * P:part * AW + (h + 1) * P],
                                     ident[:, :])
                m.then_inc(aready, 1)
        for b_ in range(DEC):
            b = abank()
            pe.matmul(b[:, :], selb[:, b_, :], z[0:DEC, TILES, 0:AW], start=True, stop=True).then_inc(aready, 1)
        pe.wait_ge(sconst, 16 * 3)
        b = abank()
        for i in range(2):
            m = pe.matmul(b[:, i * HEADS:(i + 1) * HEADS], ohd[:, i, :], rbs, start=True, stop=True)
        m.then_inc(aready, 1)
        pe.wait_ge(mixin, 1)
        b = vbank()
        pe.transpose(b[0:64, 0:P], kq[:, 0:64], ident[:, :]).then_inc(vready, 1)
        pe.wait_ge(mixin, 2)
        b = vbank()
        pe.matmul(b[:, 0:64], ones[0:64, :], kq[0:64, 64:128], start=True, stop=True).then_inc(vready, 1)
        pe.wait_ge(mixin, 3)
        b = vbank()
        pe.matmul(b[:, 0:64], ones[:, :], kq[:, 0:64], start=True, stop=True).then_inc(vready, 1)
        o = vbank()
        pe.matmul(o[:, 0:64], ones[:, :], kq[:, 64:128], start=True, stop=False, skip_group_check=True)
        for h in range(HEADS):
            pe.matmul(o[:, 0:64].rearrange("p (b h c) -> p h b c", h=HEADS, c=2)[:, h, :, :],
                      z[0:DEC, TILES, 2 * AW + h * P:2 * AW + (h + 1) * P],
                      s[0:DEC, :, PAGES, 2 * h:2 * h + 2], start=False, stop=False, skip_group_check=True)
        ng = PAGES // PG
        with pe.Fori(0, DEC) as b_:
            for g in range(ng):
                wait_apart(pe, go, kland[g % PSLOTS], b_ * (16 * PG * ng // PSLOTS) + 16 * PG * (DEC * ng // PSLOTS + g // PSLOTS + 1))
                for i in range(PG):
                    for h in range(HEADS):
                        m = pe.matmul(o[:, bass.ds(b_ * 8 + 2 * h, 2)], pages[:, g % PSLOTS, i, h * P:(h + 1) * P],
                                      s[:, bass.ds(b_, 1), g * PG + i, 2 * h:2 * h + 2].rearrange("p a c -> p (a c)"),
                                      start=False, stop=False, skip_group_check=True)
                m.then_inc(kfree, 1)
        pe.matmul(o[:, 0:64], ones[:, :], kq[:, 64:128], start=False, stop=True, skip_group_check=True)\
            .then_inc(vready, 1)
        pe.wait_ge(mixin, 4)
        b = vbank()
        pe.matmul(b[:, 0:32], ones[:, :], kq[:, 32:64], start=True, stop=True).then_inc(vready, 1)
        pe.wait_ge(sconst, 16 * 6)
        for h in range(HEADS):
            pe.wait_ge(acts, h + 1)
            for c0 in (0, 320):
                b = abank()
                pe.matmul(b[:, 0:min(320, SEQ + P - 1 - c0)], rbw, ohs[:, c0:min(c0 + 320, SEQ + P - 1)],
                          start=True, stop=True).then_inc(aready, 1)
        n = 0
        for h in range(HEADS):
            for i in range(TILES):
                keys_n = (i + 1) * P
                for c in range(2):
                    b = vbank()
                    pe.matmul(b[:, 0:keys_n], qT[c * HD:(c + 1) * HD, h, i * P:(i + 1) * P],
                              kT[c * HD:(c + 1) * HD, h, 0:keys_n], start=True, stop=True).then_inc(vready, 1)
                pe.wait_ge(attn, n + 1)
                b = abank()
                for kb in range(i + 1):
                    m = pe.transpose(b[:, kb * P:(kb + 1) * P], wt[:, kb * P:(kb + 1) * P], ident[:, :])
                m.then_inc(aready, 1)
                pe.wait_ge(afree, na[0])
                b = abank()
                for kb in range(i + 1):
                    m = pe.matmul(b[:, 0:P], z[:, kb, 2 * AW + h * P:2 * AW + (h + 1) * P], pT[:, kb * P:(kb + 1) * P],
                                  start=(kb == 0), stop=(kb == i))
                m.then_inc(aready, 1)
                n += 1
            pe.wait_ge(asm_, h + 1)
            b = vbank()
            pe.matmul(b[:, :], ones[:, :], sq, start=True, stop=True).then_inc(vready, 1)
        pe.wait_ge(rgst, 1)
        pe.wait_ge(sconst, 16 * 8)
        for m_ in range(2):
            for c in range(RB):
                for half in range(2):
                    b = abank()
                    pe.matmul(b[:, 0:HALF], wab[:, m_, c, :], xc[:, c, half * HALF:(half + 1) * HALF],
                              start=True, stop=True).then_inc(aready, 1)
        pe.wait_ge(mixin, 5)
        for _ in range(2):
            natural(vbank, vready, cat)

        def peer(l, norm):
            transposes(norm)
            pe.wait_ge(afree, na[0])
            for _ in range(4):
                tlayout(abank, aready, na)
            pe.wait_ge(afree, na[0])
            pe.wait_ge(keyl, 16 * (l + 1))
            for t in range(TILES + 1):
                for g in range(HC // 4):
                    b = abank()
                    for c in range(4):
                        hc = 4 * g + c
                        m = pe.matmul(b[0:rows(t), c * P:(c + 1) * P], pq[:, hc, cols(t)], keys[:, hc, :],
                                      start=True, stop=True)
                    m.then_inc(aready, 1)
            pe.wait_ge(chosen, l * (TILES + 2) + TILES + 1)
            for c in range(2):
                b = abank()
                pe.matmul(b[:, :], rep[:, :], hn[0:DEC, TILES, c * 512:(c + 1) * 512], start=True, stop=True)\
                    .then_inc(aready, 1)
            b = vbank()
            pe.matmul(b[:, 0:2 * SEL], rep[:, :], e2f[0:DEC, :, :], start=True, stop=True).then_inc(vready, 1)
            pe.wait_ge(decs, l + 1)
            b0, b1 = vbank(), vbank()
            for h in range(PH):
                use = (l + 1) * (TILES * 2 * SEL // GSLOTS + 2)
                pe.wait_ge(rland[h], 16 * use)
                for c, b in enumerate((b0, b1)):
                    m = pe.matmul(b[0:DEC, :], dw[:, h, :], ring[:, h, c * 512:(c + 1) * 512],
                                  start=(h == 0), stop=(h == PH - 1))
                m.then_inc(rfree, 1)
            pe.wait_ge(rfree, (l + 1) * (TILES * 2 * SEL + 2 * PH) + GSLOTS)
            pe.sem_inc(vready, 2)

        peer(0, 1)
        transposes(2)
        pe.wait_ge(afree, na[0])
        for _ in range(2):
            tlayout(abank, aready, na)
        for _ in range(2):
            tlayout(vbank, vready, nv)
        for _ in range(2):
            tlayout(abank, aready, na)
        pe.wait_ge(mixin, 6)
        for _ in range(2):
            natural(vbank, vready, cat)
        peer(1, 3)

    @block.scalar
    def _(act):
        na = [0]
        step = Chain(act, act_s)

        def take():
            g = na[0]
            na[0] += 1
            act.wait_ge(aready, g + 1)
            return ps[g % 4]

        def roots(n):
            act.wait_ge(meansq, n + 1)
            v = st[:, 40:40 + TILES + 1]
            act.activation(v, v, ACT.Sqrt).then_inc(rstd, 1)

        def t_out(norm):
            roots(norm)
            for t in range(TILES + 1):
                r = rows(t)
                for k0 in range(0, KD, 4):
                    b = take()
                    act.copy(hT[:, k0:k0 + 4, cols(t)],
                             b[:, :].rearrange("p (k c) -> p k c", k=4)[:, :, 0:r]).then_inc(afree, 1)

        act.dma_start(gain[:, :], ins["gain0"].broadcast_to([P, D])).then_inc(gland, 16)
        act.wait_ge(lamq, 1)
        step(act.activation(st[:, 8:10], st[:, 8:10], ACT.Exp))
        act.activation(st[:, 24:28], st[:, 24:28], ACT.Exp).then_inc(lamd, 1)
        t_out(0)
        act.wait_ge(normed, TILES + 1)
        act.wait_ge(aready, na[0])
        for j in range(3):
            for t in range(TILES + 1):
                b = take()
                act.copy(z[0:rows(t), t, j * AW:(j + 1) * AW], b[0:rows(t), :]).then_inc(afree, 1)
        for j in range(2):
            for c in range(RB):
                b = take()
                if j == 0:
                    act.copy(xp[:, c, RGC - 1:RGC - 1 + HALF], b[:, 0:HALF]).then_inc(afree, 1)
                else:
                    act.copy(grT[:, c, 0:HALF], b[:, 0:HALF]).then_inc(afree, 1)
                b = take()
                if j == 0:
                    step(act.copy(xp[:, c, RGC - 1 + HALF:RGC - 1 + SEQ], b[:, 0:SEQ - HALF]))
                    act.copy(xd[:, c, :, RGC - 1], b[:, SEQ - HALF:HALF]).then_inc(afree, 1)
                else:
                    act.copy(grT[:, c, HALF:TOK], b[:, 0:HALF]).then_inc(afree, 1)
        act.wait_ge(afree, na[0])
        act.dma_start(ohd, ins["c_ohd"]).then_inc(sconst, 16)
        act.dma_start(rbs, ins["rel_bias"]).then_inc(sconst, 16)
        act.dma_start(rb0, ins["rel_bias"][0:1, :].broadcast_to([DEC, HEADS])).then_inc(sconst, 16)
        k3 = outs["k_prompt"].rearrange("(t p) d -> p t d", p=P)
        v3 = outs["v_prompt"].rearrange("(t p) d -> p t d", p=P)
        act.dma_start(k3, z[:, 0:TILES, AW:2 * AW]).then_inc(tpost, 16)
        act.dma_start(v3, z[:, 0:TILES, 2 * AW:3 * AW]).then_inc(tpost, 16)
        act.dma_start(outs["k_sample"], z[0:DEC, TILES, AW:2 * AW]).then_inc(tpost, 16)
        act.dma_start(outs["v_sample"], z[0:DEC, TILES, 2 * AW:3 * AW]).then_inc(tpost, 16)
        for t in range(TILES):
            for part in range(2):
                b = take()
                dst = (qT if part == 0 else kT)[:, :, cols(t)]
                src = b[:, :].rearrange("p (h c) -> p h c", h=HEADS)
                act.mul(dst, src, HD ** -0.5 if part == 0 else 1.0).then_inc(afree, 1)
        for b_ in range(DEC):
            b = take()
            act.mul(qb[:, b_, :], b[:, :], HD ** -0.5).then_inc(afree, 1)
        b = take()
        for c in range(2):
            m = act.copy(bd[:, :, :].rearrange("p a (h c) -> p a h c", c=2)[:, :, :, c],
                         b[:, 0:8].rearrange("p (a h) -> p a h", a=2))
            if c == 0:
                step(m)
            else:
                m.then_inc(afree, 1)
        act.wait_ge(afree, na[0])
        act.wait_ge(kdone, 1)
        act.activation(s[:, :, :, :], s[:, :, :, :], ACT.Exp).then_inc(expd, 1)
        act.wait_ge(dnorm, 1)
        act.activation(kq[:, 64:96], kq[:, 64:96], ACT.Sqrt).then_inc(dnorm, 1)
        act.wait_ge(mixin, 4)
        act.dma_start(ohs, ins["c_oh"]).then_inc(sconst, 16)
        act.dma_start(rbx[0:BUCKETS, :], ins["rel_bias"]).then_inc(sconst, 16)
        act.dma_start(rbx[BUCKETS:BUCKETS + 1, :], ins["c_mask"]).then_inc(sconst, 16)
        act.wait_ge(sconst, 16 * 6)
        for h in range(HEADS):
            if h:
                act.wait_ge(aready, na[0])
            act.copy(rbw, rbx[:, h:h + 1].broadcast_to([BUCKETS + 1, P])).then_inc(acts, 1)
            if h:
                act.wait_ge(pt_, 16 * h)
            b = take()
            step(act.copy(wide[:, 0:320], b[:, 0:320]))
            act.sem_inc(afree, 1)
            b = take()
            act.copy(wide[:, 320:SEQ + P - 1], b[:, 0:SEQ + P - 1 - 320]).then_inc(afree, 1)
            act.wait_ge(afree, na[0])
            act.sem_inc(toepl, 1)
        n = 0
        for h in range(HEADS):
            for i in range(TILES):
                for c in range(2):
                    act.wait_ge(scored, 2 * n + c + 1)
                    act.activation(lg[:, c, 0:(i + 1) * P], lg[:, c, 0:(i + 1) * P], ACT.Exp,
                                   bias=st[:, 16 + c:17 + c], accum_out=st[:, 18 + c:19 + c]).then_inc(expd, 1)
                b = take()
                act.copy(pT[:, 0:(i + 1) * P], b[:, 0:(i + 1) * P]).then_inc(afree, 1)
                b = take()
                step(act.copy(cat[:, h, i * P:(i + 1) * P], b[:, 0:P]))
                act.sem_inc(afree, 1)
                n += 1
            act.activation(sq, cat[:, h, 0:SEQ], ACT.Square).then_inc(asm_, 1)
            act.wait_ge(headq, h + 1)
            act.activation(rs, rs, ACT.Sqrt).then_inc(headd, 1)
        act.wait_ge(rgst, 1)
        act.dma_start(wab[:, 0, :, :], ins["wa_bd"]).then_inc(sconst, 16)
        act.dma_start(wab[:, 1, :, :], ins["wi_bd"]).then_inc(sconst, 16)
        for m_, dst in enumerate((gr_, gi_)):
            for c in range(RB):
                for half in range(2):
                    b = take()
                    o = PRM["ba" if m_ == 0 else "bi"] + c
                    act.activation(dst[:, c, half * HALF:(half + 1) * HALF], b[:, 0:HALF], ACT.Sigmoid,
                                   bias=prm[:, o:o + 1]).then_inc(afree, 1)
        act.wait_ge(afree, na[0])
        act.wait_ge(rgst, 2)
        for c in range(RB):
            step(act.activation(gr_[:, c, :], gr_[:, c, :], ACT.Tanh, scale=st[:, 4 + c:5 + c]))
        act.activation(gg[:, :, :], grT[:, :, :], ACT.Gelu_apprx_tanh).then_inc(asm_, 1)
        act.wait_ge(headq, HEADS + 1)
        act.activation(gr_[:, :, :], gr_[:, :, :], ACT.Sqrt, scale=4.0).then_inc(headd, 1)
        act.wait_ge(rgst, 3)
        act.dma_start(outs["hs"], hs[:, :, SEQ - 1:TOK]).then_inc(tpost, 16)
        act.dma_start(outs["rgp"], xp[:, :, SEQ:SEQ + RGC - 1]).then_inc(tpost, 16)
        act.dma_start(outs["rgs"], xd[:, :, :, 1:RGC]).then_inc(tpost, 16)
        act.wait_ge(tpost, 16 * 7)

        def peer(l, norm):
            act.wait_ge(mixin, 5 + l)
            act.dma_start(keys[:, :, :], ins[f"keys{l}"]).then_inc(keyl, 16)
            t_out(norm)
            for j in range(4):
                for c in range(BLK // P):
                    for half in range(2):
                        b = take()
                        act.copy(pq[:, j * 4 + c, half * HALF:(half + 1) * HALF], b[:, 0:HALF]).then_inc(afree, 1)
            for t in range(TILES + 1):
                if l * (TILES + 1) + t:
                    act.wait_ge(scfree, l * (TILES + 1) + t)
                for g in range(HC // 4):
                    b = take()
                    m = act.copy(sc[0:rows(t), 4 * g:4 * g + 4, :],
                                 b[0:rows(t), :].rearrange("p (a c) -> p a c", a=4))
                    m.then_inc(afree, 1)
                act.wait_ge(afree, na[0])
                act.sem_inc(peerd, 1)
                act.wait_ge(dexs, l * (TILES + 1) + t + 1)
                act.activation(s16[0:rows(t), :, :], s16[0:rows(t), :, :], ACT.Exp).then_inc(geld, 1)
            act.wait_ge(scfree, (l + 1) * (TILES + 1))
            for c in range(2):
                b = take()
                act.copy(xrep[:, c * 512:(c + 1) * 512], b[:, :]).then_inc(afree, 1)
            act.wait_ge(afree, na[0])
            act.sem_inc(repd, 1)
            for t in range(TILES + 1):
                act.wait_ge(dotd, l * (TILES + 1) + t + 1)
                src = dots[:, :] if t < TILES else ddot[:, :]
                act.activation(src, src, ACT.Gelu_apprx_tanh).then_inc(acts, 1)

        def next_gain(n):
            act.wait_ge(gused, n)
            act.dma_start(gain[:, :], ins[f"gain{n}"].broadcast_to([P, D])).then_inc(gland, 16)

        next_gain(1)
        peer(0, 1)
        next_gain(2)
        t_out(2)
        act.wait_ge(afree, na[0])
        act.dma_start(cxd[:, :, :, 0:SCC - 1], ins["sbuf0"]).then_inc(sconst, 16)
        for dst in (cgT, None, bgT):
            if dst is None:
                continue
            for j in range(2):
                for c in range(BLK // P):
                    for half in range(2):
                        b = take()
                        act.copy(dst[:, j * 4 + c, half * HALF:(half + 1) * HALF], b[:, 0:HALF]).then_inc(afree, 1)
        act.wait_ge(rgst, 4)
        act.dma_start(outs["scp"], cxp[:, :, SEQ:SEQ + SCC - 1]).then_inc(sconst, 16)
        act.wait_ge(sconst, 160)
        act.dma_start(outs["scs"], cxd[:, :, :, 1:SCC]).then_inc(tpost, 16)
        act.wait_ge(tpost, 16 * 8)
        next_gain(3)
        peer(1, 3)
        next_gain(4)
        roots(4)

    @block.vector
    def _(dve):
        step = Chain(dve, dve_s)
        nv, nn = [0], [0]

        def take():
            g = nv[0]
            nv[0] += 1
            dve.wait_ge(vready, g + 1)
            return ps[4 + g % 4]

        def norm():
            n = nn[0]
            nn[0] += 1
            dve.wait_ge(gland, 16 * (n + 1))
            for t in range(TILES + 1):
                r = rows(t)
                step(dve.tensor_tensor_reduce(junk[0:r, :], xs[0:r, t, :], xs[0:r, t, :], 1.0 / D, EPS,
                                              ALU.mult, ALU.add, st[0:r, 40 + t:41 + t]))
            dve.sem_inc(meansq, 1)
            dve.wait_ge(rstd, n + 1)
            step(dve.reciprocal(st[:, 40:40 + TILES + 1], st[:, 40:40 + TILES + 1]))
            for t in range(TILES + 1):
                r = rows(t)
                dve.scalar_tensor_tensor(hn[0:r, t, :], xs[0:r, t, :], st[0:r, 40 + t:41 + t], gain[0:r, :], ALU.mult, ALU.mult)\
                    .then_inc(normed, 1)
                dve.wait_ge(normed, n * (TILES + 1) + t + 1)
            dve.sem_inc(gused, 1)

        def add_out():
            for j in range(2):
                for t in range(TILES + 1):
                    r = rows(t)
                    b = take()
                    x = xs[0:r, t, j * BLK:(j + 1) * BLK]
                    dve.tensor_tensor(x, x, b[0:r, :], ALU.add).then_inc(vfree, 1)
            dve.wait_ge(vfree, nv[0])

        step(dve.memset(st[:, :], 1.0))
        dve.wait_ge(consts, 16 * 9)
        for i in range(2):
            step(dve.tensor_tensor_reduce(junk[:, 0:HD], lamv[:, 2 * i, :], lamv[:, 2 * i + 1, :], 1.0, 0.0,
                                          ALU.mult, ALU.add, st[:, 8 + i:9 + i]))
        lam_ = prm[:, PRM["lam"]:PRM["lam"] + RB]
        step(dve.scalar_tensor_tensor(st[:, 24:28], lam_, -1.0, lam_, ALU.mult, ALU.min))
        dve.sem_inc(lamq, 1)
        dve.sem_inc(rfree, GSLOTS)
        dve.wait_ge(xland, 32)
        norm()
        step(dve.memset(xp[:, :, 0:RGC - 1], 0.0))
        dve.wait_ge(sconst, 16 * 3)
        q_, k_ = z[0:DEC, TILES, 0:AW], z[0:DEC, TILES, AW:2 * AW]
        step(dve.tensor_tensor(snew, q_, k_, ALU.mult))
        step(dve.tensor_reduce(sn8, snew.rearrange("p (a d) -> p a d", d=HD), AX.X, ALU.add))
        step(dve.scalar_tensor_tensor(sn8.rearrange("p (h c) -> p h c", c=2), sn8.rearrange("p (h c) -> p h c", c=2),
                                      HD ** -0.5, rb0.unsqueeze(2).broadcast_to([DEC, HEADS, 2]), ALU.mult, ALU.add))
        step(dve.memset(s[:, :, PAGES, :], MASK))
        eye = ident[0:DEC, 0:DEC].unsqueeze(2).broadcast_to([DEC, DEC, 8])
        sd = sdg.rearrange("p (b c) -> p b c", b=DEC)
        step(dve.tensor_scalar(sd, eye, -MASK, MASK, ALU.mult, ALU.add))
        step(dve.tensor_tensor(s[0:DEC, :, PAGES, :], sn8.unsqueeze(1).broadcast_to([DEC, DEC, 8]), eye, ALU.mult))
        step(dve.tensor_tensor(s[0:DEC, :, PAGES, :], s[0:DEC, :, PAGES, :], sd, ALU.add))
        dve.wait_ge(afree, A_QB)
        dve.sem_inc(kfree, PSLOTS)
        ng = PAGES // PG
        with dve.Fori(0, DEC) as b_:
            step.clear()
            for g in range(ng):
                kp = pages[:, g % PSLOTS, :, :]
                wait_apart(dve, go, kland[g % PSLOTS], b_ * (16 * PG * ng // PSLOTS) + 16 * PG * (g // PSLOTS + 1))
                step(dve.tensor_tensor(kp, kp, qb[:, bass.ds(b_, 1), :].broadcast_to([P, PG, AW]), ALU.mult))
                dve.tensor_reduce(s[:, bass.ds(b_, 1), g * PG:(g + 1) * PG, :].rearrange("p a j c -> p (a j c)"),
                                  kp.rearrange("p g c -> p (g c)").rearrange("p (a d) -> p a d", d=HD), AX.X, ALU.add)\
                    .then_inc(kfree, 1)
            wait_apart(dve, go, kfree, b_ * ng + ng + PSLOTS)
        step.clear()
        for j in range(2):
            pg_ = slice(0, PAGES - 1) if j == 0 else slice(PAGES - 1, PAGES)
            n = PAGES - 1 if j == 0 else 1
            for b_ in range(DEC):
                v = s[:, b_, pg_, :]
                step(dve.tensor_tensor(v, v, bd[:, j, :].unsqueeze(1).broadcast_to([P, n, 8]), ALU.add))
        mx = kq[:, 0:64]
        byc = s[:, :, :, :].rearrange("p b j c -> p b c j")
        mx3 = mx.rearrange("p (b c) -> p b c", b=DEC)
        dve.tensor_reduce(mx3, byc, AX.X, ALU.max).then_inc(mixin, 1)
        b = take()
        step(dve.tensor_reduce(st[0:64, 2:3], b[0:64, 0:P], AX.X, ALU.max))
        dve.sem_inc(vfree, 1)
        dve.tensor_scalar(kq[0:64, 64:128], ident[0:64, 0:64], st[0:64, 2:3], None, ALU.mult).then_inc(mixin, 1)
        b = take()
        step(dve.tensor_copy(kq[:, 0:64], b[:, 0:64]))
        dve.sem_inc(vfree, 1)
        step(dve.memset(kq[:, 64:128], 0.0))
        for b_ in range(DEC):
            v = s[:, b_, :, :]
            step(dve.tensor_tensor(v, v, kq[:, b_ * 8:b_ * 8 + 8].unsqueeze(1).broadcast_to([P, PAGES + 1, 8]),
                                   ALU.subtract))
        dve.sem_inc(kdone, 1)
        dve.wait_ge(expd, 1)
        dve.tensor_reduce(mx3, byc, AX.X, ALU.add).then_inc(mixin, 1)
        b = take()
        step(dve.reciprocal(kq[:, 128:160], b[:, 0:64].rearrange("p (a c) -> p a c", c=2)[:, :, 0]))
        step(dve.reciprocal(kq[:, 0:32], b[:, 0:64].rearrange("p (a c) -> p a c", c=2)[:, :, 1]))
        dve.sem_inc(vfree, 1)
        dve.wait_ge(lamd, 1)
        step(dve.tensor_tensor(st[:, 10:11], st[:, 8:9], st[:, 9:10], ALU.subtract))
        step(dve.tensor_scalar(st[:, 11:12], st[:, 10:11], LAM0, -1.0, ALU.add, ALU.mult))
        b = take()
        o2 = b[:, 0:64].rearrange("p (a c) -> p a c", c=2)
        step(dve.scalar_tensor_tensor(kq[:, 0:32], o2[:, :, 1], st[:, 11:12], kq[:, 0:32], ALU.mult, ALU.mult))
        step(dve.tensor_tensor(kq[:, 128:160], o2[:, :, 0], kq[:, 128:160], ALU.mult))
        dve.sem_inc(vfree, 1)
        step(dve.tensor_tensor(kq[:, 0:32], kq[:, 0:32], kq[:, 128:160], ALU.add))
        dve.tensor_tensor(kq[:, 32:64], kq[:, 0:32], kq[:, 0:32], ALU.mult).then_inc(mixin, 1)
        b = take()
        step(dve.tensor_scalar(kq[:, 64:96], b[:, 0:32], 1.0 / P, EPS, ALU.mult, ALU.add))
        dve.sem_inc(vfree, 1)
        dve.sem_inc(dnorm, 1)
        dve.wait_ge(dnorm, 2)
        step(dve.reciprocal(kq[:, 64:96], kq[:, 64:96]))
        step(dve.tensor_scalar(st[:, 12:13], prm[:, PRM["subln"]:PRM["subln"] + 1], 1.0 - LAM0, None, ALU.mult))
        step(dve.scalar_tensor_tensor(cat[:, 0:HEADS, SEQ:TOK], kq[:, 0:32].rearrange("p (b h) -> p h b", h=HEADS),
                                      st[:, 12:13], kq[:, 64:96].rearrange("p (b h) -> p h b", h=HEADS),
                                      ALU.mult, ALU.mult))
        n = 0
        for h in range(HEADS):
            dve.wait_ge(pt_, 16 * HEADS)
            for i in range(TILES):
                w = (i + 1) * P
                for c in range(2):
                    b = take()
                    step(dve.tensor_tensor(lg[:, c, 0:w], b[:, 0:w], bias[:, h, (TILES - 1 - i) * P:SEQ], ALU.add))
                    dve.sem_inc(vfree, 1)
                    dve.tensor_reduce(st[:, 16 + c:17 + c], lg[:, c, 0:w], AX.X, ALU.max, negate=True)\
                        .then_inc(scored, 1)
                dve.wait_ge(expd, 1 + 2 * n + 2)
                step(dve.reciprocal(st[:, 20:22], st[:, 18:20]))
                step(dve.tensor_tensor(st[:, 21:22], st[:, 21:22], st[:, 11:12], ALU.mult))
                step(dve.tensor_scalar(lg[:, 0, 0:w], lg[:, 0, 0:w], st[:, 20:21], None, ALU.mult))
                dve.scalar_tensor_tensor(wt[:, 0:w], lg[:, 1, 0:w], st[:, 21:22], lg[:, 0, 0:w], ALU.mult, ALU.add)\
                    .then_inc(attn, 1)
                dve.wait_ge(attn, n + 1)
                n += 1
            b = take()
            step(dve.tensor_scalar(rs, b[:, :], 1.0 / P, EPS, ALU.mult, ALU.add))
            dve.sem_inc(vfree, 1)
            dve.sem_inc(headq, 1)
            dve.wait_ge(headd, h + 1)
            step(dve.reciprocal(rs, rs))
            step(dve.scalar_tensor_tensor(cat[:, h, 0:SEQ], cat[:, h, 0:SEQ], st[:, 12:13], rs, ALU.mult, ALU.mult))
        dve.wait_ge(tpost, 16 * 4)
        dve.wait_ge(hland, 32)
        for c in range(RB):
            for dst, src in ((xc[:, c, 0:SEQ], lambda i: xp[:, c, i:i + SEQ]), (xc[:, c, SEQ:TOK], lambda i: xd[:, c, :, i])):
                o = PRM["conv_w"] + c * RGC
                bb = PRM["conv_b"] + c
                step(dve.tensor_scalar(dst, src(0), prm[:, o:o + 1], prm[:, bb:bb + 1], ALU.mult, ALU.add))
                for i in range(1, RGC):
                    step(dve.scalar_tensor_tensor(dst, src(i), prm[:, o + i:o + i + 1], dst, ALU.mult, ALU.add))
        dve.sem_inc(rgst, 1)
        sp_ = st[:, 4:8]
        y_, t_, q2 = st[:, 24:28], st[:, 28:32], st[:, 32:36]
        dve.wait_ge(lamd, 1)
        step(dve.tensor_scalar(t_, y_, 2.0, None, ALU.add))
        step(dve.reciprocal(t_, t_))
        step(dve.tensor_tensor(y_, y_, t_, ALU.mult))
        step(dve.tensor_tensor(q2, y_, y_, ALU.mult))
        step(dve.memset(t_, 1.0 / 19))
        for k in range(17, 0, -2):
            step(dve.tensor_tensor(t_, t_, q2, ALU.mult))
            step(dve.tensor_scalar(t_, t_, 1.0 / k, None, ALU.add))
        step(dve.tensor_tensor(t_, t_, y_, ALU.mult))
        step(dve.tensor_scalar(y_, prm[:, PRM["lam"]:PRM["lam"] + 4], -1.0, 0.0, ALU.mult, ALU.max))
        step(dve.scalar_tensor_tensor(sp_, t_, 2.0, y_, ALU.mult, ALU.add))
        step(dve.tensor_scalar(sp_, sp_, 4.0, None, ALU.mult))
        dve.sem_inc(rgst, 1)
        dve.wait_ge(asm_, HEADS + 1)
        u = gr_[:, :, :]
        step(dve.tensor_scalar(ua, u, 1.0, None, ALU.add))
        step(dve.reciprocal(ua, ua))
        step(dve.tensor_scalar(ub, u, -1.0, 1.0, ALU.mult, ALU.add))
        step(dve.tensor_tensor(ub, ub, ua, ALU.mult))
        dve.sem_inc(headq, 1)
        dve.wait_ge(headd, HEADS + 1)
        step(dve.tensor_tensor(u, u, ua, ALU.mult))
        step(dve.tensor_tensor(u, u, gi_, ALU.mult))
        step(dve.tensor_tensor(u, u, xc, ALU.mult))
        for c in range(RB):
            step(dve.tensor_tensor_scan(hs[:, c, 0:SEQ], ub[:, c, 0:SEQ], u[:, c, 0:SEQ], 0.0, ALU.mult, ALU.add))
        dve.wait_ge(hland, 32)
        step(dve.tensor_tensor(hs[:, :, SEQ:TOK], ub[:, :, SEQ:TOK], h0s[:, :, :], ALU.mult))
        step(dve.tensor_tensor(hs[:, :, SEQ:TOK], hs[:, :, SEQ:TOK], u[:, :, SEQ:TOK], ALU.add))
        dve.sem_inc(rgst, 1)
        step(dve.tensor_tensor(cat[:, HEADS:HEADS + RB, :], hs, gg, ALU.mult))
        dve.sem_inc(mixin, 1)
        add_out()

        def choose(r):
            for hc in range(HC):
                row, two = sc[0:r, hc, :], sc2[0:r, 0:NKEY]
                step(dve.max(v16[0:r, hc, 0:8], row))
                step(dve.max_index(i16[0:r, hc, 0:8], v16[0:r, hc, 0:8], row))
                step(dve.match_replace(two, v16[0:r, hc, 0:8], row, LOW))
                step(dve.max(v16[0:r, hc, 8:16], two))
                step(dve.max_index(i16[0:r, hc, 8:16], v16[0:r, hc, 8:16], two))
            dve.sem_inc(scfree, 1)
            step(dve.tensor_copy(i16f[0:r, :, :], i16[0:r, :, :]))
            for h in range(PH):
                step(dve.tensor_tensor(cand[0:r, h, :].rearrange("p (a b) -> p a b", a=TOPK),
                                       v16[0:r, 2 * h, :].unsqueeze(2).broadcast_to([r, TOPK, TOPK]),
                                       v16[0:r, 2 * h + 1, :].unsqueeze(1).broadcast_to([r, TOPK, TOPK]), ALU.add))
                row, two, c = cand[0:r, h, :], sc2[0:r, :], c16[0:r, h * TOPK:(h + 1) * TOPK]
                step(dve.max(s16[0:r, h, 0:8], row))
                step(dve.max_index(c[:, 0:8], s16[0:r, h, 0:8], row))
                step(dve.match_replace(two, s16[0:r, h, 0:8], row, LOW))
                step(dve.max(s16[0:r, h, 8:16], two))
                step(dve.max_index(c[:, 8:16], s16[0:r, h, 8:16], two))
            step(dve.tensor_copy(gsum[0:r, :], s16[0:r, :, 0]))
            step(dve.tensor_tensor(s16[0:r, :, :], s16[0:r, :, :], gsum[0:r, :].unsqueeze(2).broadcast_to([r, PH, TOPK]),
                                   ALU.subtract))
            dve.sem_inc(dexs, 1)
            step(dve.tensor_scalar(chi[0:r, :], c16[0:r, :], 4, None, ALU.logical_shift_right))
            step(dve.tensor_scalar(clo[0:r, :], c16[0:r, :], 15, None, ALU.bitwise_and))
            step(dve.tensor_copy(hif[0:r, :], chi[0:r, :]))
            step(dve.tensor_copy(lof[0:r, :], clo[0:r, :]))
            big = cand[0:r, :, :].rearrange("p h (k j) -> p h k j", j=TOPK)
            flat = cand[0:r, :, :].rearrange("p h (k j) -> p (h k) j", j=TOPK)
            for half, (pos, dst) in enumerate(((hif, e1f[0:r, :]), (lof, e2f[0:r, 0, :]))):
                step(dve.tensor_tensor(flat, pos[0:r, :].unsqueeze(2).broadcast_to([r, SEL, TOPK]),
                                       small[0:r, 0:16].unsqueeze(1).broadcast_to([r, SEL, TOPK]), ALU.is_equal))
                idx = i16f[0:r, :, :].rearrange("p (h c) j -> p h c j", c=2)[:, :, half, :]
                step(dve.tensor_tensor(big, big, idx.unsqueeze(2).broadcast_to([r, PH, TOPK, TOPK]), ALU.mult))
                step(dve.tensor_reduce(dst, flat, AX.X, ALU.add))
            step(dve.scalar_tensor_tensor(e2f[0:r, 0, :], e1f[0:r, :], float(NKEY), e2f[0:r, 0, :], ALU.mult, ALU.add))

        def gates(r, dst):
            step(dve.tensor_reduce(gsum[0:r, :], s16[0:r, :, :], AX.X, ALU.add))
            step(dve.reciprocal(gsum[0:r, :], gsum[0:r, :]))
            step(dve.tensor_tensor(dst, s16[0:r, :, :], gsum[0:r, :].unsqueeze(2).broadcast_to([r, PH, TOPK]), ALU.mult))

        def peer(l):
            norm()
            with dve.Fori(0, TILES) as t:
                step.clear()
                wait_apart(dve, go, peerd, t + (l * (TILES + 1) + 1))
                choose(P)
                wait_apart(dve, go, geld, t + (l * (TILES + 1) + 1))
                gates(P, coef.rearrange("p (h k) -> p h k", h=PH))
                step(dve.tensor_copy(gt[:, bass.ds(t, 1), :].rearrange("p a c -> p (a c)"), coef))
                step(dve.tensor_copy(eix[:, bass.ds(t, 1), :].rearrange("p a c -> p (a c)"), e2f[:, 0, :]))
                dve.sem_inc(chosen, 1)
            step.clear()
            dve.wait_ge(peerd, (l + 1) * (TILES + 1))
            choose(DEC)
            dve.wait_ge(geld, (l + 1) * (TILES + 1))
            gates(DEC, e2f[0:DEC, 1, :].rearrange("p (h k) -> p h k", h=PH))
            dve.sem_inc(chosen, 1)
            b = take()
            step(dve.tensor_tensor(dsel.rearrange("p a h k -> p (a h) k"), b[:, 0:2 * SEL].rearrange("p (a k) -> p a k", k=TOPK),
                                   small[:, 16:32].unsqueeze(1).broadcast_to([P, 2 * PH, TOPK]), ALU.mult))
            dve.sem_inc(vfree, 1)
            step(dve.tensor_reduce(dex, dsel.rearrange("p a h k -> p (a h) k"), AX.X, ALU.add))
            step(dve.tensor_copy(dix[:, :], dex[:, 0:PH]))
            dve.sem_inc(chosen, 1)
            use0 = l * (TILES * 2 * SEL // GSLOTS + 2)
            for t in range(TILES):
                with dve.Fori(0, LAST) as i:
                    step.clear()
                    for r in range(GBODY):
                        wait_apart(dve, go, rland[r % GSLOTS], i * 32 + 16 * (use0 + t * 32 + r // GSLOTS + 1))
                        step(dve.tensor_tensor_reduce(junk[:, :], ring[:, r % GSLOTS, :], hn[:, t, :], 1.0, 0.0,
                                                      ALU.mult, ALU.add, d16[:, r:r + 1]))
                        dve.sem_inc(rfree, 1)
                    step(dve.tensor_copy(dots[:, bass.ds(i * GBODY, GBODY)], d16[:, :]))
                step.clear()
                dve.sem_inc(dotd, 1)
                dve.wait_ge(acts, HEADS + l * (TILES + 1) + t + 1)
                step(dve.tensor_tensor(coef[:, :], dots[:, :], gt[:, t, :], ALU.mult))
                with dve.Fori(0, LAST) as i:
                    step.clear()
                    step(dve.tensor_copy(d16[:, :], coef[:, bass.ds(i * GBODY, GBODY)]))
                    for r in range(GBODY):
                        wait_apart(dve, go, rland[r % GSLOTS], i * 32 + 16 * (use0 + t * 32 + 16 + r // GSLOTS + 1))
                        step(dve.scalar_tensor_tensor(xs[:, t, :], ring[:, r % GSLOTS, :], d16[:, r:r + 1], xs[:, t, :],
                                                      ALU.mult, ALU.add))
                        dve.sem_inc(rfree, 1)
                step.clear()
            dve.wait_ge(repd, l + 1)
            for h in range(PH):
                dve.wait_ge(rland[h], 16 * (use0 + TILES * 32 + 1))
                step(dve.tensor_tensor_reduce(junk[:, :], ring[:, h, :], xrep, 1.0, 0.0, ALU.mult, ALU.add,
                                              ddot[:, h:h + 1]))
                dve.sem_inc(rfree, 1)
            dve.sem_inc(dotd, 1)
            dve.wait_ge(acts, HEADS + (l + 1) * (TILES + 1))
            step(dve.tensor_tensor(dcf, ddot, dex[:, PH:2 * PH], ALU.mult))
            step(dve.tensor_tensor(dw, small[:, 32:32 + DEC].unsqueeze(1).broadcast_to([P, PH, DEC]),
                                   dcf.unsqueeze(2).broadcast_to([P, PH, DEC]), ALU.mult))
            dve.sem_inc(decs, 1)
            for c in range(2):
                b = take()
                x = xs[0:DEC, TILES, c * 512:(c + 1) * 512]
                dve.tensor_tensor(x, x, b[0:DEC, :], ALU.add).then_inc(vfree, 1)
            dve.wait_ge(vfree, nv[0])

        peer(0)
        norm()
        step(dve.memset(cxp[:, :, 0:SCC - 1], 0.0))
        dve.wait_ge(afree, A_CG)
        for k in range(KD):
            b = take()
            dve.tensor_tensor(cxp[:, k, SCC - 1:SCC - 1 + HALF], b[:, 0:HALF], cgT[:, k, 0:HALF], ALU.mult)\
                .then_inc(vfree, 1)
            b = take()
            step(dve.tensor_tensor(cxp[:, k, SCC - 1 + HALF:SCC - 1 + SEQ], b[:, 0:SEQ - HALF], cgT[:, k, HALF:SEQ], ALU.mult))
            dve.tensor_tensor(cxd[:, k, :, SCC - 1], b[:, SEQ - HALF:HALF], cgT[:, k, SEQ:TOK], ALU.mult)\
                .then_inc(vfree, 1)
        dve.wait_ge(vfree, nv[0])
        dve.wait_ge(sconst, 16 * 9)
        dve.sem_inc(rgst, 1)
        for k in range(KD):
            o = PRM["sconv"] + k * SCC
            for dst, src in ((cvT[:, k, 0:SEQ], lambda i: cxp[:, k, i:i + SEQ]), (cvT[:, k, SEQ:TOK], lambda i: cxd[:, k, :, i])):
                step(dve.tensor_scalar(dst, src(0), prm[:, o:o + 1], None, ALU.mult))
                for i in range(1, SCC):
                    step(dve.scalar_tensor_tensor(dst, src(i), prm[:, o + i:o + i + 1], dst, ALU.mult, ALU.add))
        dve.wait_ge(afree, A_BG)
        step(dve.tensor_tensor(cat[:, :, :], cvT, bgT, ALU.mult))
        dve.sem_inc(mixin, 1)
        add_out()
        peer(1)
        norm()


def blocks(w, first=0, n=None):
    return np.ascontiguousarray(w.reshape(KD, P, -1, BLK).transpose(2, 1, 0, 3))


def chan(a, nb):
    a = a.reshape(*a.shape[:-1], nb, P)
    return np.ascontiguousarray(np.moveaxis(a, (-1, -2), (0, 1)))


def blockdiag(w):
    out = np.zeros((P, RB, P), w.dtype)
    h = P // 2
    for c in range(RB):
        out[:h, c, :h] = w[2 * c]
        out[h:, c, h:] = w[2 * c + 1]
    return out


OUTS = {"y_prompt": [SEQ, D], "y_sample": [DEC, D], "k_prompt": [SEQ, AW], "v_prompt": [SEQ, AW],
        "k_sample": [DEC, AW], "v_sample": [DEC, AW], "hs": [P, RB, DEC + 1], "rgp": [P, RB, RGC - 1],
        "rgs": [P, RB, DEC, RGC - 1], "scp": [P, KD, SCC - 1], "scs": [P, KD, DEC, SCC - 1]}


def kernel(**a):
    import concourse.bacc as bacc
    from concourse.bass_utils import run_bass_kernel_spmd

    a = {k: np.asarray(v) for k, v in a.items()}
    f = {
        "x_prompt": a["x_prompt"][0], "x_sample": a["x_sample"][:, 0],
        "cache_k": a["cache_k"][0].reshape(NPHYS * P, AW), "cache_v": a["cache_v"][0].reshape(NPHYS * P, AW),
        "page_table": a["page_table"].reshape(1, DEC * PAGES), "rel_bias": a["rel_bias"],
        "gain0": a["norm_mix"][0:1], "gain1": a["norm_ffn"][0:1], "gain2": a["norm_mix"][1:2],
        "gain3": a["norm_ffn"][1:2], "gain4": a["norm_final"].reshape(1, D),
        "w_in_a": blocks(a["w_in_a"][0]), "w_out_a": blocks(a["w_out_a"][0]), "w_in_c": blocks(a["w_in_c"][0]),
        "w_out_c": blocks(a["w_out_c"][0]), "wq0": blocks(a["peer_wq"][0]), "wq1": blocks(a["peer_wq"][1]),
        "lambda_q1": a["lambda_q1"], "lambda_k1": a["lambda_k1"], "lambda_q2": a["lambda_q2"],
        "lambda_k2": a["lambda_k2"],
        "wa_bd": blockdiag(a["rg_wa"][0]), "wi_bd": blockdiag(a["rg_wi"][0]),
        "h0": chan(a["state_rglru_h"][0], RB),
        "rgbuf": chan(a["state_rglru_conv"][0], RB), "sbuf0": chan(a["state_sconv"][0], KD),
    }
    prm = np.zeros((P, NPRM), np.float32)
    prm[:, 0:16] = chan(a["rg_conv_w"][0], RB).reshape(P, -1)
    prm[:, 16:20] = chan(a["rg_conv_b"][0], RB)
    prm[:, 20:24] = chan(a["rg_ba"][0], RB)
    prm[:, 24:28] = chan(a["rg_bi"][0], RB)
    prm[:, 28:32] = chan(a["rg_lambda"][0], RB)
    prm[:, 32] = a["subln_g"][0]
    prm[:, 33:] = chan(a["sc_conv_w"][0], KD).reshape(P, -1)
    f["prm"] = prm
    for l in range(2):
        f[f"keys{l}"] = a["peer_keys"][l].transpose(3, 0, 1, 2).reshape(P, HC, NKEY)
        f[f"peer_u{l}"] = a["peer_u"][l]
        f[f"peer_v{l}"] = a["peer_v"][l]
    f.update(shape_constants())
    f["c_mask"] = np.full((1, HEADS), MASK, np.float32)

    nc = bacc.Bacc("TRN2", target_bir_lowering=False, num_devices=1)
    arrays, ins, outs = {}, {}, {}
    for name, v in f.items():
        v = np.ascontiguousarray(v)
        arrays[name + "_in"] = v
        ins[name] = nc.dram_tensor(name + "_in", v.shape, mybir.dt.from_np(v.dtype), kind="ExternalInput").ap()
    ins["skew"] = nc.dram_tensor("skew", [HEADS, P, SEQ + P - 1], F32).ap()
    for name, shape in OUTS.items():
        outs[name] = nc.dram_tensor(name, shape, F32, kind="ExternalOutput").ap()
    build(nc, ins, outs)
    r = run_bass_kernel_spmd(nc, [arrays], core_ids=[0]).results[0]

    def back(v):
        v = np.moveaxis(v, (0, 1), (-1, -2))
        return np.ascontiguousarray(v.reshape(*v.shape[:-2], -1))

    kv = lambda v: v.reshape(1, 1, SEQ, HEADS, P)
    kvs = lambda v: v.reshape(1, DEC, 1, HEADS, P)
    h = back(r["hs"])
    return (r["y_prompt"].reshape(1, SEQ, D), r["y_sample"].reshape(DEC, 1, D), kv(r["k_prompt"]), kv(r["v_prompt"]),
            kvs(r["k_sample"]), kvs(r["v_sample"]), h[0:1].reshape(1, 1, AW), h[1:].reshape(1, DEC, AW),
            back(r["rgp"]).reshape(1, 1, RGC - 1, AW), back(r["rgs"]).reshape(1, DEC, RGC - 1, AW),
            back(r["scp"]).reshape(1, 1, SCC - 1, D), back(r["scs"]).reshape(1, DEC, SCC - 1, D))
```

```python
import math
from contextlib import ExitStack

import concourse.bass as bass
import numpy as np
from concourse import mybir

F32 = mybir.dt.float32
I32 = mybir.dt.int32
U32 = mybir.dt.uint32
ALU = mybir.AluOpType
ACT = mybir.ActivationFunctionType
AX = mybir.AxisListType

P = 128
D = 1024
KD = D // P
SEQ = 512
TILES = SEQ // P
DEC = 8
TOK = SEQ + DEC
HALF = TOK // 2
HEADS = 4
HD = 64
AW = 512
PAST = 4096
PAGES = PAST // P
NPHYS = 320
RB = 4
RGC = 4
SCC = 3
BUCKETS = 32
PH = 8
TOPK = 16
NKEY = 128
NEXP = NKEY * NKEY
HC = 2 * PH
SEL = PH * TOPK
EPS = 1e-6
LOW = -3.0e38
MASK = -1.0e30
LAM0 = 0.8 - 0.6 * math.exp(0.0)
BLK = 512
PG = 4
NG = PAGES // PG
GP = PG * P
SUB = GP // P
PSLOTS = 4
GSLOTS = 8
GBODY = 2 * GSLOTS
LAST = SEL // GBODY
GRP = 4
DT = 2
GT = TILES - DT
NCH = NEXP // P
RANGES = 4
CH = NCH // RANGES
CB = 4
OT = DT * P // CH

PRM = dict(conv_w=0, conv_b=16, ba=20, bi=24, lam=28, subln=32, sconv=33)
NPRM = 33 + KD * SCC


def bucket(dist):
    exact = BUCKETS // 2
    n = np.maximum(dist, 0)
    nf = np.maximum(n, 1).astype(np.float32)
    far = exact + (np.log(nf / np.float32(exact)) / np.float32(math.log(128 / exact))
                   * np.float32(BUCKETS - exact)).astype(np.int32)
    return np.where(n < exact, n, np.minimum(far, BUCKETS - 1))


def shape_constants():
    w = 2 * SEQ
    j = np.arange(SEQ + P - 1)
    oh = np.zeros((BUCKETS + 1, SEQ + P - 1), np.float32)
    dist = SEQ - 1 - j
    ok = dist >= 0
    oh[bucket(dist)[ok], j[ok]] = 1.0
    oh[BUCKETS, ~ok] = 1.0
    b = bucket(PAST - np.arange(PAST))
    assert (b[:-GP] == BUCKETS - 1).all()
    ohd = np.zeros((BUCKETS, SUB + 1, P), np.float32)
    ohd[BUCKETS - 1, SUB, :] = 1.0
    for i in range(SUB):
        ohd[b[-GP + i::SUB], i, np.arange(P)] = 1.0
    ident = np.eye(P, dtype=np.float32)
    sel = np.zeros((DEC, DEC, P), np.float32)
    for i in range(DEC):
        sel[i, i] = 1.0
    part = np.arange(P)
    rep = (part[None, :] // TOPK == np.arange(DEC)[:, None]).astype(np.float32)
    small = np.zeros((P, 16 + 16 + DEC + P + 1), np.float32)
    small[:, 40 + P] = part % (P // PG)
    small[:, 40:40 + P] = np.arange(P)
    small[:, 0:16] = np.arange(16)
    small[:, 16:32] = part[:, None] % TOPK == np.arange(16)[None, :]
    small[:, 32:32 + DEC] = part[:, None] // TOPK == np.arange(DEC)[None, :]
    return {"c_oh": oh, "c_ohd": ohd, "c_ident": ident, "c_sel": sel, "c_rep": rep, "c_small": small}


class Chain:

    def __init__(self, eng, sem):
        self.eng, self.sem, self.n = eng, sem, 0

    def __call__(self, ins):
        self.n += 1
        ins.then_inc(self.sem, 1)
        self.eng.wait_ge(self.sem, self.n)

    def clear(self):
        self.eng.sem_clear(self.sem)
        self.n = 0


def wait_apart(eng, go, sem, value):
    eng.wait_ge(sem, value)
    eng.sem_inc(go, 1)


def rows(t):
    return P if t < TILES else DEC


def cols(t):
    return slice(t * P, t * P + rows(t))


def build(nc, ins, outs):
    with ExitStack() as ctx:
        program(nc, ins, outs, ctx)


def program(nc, ins, outs, ctx):
    def sb(name, shape, dt=F32):
        return ctx.enter_context(nc.sbuf_tensor(name, shape, dt))

    def sem(name):
        return ctx.enter_context(nc.semaphore(name))

    xs = sb("xs", [P, TILES + 1, D])
    hn = sb("hn", [P, TILES + 1, D])
    hT = sb("hT", [P, KD, TOK])
    gain = sb("gain", [P, D])
    ident = sb("ident", [P, P])
    ones = sb("ones", [P, P])
    rep = sb("rep", [DEC, P])
    small = sb("small", [P, 16 + 16 + DEC + P + 1])
    io128 = small[:, 40:40 + P]
    prm = sb("prm", [P, NPRM])
    h0s = sb("h0s", [P, RB, DEC])
    st = sb("st", [P, 64])
    kq = sb("kq", [P, 160])
    AREA = 36860
    area = sb("area", [P, AREA])

    def at(off, *shape):
        n = math.prod(shape)
        assert off + n <= AREA, (off, shape)
        v = area[:, off:off + n]
        if len(shape) == 2:
            v = v.rearrange("p (a b) -> p a b", a=shape[0])
        elif len(shape) == 3:
            v = v.rearrange("p (a b c) -> p a b c", a=shape[0], b=shape[1])
        return v

    cat = hT
    wr = area[:, 26400:26400 + 2 * KD * BLK].rearrange("p (s k c) -> p s k c", s=2, k=KD)
    lamv = at(24000, 4, HD)
    selb = area[0:DEC, 34600:34600 + DEC * P].rearrange("p (b c) -> p b c", b=DEC)
    z = at(0, TILES + 1, 3 * AW)
    qT = at(7680, HEADS, SEQ)
    kT = at(9728, HEADS, SEQ)
    xp = at(11776, RB, SEQ + RGC - 1)
    xd = at(13836, RB, DEC, RGC)
    grT = at(13964, RB, TOK)
    s = at(16044, DEC, PAGES + 1, 8)
    pages = at(18156, PSLOTS, SUB, AW)
    pgi = area[:, 35640:35640 + DEC * NG].bitcast(I32)
    pgf = at(35704, DEC * NG)
    pgs = area[:, 35768:35768 + 2 * PSLOTS].bitcast(I32)
    qb = hn[:, 0:TILES, :].rearrange("p t c -> p (t c)").rearrange("p (b c) -> p b c", b=DEC)
    obs = hn[0:8, 0:TILES, :].rearrange("p t c -> p (t c)").rearrange("p (b c) -> p b c", b=DEC)
    bias = at(26400, HEADS, SEQ)
    lg = at(28448, 2, 2, SEQ)
    wt = at(30496, 2, SEQ)
    pT = at(31520, SEQ)
    sq = at(32032, SEQ)
    rs = at(32544, SEQ)
    wide = at(33056, SEQ + P - 1)
    ohs = area[0:BUCKETS + 1, 33700:33700 + SEQ + P - 1]
    rbx = area[0:BUCKETS + 1, 34340:34340 + HEADS]
    rbw = area[0:BUCKETS + 1, 34350:34350 + P]
    bd = hn[:, TILES, 0:(SUB + 1) * 8].rearrange("p (a b) -> p a b", a=SUB + 1)
    ohd = area[0:BUCKETS, 35800:35800 + (SUB + 1) * P].rearrange("p (a b) -> p a b", a=SUB + 1)
    rbs = hn[0:BUCKETS, TILES, 400:404]
    rb0 = hn[0:DEC, TILES, 408:412]
    snew = hn[0:DEC, TILES, 512:1024]
    sn8 = hn[0:DEC, TILES, 416:424]
    sdg = hn[0:DEC, TILES, 432:496]
    xc = at(0, RB, TOK)
    gr_ = at(2080, RB, TOK)
    gi_ = at(4160, RB, TOK)
    ua = at(6240, RB, TOK)
    ub = at(8320, RB, TOK)
    hs = at(18156, RB, TOK)
    gg = at(20236, RB, TOK)
    wab = at(22316, 2, RB, P)
    cgT = at(0, KD, TOK)
    cxp = at(4160, KD, SEQ + SCC - 1)
    cxd = at(8272, KD, DEC, SCC)
    bgT = at(8464, KD, TOK)
    cvT = at(12624, KD, TOK)
    wqs = [at(j * KD * BLK, KD, BLK) for j in range(4)]
    keys = at(16384, HC, NKEY)
    pq = at(18432, 2, HC, P)
    sc = at(22528, HC, NKEY)
    v16 = at(24832, HC, TOPK)
    i16 = area[:, 25088:25344].bitcast(U32).rearrange("p (a b) -> p a b", a=HC)
    i16f = at(25344, HC, TOPK)
    cand = at(25600, PH, 256)
    s16 = at(27648, PH, TOPK)
    c16 = area[:, 27776:27904].bitcast(U32)
    chi = area[:, 27904:28032].bitcast(U32)
    clo = area[:, 28032:28160].bitcast(U32)
    hif = at(28160, SEL)
    lof = at(28288, SEL)
    e1f = at(28416, SEL)
    e2f = at(28544, 2, SEL)
    e2s = at(28808, SEL)
    gsum = at(28800, PH)
    dsel = at(25600, 2, PH, TOPK)
    eT = at(29000, 3, DT * P)
    eix = area[:, 29768:29768 + GT * SEL].bitcast(I32).rearrange("p (a b) -> p a b", a=GT)
    gt = at(30024, GT, SEL)
    dots = at(30280, SEL)
    coef = at(30408, SEL)
    d16 = at(30536, GBODY)
    ixs = area[:, 30552:30568].bitcast(I32)
    dex = at(30568, 2 * PH)
    dix = area[:, 30584:30592].bitcast(I32)
    ddot = at(30592, PH)
    dcf = at(30600, PH)
    dw = at(30608, PH, DEC)
    G = [at(i * CH * DT * P, CH, DT * P) for i in range(2)]
    us = [at(16384 + i * D, KD, P) for i in range(4)]
    vs = [at(20480 + i * D, D) for i in range(2)]
    e2oh = [at(22528 + i * OT * P, OT, P) for i in range(2)]
    e1oh = [at(24576 + i * OT * CH, OT, CH) for i in range(2)]
    ga = at(25088, 2, DT * P)
    cT = at(25600, 2, DT * P)
    ring = [at(30700 + i * D, D) for i in range(6)] + [at(26112 + i * D, D) for i in range(2)]
    xrep = at(16384, D)

    ps = [ctx.enter_context(nc.psum_tensor(f"ps{i}", [P, 512], F32)) for i in range(8)]

    go = sem("go")
    consts = sem("consts")
    xland = sem("xland")
    gland = sem("gland")
    gused = sem("gused")
    normed = sem("normed")
    dve_s, act_s, pool_s = sem("dve_s"), sem("act_s"), sem("pool_s")
    wland = [sem("wland0"), sem("wland1")]
    wused = sem("wused")
    aready, afree = sem("aready"), sem("afree")
    vready, vfree = sem("vready"), sem("vfree")
    stored = sem("stored")
    mixin = sem("mixin")
    rgst = sem("rgst")
    tpost = sem("tpost")
    kfree = sem("kfree")
    kland = [sem(f"kland{i}") for i in range(PSLOTS)]
    kdone = sem("kdone")
    ptl, pgready = sem("ptl"), sem("pgready")
    odone = sem("odone")
    ofree = sem("ofree")
    pt_ = sem("pt_")
    toepl = sem("toepl")
    attn = sem("attn")
    asm_ = sem("asm_")
    acts = sem("acts")
    scored = sem("scored")
    scfree = sem("scfree")
    chosen = sem("chosen")
    expd = sem("expd")
    rland = [sem(f"rland{i}") for i in range(2)]
    rfree = sem("rfree")
    wqland = sem("wqland")
    efree = sem("efree")
    uland = [sem(f"uland{i}") for i in range(4)]
    vland = [sem(f"vland{i}") for i in range(2)]
    uready = sem("uready")
    gelud = sem("gelud")
    mulr = sem("mulr")
    vdn = sem("vdn")
    oready = sem("oready")
    gready = sem("gready")
    gevac = sem("gevac")
    ydone, yfree = sem("ydone"), sem("yfree")
    peerover = sem("peerover")
    dexs = sem("dexs")
    keyl = sem("keyl")
    dotd = sem("dotd")
    geld = sem("geld")
    decs = sem("decs")
    repd = sem("repd")
    peerd = sem("peerd")
    sconst = sem("sconst")
    meansq, rstd, dnorm = sem("meansq"), sem("rstd"), sem("dnorm")
    headq, headd = sem("headq"), sem("headd")
    lamq, lamd, hland = sem("lamq"), sem("lamd"), sem("hland")

    AST = (16, 48)

    block = ctx.enter_context(nc.Block())

    W_ORDER = [("w_in_a", j) for j in range(5)] + [("w_out_a", j) for j in range(2)] + \
              [("w_in_c", j) for j in (2, 3, 4, 5, 0, 1)] + [("w_out_c", j) for j in range(2)]

    A_QB = 2 * (TILES + 1) + 3 * (TILES + 1) + 2 * 2 * RB + 2 * TILES + DEC + 1
    A_PEER = 2 * (TILES + 1) + HC // 4 * (TILES + 1) * 2 + DT + 2
    A_CG = A_QB + 2 * HEADS + 2 * HEADS * TILES + 4 * RB + A_PEER + 2 * (TILES + 1) + 2 * KD
    A_BG = A_CG + 2 * KD

    GROUPS = GT * 2 * SEL // GRP + 2 * PH // GRP

    n_stores = [0]

    @block.sync
    def _(sp):
        for c, v in (("c_ident", ident[:, :]), ("c_sel", selb[:, :, :]), ("c_rep", rep[:, :]),
                     ("c_small", small[:, :]), ("prm", prm[:, :])):
            sp.dma_start(v, ins[c]).then_inc(consts, 16)
        for i, n in enumerate(("lambda_q1", "lambda_k1", "lambda_q2", "lambda_k2")):
            sp.dma_start(lamv[:, i, :], ins[n].broadcast_to([P, HD])).then_inc(consts, 16)
        sp.dma_start(h0s[:, :, :], ins["h0"]).then_inc(hland, 16)
        sp.dma_start(xd[:, :, :, 0:RGC - 1], ins["rgbuf"]).then_inc(hland, 16)
        x3 = ins["x_prompt"].rearrange("(t p) d -> p t d", p=P)
        sp.dma_start(xs[:, 0:TILES, :], x3).then_inc(xland, 16)
        sp.dma_start(xs[0:DEC, TILES, :], ins["x_sample"]).then_inc(xland, 16)

        for i in range(PG):
            sp.dma_start(pgi[i * (P // PG):(i + 1) * (P // PG), :],
                         ins["page_table"][i:i + 1, :].broadcast_to([P // PG, DEC * NG])).then_inc(ptl, 16)

        nblk = [0]

        def weight(k=1):
            for _ in range(k):
                n = nblk[0]
                name, j = W_ORDER[n]
                if n >= 2:
                    sp.wait_ge(wused, n - 1)
                sp.dma_start(wr[:, n % 2, :, :], ins[name][j]).then_inc(wland[n % 2], 16)
                nblk[0] += 1

        weight(5)

        for h in range(HEADS):
            sp.wait_ge(toepl, h + 1)
            sp.dma_start(ins["skew"][h], wide).then_inc(stored, 16)
            n_stores[0] += 1
            sp.wait_ge(stored, 16 * n_stores[0])
            n = SEQ + P - 1
            src = bass.AP(ins["skew"].tensor, h * P * n + P - 1, [[n - 1, P], [1, SEQ]])
            sp.dma_start(bias[:, h, :], src).then_inc(pt_, 16)
            sp.wait_ge(pt_, 16 * (h + 1))

        sp.wait_ge(rgst, 1)
        weight(2)

        def tables(l):
            sp.wait_ge(mixin, 5 + l)
            sp.wait_ge(tpost, 16 * (7 + l))
            sp.wait_ge(sconst, 16 * (8 + 2 * l))
            for j in range(4):
                sp.dma_start(wqs[j], ins[f"wq{l}"][j]).then_inc(wqland, 16)
            sp.wait_ge(chosen, (l + 1) * (TILES + 2))
            with sp.Fori(0, NCH // CB) as j:
                for c in range(CB):
                    wait_apart(sp, go, uready, j * CB + (l * NCH + c + 1))
                    sp.dma_start(us[c], ins[f"peer_ut{l}"][bass.ds(j * (CB * P) + c * P, P), :, :])\
                        .then_inc(uland[c], 16)
                    wait_apart(sp, go, vdn, j * CB + (l * NCH + c + 1))
                    sp.dma_start(vs[c % 2], ins[f"peer_v{l}"][bass.ds(j * (CB * P) + c * P, P), :])\
                        .then_inc(vland[c % 2], 16)

        tables(0)
        sp.wait_ge(peerover, 1)
        weight(6)
        weight(2)
        tables(1)
        assert nblk[0] == len(W_ORDER)
        y3 = outs["y_prompt"].rearrange("(t p) d -> p t d", p=P)
        for t in range(TILES + 1):
            sp.wait_ge(normed, 4 * (TILES + 1) + t + 1)
            dst = y3[:, t, :] if t < TILES else outs["y_sample"]
            sp.dma_start(dst, hn[0:rows(t), t, :]).then_inc(stored, 16)
            n_stores[0] += 1
        sp.wait_ge(stored, 16 * (n_stores[0]))
        sp.wait_ge(sconst, 16 * 10)

    @block.gpsimd
    def _(pool):
        pool.memset(ones[:, :], 1.0).then_inc(go, 1)
        pool.wait_ge(go, 1)

        def page_gathers(cache, g0):
            with pool.Fori(0, DEC) as b:
                pool.sem_clear(pool_s)
                for g in range(NG):
                    if g % PSLOTS == 0:
                        o = g % (2 * PSLOTS)
                        pool.tensor_copy(pgs[:, o:o + PSLOTS], pgi[:, bass.ds(b * NG + g, PSLOTS)]).then_inc(pool_s, 1)
                    wait_apart(pool, go, kfree, b * NG + (g0 + g + 1))
                    pool.wait_ge(pool_s, g // PSLOTS + 1)
                    o = g % (2 * PSLOTS)
                    pool.indirect_dma_start(pages[:, g % PSLOTS, :, :].rearrange("p a c -> p (a c)"), None, ins[cache],
                                            bass.IndirectOffsetOnAxis(ap=pgs[:, o:o + 1], axis=0))\
                        .then_inc(kland[g % PSLOTS], 16)

        pool.wait_ge(pgready, 1)
        page_gathers("cache_k", 0)
        page_gathers("cache_v", DEC * NG)

        def group(l, what, idx, half):
            for i in range(GRP):
                r = half * GRP + i
                pool.indirect_dma_start(ring[r], None, ins[what + str(l)],
                                        bass.IndirectOffsetOnAxis(ap=idx[:, i:i + 1], axis=0)).then_inc(rland[half], 16)

        def gathers(l, what, tile_ix, g0):
            with pool.Fori(0, LAST) as i:
                pool.sem_clear(pool_s)
                for n in range(GBODY // GRP):
                    if n % 2 == 0:
                        o = n // 2 * GSLOTS
                        pool.tensor_copy(ixs[:, o:o + GSLOTS], tile_ix[:, bass.ds(i * GBODY + o, GSLOTS)])\
                            .then_inc(pool_s, 1)
                    wait_apart(pool, go, rfree, i * (GBODY // GRP) + (g0 + n + 1))
                    pool.wait_ge(pool_s, n // 2 + 1)
                    group(l, what, ixs[:, n * GRP:(n + 1) * GRP], n % 2)

        for l in range(2):
            base = l * GROUPS
            pool.wait_ge(chosen, (l + 1) * (TILES + 2))
            for t in range(GT):
                gathers(l, "peer_u", eix[:, t, :], base + t * 2 * SEL // GRP)
                gathers(l, "peer_v", eix[:, t, :], base + (t * 2 + 1) * SEL // GRP)
            g0 = base + GT * 2 * SEL // GRP
            for n, what in enumerate(("peer_u", "peer_v")):
                for half in range(2):
                    pool.wait_ge(rfree, g0 + 2 * n + half + 1)
                    group(l, what, dix[:, half * GRP:(half + 1) * GRP], half)

    @block.tensor
    def _(pe):
        na, nv, nb = [0], [0], [0]
        turns = [4, 0]

        def abank():
            g = na[0]
            na[0] += 1
            if g >= 4:
                pe.wait_ge(afree, g - 3)
            return ps[g % 4]

        def vbank():
            g = nv[0]
            nv[0] += 1
            k, since = turns
            if g - since >= k:
                pe.wait_ge(vfree, g - k + 1)
            return ps[4 + (g - since) % k]

        def take_turns(k):
            pe.wait_ge(vfree, nv[0])
            turns[:] = [k, nv[0]]

        def wblock():
            n = nb[0]
            nb[0] += 1
            pe.wait_ge(wland[n % 2], 16 * (n // 2 + 1))
            return wr[:, n % 2, :, :]

        def transposes(norm):
            for t in range(TILES + 1):
                r = rows(t)
                pe.wait_ge(normed, norm * (TILES + 1) + t + 1)
                for k0 in range(0, KD, 4):
                    b = abank()
                    for k in range(4):
                        m = pe.transpose(b[:, k * P:k * P + r], hn[0:r, t, (k0 + k) * P:(k0 + k + 1) * P],
                                         ident[0:r, 0:r])
                    m.then_inc(aready, 1)

        def natural(bank_of, ready, lhs):
            w = wblock()
            for t in range(TILES + 1):
                b = bank_of()
                for k in range(KD):
                    m = pe.matmul(b[0:rows(t), :], lhs[:, k, cols(t)], w[:, k, :], start=(k == 0), stop=(k == KD - 1))
                m.then_inc(ready, 1)
            pe.wait_ge(ready, (na if bank_of is abank else nv)[0])
            pe.sem_inc(wused, 1)

        def tlayout(bank_of, ready, counter):
            w = wblock()
            for c in range(BLK // P):
                for half in range(2):
                    b = bank_of()
                    for k in range(KD):
                        m = pe.matmul(b[:, 0:HALF], w[:, k, c * P:(c + 1) * P], hT[:, k, half * HALF:(half + 1) * HALF],
                                      start=(k == 0), stop=(k == KD - 1))
                    m.then_inc(ready, 1)
            pe.wait_ge(ready, counter[0])
            pe.sem_inc(wused, 1)

        pe.wait_ge(consts, 16 * 9)
        pe.wait_ge(go, 1)
        pe.sem_inc(uready, 4)
        pe.sem_inc(vdn, 2)
        pe.sem_inc(gready, 2)
        transposes(0)
        pe.wait_ge(afree, na[0])
        for _ in range(3):
            natural(abank, aready, hT)
        for _ in range(2):
            tlayout(abank, aready, na)
        pe.wait_ge(afree, na[0])
        for t in range(TILES):
            for part in range(2):
                b = abank()
                for h in range(HEADS):
                    m = pe.transpose(b[:, h * P:(h + 1) * P], z[:, t, part * AW + h * P:part * AW + (h + 1) * P],
                                     ident[:, :])
                m.then_inc(aready, 1)
        for b_ in range(DEC):
            b = abank()
            pe.matmul(b[:, :], selb[:, b_, :], z[0:DEC, TILES, 0:AW], start=True, stop=True).then_inc(aready, 1)
        pe.wait_ge(sconst, 16 * 6)
        b = abank()
        for i in range(SUB + 1):
            m = pe.matmul(b[:, i * HEADS:(i + 1) * HEADS], ohd[:, i, :], rbs, start=True, stop=True)
        m.then_inc(aready, 1)
        for h in range(HEADS):
            pe.wait_ge(acts, h + 1)
            for c0 in (0, 320):
                b = abank()
                pe.matmul(b[:, 0:min(320, SEQ + P - 1 - c0)], rbw, ohs[:, c0:min(c0 + 320, SEQ + P - 1)],
                          start=True, stop=True).then_inc(aready, 1)
        pe.wait_ge(mixin, 1)
        b = vbank()
        pe.transpose(b[0:64, 0:P], kq[:, 0:64], ident[:, :]).then_inc(vready, 1)
        pe.wait_ge(mixin, 2)
        b = vbank()
        pe.matmul(b[:, 0:64], ones[0:64, :], kq[0:64, 64:128], start=True, stop=True).then_inc(vready, 1)
        pe.wait_ge(mixin, 3)
        b = vbank()
        pe.matmul(b[:, 0:64], ones[:, :], kq[:, 0:64], start=True, stop=True).then_inc(vready, 1)
        take_turns(3)
        o = ps[7]

        def values(g):
            b_, j = divmod(g, NG)
            if j == 0:
                if b_:
                    pe.wait_ge(ofree, b_)
                pe.matmul(o[0:8, :], s[0:DEC, b_, PAGES, :], z[0:DEC, TILES, 2 * AW:3 * AW],
                          start=True, stop=False, skip_group_check=True)
            pe.wait_ge(kland[g % PSLOTS], 16 * ((DEC * NG + g) // PSLOTS + 1))
            for i in range(SUB):
                m = pe.matmul(o[0:8, :], s[:, b_, j * SUB + i, :], pages[:, g % PSLOTS, i, :],
                              start=False, stop=(j == NG - 1 and i == SUB - 1), skip_group_check=True)
            m.then_inc(kfree, 1)
            if j == NG - 1:
                pe.wait_ge(kfree, PSLOTS + DEC * NG + g + 1)
                pe.sem_inc(odone, 1)

        def logits(n):
            h, i = divmod(n, TILES)
            keys_n = (i + 1) * P
            for c in range(2):
                b = vbank()
                pe.matmul(b[:, 0:keys_n], qT[c * HD:(c + 1) * HD, h, i * P:(i + 1) * P],
                          kT[c * HD:(c + 1) * HD, h, 0:keys_n], start=True, stop=True).then_inc(vready, 1)

        blocks_n = HEADS * TILES
        each = DEC * NG // blocks_n
        logits(0)
        for n in range(blocks_n):
            h, i = divmod(n, TILES)
            if n + 1 < blocks_n:
                logits(n + 1)
            for g in range(each * n, each * (n + 1)):
                values(g)
            pe.wait_ge(attn, n + 1)
            b = abank()
            for kb in range(i + 1):
                m = pe.transpose(b[:, kb * P:(kb + 1) * P], wt[:, n % 2, kb * P:(kb + 1) * P], ident[:, :])
            m.then_inc(aready, 1)
            pe.wait_ge(afree, na[0])
            b = abank()
            for kb in range(i + 1):
                m = pe.matmul(b[:, 0:P], z[:, kb, 2 * AW + h * P:2 * AW + (h + 1) * P], pT[:, kb * P:(kb + 1) * P],
                              start=(kb == 0), stop=(kb == i))
            m.then_inc(aready, 1)
            if i == TILES - 1:
                pe.wait_ge(asm_, h + 1)
                b = vbank()
                pe.matmul(b[:, :], ones[:, :], sq, start=True, stop=True).then_inc(vready, 1)
        pe.wait_ge(ofree, DEC)
        for b_ in range(DEC):
            for h in range(HEADS):
                m = pe.matmul(o[:, b_ * 8 + 2 * h:b_ * 8 + 2 * h + 2], obs[:, b_, h * P:(h + 1) * P],
                              ident[0:8, 2 * h:2 * h + 2], start=True, stop=True, skip_group_check=True)
        m.then_inc(odone, 1)
        take_turns(4)
        pe.wait_ge(mixin, 4)
        b = vbank()
        pe.matmul(b[:, 0:32], ones[:, :], kq[:, 32:64], start=True, stop=True).then_inc(vready, 1)
        pe.wait_ge(rgst, 1)
        pe.wait_ge(sconst, 16 * 8)
        for m_ in range(2):
            for c in range(RB):
                for half in range(2):
                    b = abank()
                    pe.matmul(b[:, 0:HALF], wab[:, m_, c, :], xc[:, c, half * HALF:(half + 1) * HALF],
                              start=True, stop=True).then_inc(aready, 1)
        pe.wait_ge(mixin, 5)
        for _ in range(2):
            natural(vbank, vready, cat)

        def peer(l, norm):
            transposes(norm)
            pe.wait_ge(afree, na[0])
            pe.wait_ge(wqland, 64 * (l + 1))
            pe.wait_ge(keyl, 16 * (l + 1))

            def queries(t):
                for g in range(HC // 4):
                    b = abank()
                    for c in range(4):
                        for k in range(KD):
                            m = pe.matmul(b[:, c * P:c * P + rows(t)], wqs[g][:, k, c * P:(c + 1) * P], hT[:, k, cols(t)],
                                          start=(k == 0), stop=(k == KD - 1))
                    m.then_inc(aready, 1)
                return na[0]

            def scores(t, got):
                pe.wait_ge(afree, got)
                for g in range(HC // 4):
                    b = abank()
                    for c in range(4):
                        m = pe.matmul(b[0:rows(t), c * P:(c + 1) * P], pq[:, t % 2, 4 * g + c, 0:rows(t)],
                                      keys[:, 4 * g + c, :], start=True, stop=True)
                    m.then_inc(aready, 1)

            def turn(t):
                pe.wait_ge(chosen, l * (TILES + 2) + t + 1)
                b = abank()
                for i, v in enumerate((e1f, e2s, coef)):
                    m = pe.transpose(b[:, i * P:(i + 1) * P], v, ident[:, :])
                m.then_inc(aready, 1)

            q = [queries(0), queries(1)]
            scores(0, q[0])
            q.append(queries(2))
            scores(1, q[1])
            turn(0)
            q.append(queries(3))
            scores(2, q[2])
            turn(1)
            q.append(queries(4))
            scores(3, q[3])
            scores(4, q[4])
            pe.wait_ge(chosen, l * (TILES + 2) + TILES + 1)
            b = vbank()
            pe.matmul(b[:, 0:2 * SEL], rep[:, :], e2f[0:DEC, :, :], start=True, stop=True).then_inc(vready, 1)
            pe.wait_ge(vfree, nv[0])
            pe.wait_ge(afree, na[0])
            pe.wait_ge(chosen, (l + 1) * (TILES + 2))
            for i in range(4):
                pe.matmul(ps[2 + i][:, :], ones[:, :], cT[:, :, :], start=True, stop=False, skip_group_check=True)

            def first(n, c):
                wait_apart(pe, go, gelud, n + 1)
                wait_apart(pe, go, uland[c], (n - c) * 4 + 16)
                for k in range(KD):
                    m = pe.matmul(ps[c % 2][:, 0:DT * P], us[c][:, k, :], hT[:, k, 0:DT * P],
                                  start=(k == 0), stop=(k == KD - 1))
                m.then_inc(uready, 1)

            def second(n, c):
                wait_apart(pe, go, mulr, n + 3)
                wait_apart(pe, go, vland[c % 2], (n - c) * 8 + 16 * (c // 2 + 1))
                for t in range(DT):
                    for h in range(2):
                        m = pe.matmul(ps[2 + 2 * t + h][:, :], cT[:, c % 2, t * P:(t + 1) * P],
                                      vs[c % 2][:, h * 512:(h + 1) * 512], start=False, stop=False, skip_group_check=True)
                m.then_inc(vdn, 1)

            def gates(n, c):
                wait_apart(pe, go, oready, n + 1)
                wait_apart(pe, go, gevac, n + 1)
                for i in range(OT):
                    m = pe.matmul(ps[6 + c % 2][:, i * CH:(i + 1) * CH], e2oh[c % 2][:, i, :], e1oh[c % 2][:, i, :],
                                  start=True, stop=True)
                m.then_inc(gready, 1)

            with pe.Fori(0, CH // CB) as j:
                for c in range(CB):
                    gates(j * CB + (l * NCH + c), c)
            first(l * NCH, 0)

            def chunks(j, r, more=True):
                for c in range(CB):
                    n = j * CB + (l * NCH + r * CH + c)
                    if more or c < CB - 1:
                        first(n + 1, (c + 1) % CB)
                    if r < RANGES - 1:
                        gates(n + CH, c)
                    second(n, c)

            for r in range(RANGES):
                with pe.Fori(0, CH // CB - (r == RANGES - 1)) as j:
                    chunks(j, r)
            chunks(CH // CB - 1, RANGES - 1, more=False)
            pe.wait_ge(vdn, (l + 1) * NCH + 2)
            pe.sem_inc(ydone, 1)
            pe.wait_ge(yfree, l + 1)
            for c in range(2):
                b = abank()
                pe.matmul(b[:, :], rep[:, :], hn[0:DEC, TILES, c * 512:(c + 1) * 512], start=True, stop=True)\
                    .then_inc(aready, 1)
            pe.wait_ge(decs, l + 1)
            b0, b1 = vbank(), vbank()
            for h in range(PH):
                if h % GRP == 0:
                    pe.wait_ge(rland[h // GRP], 64 * (l + 1) * (GROUPS // 2))
                for c, b in enumerate((b0, b1)):
                    m = pe.matmul(b[0:DEC, :], dw[:, h, :], ring[h][:, c * 512:(c + 1) * 512],
                                  start=(h == 0), stop=(h == PH - 1))
                if h % GRP == GRP - 1:
                    m.then_inc(rfree, 1)
            pe.wait_ge(rfree, (l + 1) * GROUPS + 2)
            pe.sem_inc(vready, 2)

        peer(0, 1)
        transposes(2)
        pe.wait_ge(afree, na[0])
        for _ in range(2):
            tlayout(abank, aready, na)
        for _ in range(2):
            tlayout(vbank, vready, nv)
        for _ in range(2):
            tlayout(abank, aready, na)
        pe.wait_ge(mixin, 6)
        for _ in range(2):
            natural(vbank, vready, cat)
        peer(1, 3)

    @block.scalar
    def _(act):
        na = [0]
        step = Chain(act, act_s)

        def take():
            g = na[0]
            na[0] += 1
            act.wait_ge(aready, g + 1)
            return ps[g % 4]

        def roots(n):
            act.wait_ge(meansq, n + 1)
            v = st[:, 40:40 + TILES + 1]
            act.activation(v, v, ACT.Sqrt).then_inc(rstd, 1)

        def t_out(norm):
            roots(norm)
            for t in range(TILES + 1):
                r = rows(t)
                for k0 in range(0, KD, 4):
                    b = take()
                    act.copy(hT[:, k0:k0 + 4, cols(t)],
                             b[:, :].rearrange("p (k c) -> p k c", k=4)[:, :, 0:r]).then_inc(afree, 1)

        act.dma_start(gain[:, :], ins["gain0"].broadcast_to([P, D])).then_inc(gland, 16)
        act.sem_inc(gelud, 2)
        act.sem_inc(gevac, 2)
        act.wait_ge(lamq, 1)
        step(act.activation(st[:, 8:10], st[:, 8:10], ACT.Exp))
        act.activation(st[:, 24:28], st[:, 24:28], ACT.Exp).then_inc(lamd, 1)
        t_out(0)
        act.wait_ge(normed, TILES + 1)
        act.wait_ge(aready, na[0])
        for j in range(3):
            for t in range(TILES + 1):
                b = take()
                act.copy(z[0:rows(t), t, j * AW:(j + 1) * AW], b[0:rows(t), :]).then_inc(afree, 1)
        for j in range(2):
            for c in range(RB):
                b = take()
                if j == 0:
                    act.copy(xp[:, c, RGC - 1:RGC - 1 + HALF], b[:, 0:HALF]).then_inc(afree, 1)
                else:
                    act.copy(grT[:, c, 0:HALF], b[:, 0:HALF]).then_inc(afree, 1)
                b = take()
                if j == 0:
                    step(act.copy(xp[:, c, RGC - 1 + HALF:RGC - 1 + SEQ], b[:, 0:SEQ - HALF]))
                    act.copy(xd[:, c, :, RGC - 1], b[:, SEQ - HALF:HALF]).then_inc(afree, 1)
                else:
                    act.copy(grT[:, c, HALF:TOK], b[:, 0:HALF]).then_inc(afree, 1)
        act.wait_ge(afree, na[0])
        act.dma_start(ohd, ins["c_ohd"]).then_inc(sconst, 16)
        act.dma_start(rbs, ins["rel_bias"]).then_inc(sconst, 16)
        act.dma_start(rb0, ins["rel_bias"][0:1, :].broadcast_to([DEC, HEADS])).then_inc(sconst, 16)
        act.dma_start(ohs, ins["c_oh"]).then_inc(sconst, 16)
        act.dma_start(rbx[0:BUCKETS, :], ins["rel_bias"]).then_inc(sconst, 16)
        act.dma_start(rbx[BUCKETS:BUCKETS + 1, :], ins["c_mask"]).then_inc(sconst, 16)
        k3 = outs["k_prompt"].rearrange("(t p) d -> p t d", p=P)
        v3 = outs["v_prompt"].rearrange("(t p) d -> p t d", p=P)
        act.dma_start(k3, z[:, 0:TILES, AW:2 * AW]).then_inc(tpost, 16)
        act.dma_start(v3, z[:, 0:TILES, 2 * AW:3 * AW]).then_inc(tpost, 16)
        act.dma_start(outs["k_sample"], z[0:DEC, TILES, AW:2 * AW]).then_inc(tpost, 16)
        act.dma_start(outs["v_sample"], z[0:DEC, TILES, 2 * AW:3 * AW]).then_inc(tpost, 16)
        for t in range(TILES):
            for part in range(2):
                b = take()
                dst = (qT if part == 0 else kT)[:, :, cols(t)]
                src = b[:, :].rearrange("p (h c) -> p h c", h=HEADS)
                act.mul(dst, src, HD ** -0.5 if part == 0 else 1.0).then_inc(afree, 1)
        for b_ in range(DEC):
            b = take()
            act.mul(qb[:, b_, :], b[:, :], HD ** -0.5).then_inc(afree, 1)
        b = take()
        for c in range(2):
            m = act.copy(bd[:, :, :].rearrange("p a (h c) -> p a h c", c=2)[:, :, :, c],
                         b[:, 0:(SUB + 1) * HEADS].rearrange("p (a h) -> p a h", a=SUB + 1))
            if c == 0:
                step(m)
            else:
                m.then_inc(afree, 1)
        act.wait_ge(afree, na[0])
        act.wait_ge(sconst, 16 * 6)
        for h in range(HEADS):
            if h:
                act.wait_ge(aready, na[0])
            act.copy(rbw, rbx[:, h:h + 1].broadcast_to([BUCKETS + 1, P])).then_inc(acts, 1)
            if h:
                act.wait_ge(pt_, 16 * h)
            b = take()
            step(act.copy(wide[:, 0:320], b[:, 0:320]))
            act.sem_inc(afree, 1)
            b = take()
            act.copy(wide[:, 320:SEQ + P - 1], b[:, 0:SEQ + P - 1 - 320]).then_inc(afree, 1)
            act.wait_ge(afree, na[0])
            act.sem_inc(toepl, 1)
        act.wait_ge(kdone, 1)
        act.activation(s[:, :, :, :], s[:, :, :, :], ACT.Exp).then_inc(expd, 1)
        def exps(n):
            w, m = (n % TILES + 1) * P, AST[n % 2]
            for c in range(2):
                act.wait_ge(scored, 2 * n + c + 1)
                act.activation(lg[:, n % 2, c, 0:w], lg[:, n % 2, c, 0:w], ACT.Exp,
                               bias=st[:, m + c:m + c + 1], accum_out=st[:, m + 2 + c:m + 3 + c]).then_inc(expd, 1)

        exps(0)
        for n in range(HEADS * TILES):
            h, i = divmod(n, TILES)
            if n + 1 < HEADS * TILES:
                exps(n + 1)
            if n % 2 == 1:
                act.wait_ge(odone, n // 2 + 1)
                act.copy(obs[:, n // 2, :], ps[7][0:8, :]).then_inc(ofree, 1)
            b = take()
            act.copy(pT[:, 0:(i + 1) * P], b[:, 0:(i + 1) * P]).then_inc(afree, 1)
            b = take()
            step(act.copy(cat[:, h, i * P:(i + 1) * P], b[:, 0:P]))
            act.sem_inc(afree, 1)
            if i == TILES - 1:
                act.activation(sq, cat[:, h, 0:SEQ], ACT.Square).then_inc(asm_, 1)
                act.wait_ge(headq, h + 1)
                act.activation(rs, rs, ACT.Sqrt).then_inc(headd, 1)
        act.wait_ge(dnorm, 1)
        act.activation(kq[:, 64:96], kq[:, 64:96], ACT.Sqrt).then_inc(dnorm, 1)
        act.wait_ge(rgst, 1)
        act.dma_start(wab[:, 0, :, :], ins["wa_bd"]).then_inc(sconst, 16)
        act.dma_start(wab[:, 1, :, :], ins["wi_bd"]).then_inc(sconst, 16)
        for m_, dst in enumerate((gr_, gi_)):
            for c in range(RB):
                for half in range(2):
                    b = take()
                    o = PRM["ba" if m_ == 0 else "bi"] + c
                    act.activation(dst[:, c, half * HALF:(half + 1) * HALF], b[:, 0:HALF], ACT.Sigmoid,
                                   bias=prm[:, o:o + 1]).then_inc(afree, 1)
        act.wait_ge(afree, na[0])
        act.wait_ge(rgst, 2)
        for c in range(RB):
            step(act.activation(gr_[:, c, :], gr_[:, c, :], ACT.Tanh, scale=st[:, 4 + c:5 + c]))
        act.activation(gg[:, :, :], grT[:, :, :], ACT.Gelu_apprx_tanh).then_inc(asm_, 1)
        act.wait_ge(headq, HEADS + 1)
        act.activation(gr_[:, :, :], gr_[:, :, :], ACT.Sqrt, scale=4.0).then_inc(headd, 1)
        act.wait_ge(rgst, 3)
        act.dma_start(outs["hs"], hs[:, :, SEQ - 1:TOK]).then_inc(tpost, 16)
        act.dma_start(outs["rgp"], xp[:, :, SEQ:SEQ + RGC - 1]).then_inc(tpost, 16)
        act.dma_start(outs["rgs"], xd[:, :, :, 1:RGC]).then_inc(tpost, 16)
        act.wait_ge(tpost, 16 * 7)

        def peer(l, norm):
            act.wait_ge(mixin, 5 + l)
            act.dma_start(keys[:, :, :], ins[f"keys{l}"]).then_inc(keyl, 16)
            t_out(norm)

            def queries(t):
                for g in range(HC // 4):
                    b = take()
                    act.copy(pq[:, t % 2, 4 * g:4 * g + 4, 0:rows(t)],
                             b[:, :].rearrange("p (a c) -> p a c", a=4)[:, :, 0:rows(t)]).then_inc(afree, 1)

            def scores(t):
                if l * (TILES + 1) + t:
                    act.wait_ge(scfree, l * (TILES + 1) + t)
                for g in range(HC // 4):
                    b = take()
                    act.copy(sc[0:rows(t), 4 * g:4 * g + 4, :],
                             b[0:rows(t), :].rearrange("p (a c) -> p a c", a=4)).then_inc(afree, 1)
                act.wait_ge(afree, na[0])
                act.sem_inc(peerd, 1)

            def exps(t):
                act.wait_ge(dexs, l * (TILES + 1) + t + 1)
                act.activation(s16[0:rows(t), :, :], s16[0:rows(t), :, :], ACT.Exp).then_inc(geld, 1)

            def turn(t):
                b = take()
                step(act.copy(eT[:, :, t * P:(t + 1) * P], b[:, 0:3 * P].rearrange("p (a c) -> p a c", a=3)))
                act.sem_inc(afree, 1)
                act.sem_inc(efree, 1)

            queries(0)
            queries(1)
            scores(0)
            queries(2)
            exps(0)
            scores(1)
            turn(0)
            queries(3)
            exps(1)
            scores(2)
            turn(1)
            queries(4)
            exps(2)
            scores(3)
            exps(3)
            scores(4)
            exps(4)

            def gelu(n, c):
                wait_apart(act, go, uready, n + 5)
                wait_apart(act, go, mulr, n + 1)
                act.activation(ga[:, c % 2, :], ps[c % 2][:, 0:DT * P], ACT.Gelu_apprx_tanh).then_inc(gelud, 1)

            def gates(n, c, tok):
                wait_apart(act, go, gready, n + 3)
                r = (n0[0] // CH) % 2
                act.copy(G[r][:, :, bass.ds(tok, OT)],
                         ps[6 + c % 2][:, 0:OT * CH].rearrange("p (t e) -> p e t", t=OT)).then_inc(gevac, 1)

            n0 = [0]
            with act.Fori(0, CH // CB) as j:
                for c in range(CB):
                    gates(j * CB + (l * NCH + c), c, j * (CB * OT) + c * OT)
            for r in range(RANGES):
                n0[0] = (r + 1) * CH
                with act.Fori(0, CH // CB) as j:
                    for c in range(CB):
                        n = j * CB + (l * NCH + r * CH + c)
                        gelu(n, c)
                        if r < RANGES - 1:
                            gates(n + CH, c, j * (CB * OT) + c * OT)
                if r % 2 == 0:
                    act.wait_ge(dotd, l * (GT + 1) + r // 2 + 1)
                    act.activation(dots[:, :], dots[:, :], ACT.Gelu_apprx_tanh).then_inc(acts, 1)
            act.wait_ge(yfree, l + 1)
            for c in range(2):
                b = take()
                act.copy(xrep[:, c * 512:(c + 1) * 512], b[:, :]).then_inc(afree, 1)
            act.wait_ge(afree, na[0])
            act.sem_inc(repd, 1)
            act.wait_ge(dotd, (l + 1) * (GT + 1))
            act.activation(ddot[:, :], ddot[:, :], ACT.Gelu_apprx_tanh).then_inc(acts, 1)

        def next_gain(n):
            act.wait_ge(gused, n)
            act.dma_start(gain[:, :], ins[f"gain{n}"].broadcast_to([P, D])).then_inc(gland, 16)

        next_gain(1)
        peer(0, 1)
        next_gain(2)
        t_out(2)
        act.wait_ge(afree, na[0])
        act.dma_start(cxd[:, :, :, 0:SCC - 1], ins["sbuf0"]).then_inc(sconst, 16)
        for dst in (cgT, None, bgT):
            if dst is None:
                continue
            for j in range(2):
                for c in range(BLK // P):
                    for half in range(2):
                        b = take()
                        act.copy(dst[:, j * 4 + c, half * HALF:(half + 1) * HALF], b[:, 0:HALF]).then_inc(afree, 1)
        act.wait_ge(rgst, 4)
        act.dma_start(outs["scp"], cxp[:, :, SEQ:SEQ + SCC - 1]).then_inc(sconst, 16)
        act.wait_ge(sconst, 160)
        act.dma_start(outs["scs"], cxd[:, :, :, 1:SCC]).then_inc(tpost, 16)
        act.wait_ge(tpost, 16 * 8)
        next_gain(3)
        peer(1, 3)
        next_gain(4)
        roots(4)

    @block.vector
    def _(dve):
        step = Chain(dve, dve_s)
        nv, nn = [0], [0]
        turns = [4, 0]

        def take():
            g = nv[0]
            nv[0] += 1
            dve.wait_ge(vready, g + 1)
            k, since = turns
            return ps[4 + (g - since) % k]

        def norm():
            n = nn[0]
            nn[0] += 1
            dve.wait_ge(gland, 16 * (n + 1))
            for t in range(TILES + 1):
                r = rows(t)
                step(dve.tensor_tensor_reduce(hn[0:r, t, :], xs[0:r, t, :], xs[0:r, t, :], 1.0 / D, EPS,
                                              ALU.mult, ALU.add, st[0:r, 40 + t:41 + t]))
            dve.sem_inc(meansq, 1)
            dve.wait_ge(rstd, n + 1)
            step(dve.reciprocal(st[:, 40:40 + TILES + 1], st[:, 40:40 + TILES + 1]))
            for t in range(TILES + 1):
                r = rows(t)
                dve.scalar_tensor_tensor(hn[0:r, t, :], xs[0:r, t, :], st[0:r, 40 + t:41 + t], gain[0:r, :], ALU.mult, ALU.mult)\
                    .then_inc(normed, 1)
                dve.wait_ge(normed, n * (TILES + 1) + t + 1)
            dve.sem_inc(gused, 1)

        def add_out():
            for j in range(2):
                for t in range(TILES + 1):
                    r = rows(t)
                    b = take()
                    x = xs[0:r, t, j * BLK:(j + 1) * BLK]
                    dve.tensor_tensor(x, x, b[0:r, :], ALU.add).then_inc(vfree, 1)
            dve.wait_ge(vfree, nv[0])

        step(dve.memset(st[:, :], 1.0))
        dve.wait_ge(consts, 16 * 9)
        for i in range(2):
            step(dve.tensor_tensor_reduce(lamv[:, 2 * i, :], lamv[:, 2 * i, :], lamv[:, 2 * i + 1, :], 1.0, 0.0,
                                          ALU.mult, ALU.add, st[:, 8 + i:9 + i]))
        lam_ = prm[:, PRM["lam"]:PRM["lam"] + RB]
        step(dve.scalar_tensor_tensor(st[:, 24:28], lam_, -1.0, lam_, ALU.mult, ALU.min))
        dve.sem_inc(lamq, 1)
        dve.sem_inc(kfree, PSLOTS)
        dve.sem_inc(rfree, 2)
        dve.sem_inc(mulr, 2)
        dve.sem_inc(efree, 1)
        dve.wait_ge(ptl, 16 * PG)
        step(dve.tensor_copy(pgf, pgi))
        step(dve.tensor_scalar(pgf, pgf, float(P // SUB), small[:, 40 + P:41 + P], ALU.mult, ALU.add))
        step(dve.tensor_copy(pgi, pgf))
        dve.sem_inc(pgready, 1)
        dve.wait_ge(xland, 32)
        norm()
        step(dve.memset(xp[:, :, 0:RGC - 1], 0.0))
        dve.wait_ge(sconst, 16 * 6)
        q_, k_ = z[0:DEC, TILES, 0:AW], z[0:DEC, TILES, AW:2 * AW]
        step(dve.tensor_tensor(snew, q_, k_, ALU.mult))
        step(dve.tensor_reduce(sn8, snew.rearrange("p (a d) -> p a d", d=HD), AX.X, ALU.add))
        step(dve.scalar_tensor_tensor(sn8.rearrange("p (h c) -> p h c", c=2), sn8.rearrange("p (h c) -> p h c", c=2),
                                      HD ** -0.5, rb0.unsqueeze(2).broadcast_to([DEC, HEADS, 2]), ALU.mult, ALU.add))
        step(dve.memset(s[:, :, PAGES, :], MASK))
        eye = ident[0:DEC, 0:DEC].unsqueeze(2).broadcast_to([DEC, DEC, 8])
        sd = sdg.rearrange("p (b c) -> p b c", b=DEC)
        step(dve.tensor_scalar(sd, eye, -MASK, MASK, ALU.mult, ALU.add))
        step(dve.tensor_tensor(s[0:DEC, :, PAGES, :], sn8.unsqueeze(1).broadcast_to([DEC, DEC, 8]), eye, ALU.mult))
        step(dve.tensor_tensor(s[0:DEC, :, PAGES, :], s[0:DEC, :, PAGES, :], sd, ALU.add))
        dve.wait_ge(afree, A_QB)
        ng = NG
        with dve.Fori(0, DEC) as b_:
            step.clear()
            for g in range(ng):
                kp = pages[:, g % PSLOTS, :, :]
                wait_apart(dve, go, kland[g % PSLOTS], b_ * (16 * ng // PSLOTS) + 16 * (g // PSLOTS + 1))
                step(dve.tensor_tensor(kp, kp, qb[:, bass.ds(b_, 1), :].broadcast_to([P, PG, AW]), ALU.mult))
                dve.tensor_reduce(s[:, bass.ds(b_, 1), g * PG:(g + 1) * PG, :].rearrange("p a j c -> p (a j c)"),
                                  kp.rearrange("p g c -> p (g c)").rearrange("p (a d) -> p a d", d=HD), AX.X, ALU.add)\
                    .then_inc(kfree, 1)
            wait_apart(dve, go, kfree, b_ * ng + ng + PSLOTS)
        step.clear()
        for b_ in range(DEC):
            last, far = s[:, b_, PAGES - SUB:PAGES, :], s[:, b_, 0:PAGES - SUB, :]
            dve.tensor_tensor(last, last, bd[:, 0:SUB, :], ALU.add).then_inc(dve_s, 1)
            dve.tensor_tensor(far, far, bd[:, SUB, :].unsqueeze(1).broadcast_to([P, PAGES - SUB, 8]), ALU.add)\
                .then_inc(dve_s, 1)
            step.n += 2
        dve.wait_ge(dve_s, step.n)
        mx = kq[:, 0:64]
        byc = s[:, :, :, :].rearrange("p b j c -> p b c j")
        mx3 = mx.rearrange("p (b c) -> p b c", b=DEC)
        dve.tensor_reduce(mx3, byc, AX.X, ALU.max).then_inc(mixin, 1)
        b = take()
        step(dve.tensor_reduce(st[0:64, 2:3], b[0:64, 0:P], AX.X, ALU.max))
        dve.sem_inc(vfree, 1)
        dve.tensor_scalar(kq[0:64, 64:128], ident[0:64, 0:64], st[0:64, 2:3], None, ALU.mult).then_inc(mixin, 1)
        b = take()
        step(dve.tensor_copy(kq[:, 0:64], b[:, 0:64]))
        dve.sem_inc(vfree, 1)
        step(dve.memset(kq[:, 64:128], 0.0))
        for b_ in range(DEC):
            v = s[:, b_, :, :]
            step(dve.tensor_tensor(v, v, kq[:, b_ * 8:b_ * 8 + 8].unsqueeze(1).broadcast_to([P, PAGES + 1, 8]),
                                   ALU.subtract))
        dve.sem_inc(kdone, 1)
        dve.wait_ge(expd, 1)
        dve.tensor_reduce(mx3, byc, AX.X, ALU.add).then_inc(mixin, 1)
        b = take()
        step(dve.reciprocal(kq[:, 128:160], b[:, 0:64].rearrange("p (a c) -> p a c", c=2)[:, :, 0]))
        step(dve.reciprocal(kq[:, 0:32], b[:, 0:64].rearrange("p (a c) -> p a c", c=2)[:, :, 1]))
        dve.sem_inc(vfree, 1)
        dve.wait_ge(lamd, 1)
        step(dve.tensor_tensor(st[:, 10:11], st[:, 8:9], st[:, 9:10], ALU.subtract))
        step(dve.tensor_scalar(st[:, 11:12], st[:, 10:11], LAM0, -1.0, ALU.add, ALU.mult))
        step(dve.tensor_scalar(st[:, 12:13], prm[:, PRM["subln"]:PRM["subln"] + 1], 1.0 - LAM0, None, ALU.mult))
        turns[:] = [3, nv[0]]

        def logits(n):
            h, i = divmod(n, TILES)
            w, m = (i + 1) * P, AST[n % 2]
            for c in range(2):
                b = take()
                dve.tensor_tensor(lg[:, n % 2, c, 0:w], b[:, 0:w], bias[:, h, (TILES - 1 - i) * P:SEQ], ALU.add)\
                    .then_inc(vfree, 1)
            for c in range(2):
                dve.wait_ge(vfree, nv[0] - 1 + c)
                dve.tensor_reduce(st[:, m + c:m + c + 1], lg[:, n % 2, c, 0:w], AX.X, ALU.max, negate=True)\
                    .then_inc(scored, 1)

        dve.wait_ge(pt_, 16 * HEADS)
        logits(0)
        for n in range(HEADS * TILES):
            h, i = divmod(n, TILES)
            w, m, l0 = (i + 1) * P, AST[n % 2], lg[:, n % 2, 0, 0:(i + 1) * P]
            if n + 1 < HEADS * TILES:
                logits(n + 1)
            dve.wait_ge(expd, 1 + 2 * n + 2)
            step(dve.reciprocal(st[:, m + 4:m + 6], st[:, m + 2:m + 4]))
            step(dve.tensor_scalar(l0, l0, st[:, m + 4:m + 5], None, ALU.mult))
            step(dve.tensor_tensor(st[:, m + 5:m + 6], st[:, m + 5:m + 6], st[:, 11:12], ALU.mult))
            dve.scalar_tensor_tensor(wt[:, n % 2, 0:w], lg[:, n % 2, 1, 0:w], st[:, m + 5:m + 6], l0, ALU.mult, ALU.add)\
                .then_inc(attn, 1)
            dve.wait_ge(attn, n + 1)
            if i == TILES - 1:
                b = take()
                step(dve.tensor_scalar(rs, b[:, :], 1.0 / P, EPS, ALU.mult, ALU.add))
                dve.sem_inc(vfree, 1)
                dve.sem_inc(headq, 1)
                dve.wait_ge(headd, h + 1)
                step(dve.reciprocal(rs, rs))
                step(dve.scalar_tensor_tensor(cat[:, h, 0:SEQ], cat[:, h, 0:SEQ], st[:, 12:13], rs, ALU.mult, ALU.mult))
        dve.wait_ge(odone, DEC + 1)
        o2 = ps[7][:, 0:64].rearrange("p (a c) -> p a c", c=2)
        step(dve.scalar_tensor_tensor(kq[:, 0:32], o2[:, :, 1], st[:, 11:12], kq[:, 0:32], ALU.mult, ALU.mult))
        step(dve.tensor_tensor(kq[:, 128:160], o2[:, :, 0], kq[:, 128:160], ALU.mult))
        turns[:] = [4, nv[0]]
        step(dve.tensor_tensor(kq[:, 0:32], kq[:, 0:32], kq[:, 128:160], ALU.add))
        dve.tensor_tensor(kq[:, 32:64], kq[:, 0:32], kq[:, 0:32], ALU.mult).then_inc(mixin, 1)
        b = take()
        step(dve.tensor_scalar(kq[:, 64:96], b[:, 0:32], 1.0 / P, EPS, ALU.mult, ALU.add))
        dve.sem_inc(vfree, 1)
        dve.sem_inc(dnorm, 1)
        dve.wait_ge(dnorm, 2)
        step(dve.reciprocal(kq[:, 64:96], kq[:, 64:96]))
        step(dve.scalar_tensor_tensor(cat[:, 0:HEADS, SEQ:TOK], kq[:, 0:32].rearrange("p (b h) -> p h b", h=HEADS),
                                      st[:, 12:13], kq[:, 64:96].rearrange("p (b h) -> p h b", h=HEADS),
                                      ALU.mult, ALU.mult))
        dve.wait_ge(tpost, 16 * 4)
        dve.wait_ge(hland, 32)
        for c in range(RB):
            for dst, src in ((xc[:, c, 0:SEQ], lambda i: xp[:, c, i:i + SEQ]), (xc[:, c, SEQ:TOK], lambda i: xd[:, c, :, i])):
                o = PRM["conv_w"] + c * RGC
                bb = PRM["conv_b"] + c
                step(dve.tensor_scalar(dst, src(0), prm[:, o:o + 1], prm[:, bb:bb + 1], ALU.mult, ALU.add))
                for i in range(1, RGC):
                    step(dve.scalar_tensor_tensor(dst, src(i), prm[:, o + i:o + i + 1], dst, ALU.mult, ALU.add))
        dve.sem_inc(rgst, 1)
        sp_ = st[:, 4:8]
        y_, t_, q2 = st[:, 24:28], st[:, 28:32], st[:, 32:36]
        dve.wait_ge(lamd, 1)
        step(dve.tensor_scalar(t_, y_, 2.0, None, ALU.add))
        step(dve.reciprocal(t_, t_))
        step(dve.tensor_tensor(y_, y_, t_, ALU.mult))
        step(dve.tensor_tensor(q2, y_, y_, ALU.mult))
        step(dve.memset(t_, 1.0 / 19))
        for k in range(17, 0, -2):
            step(dve.tensor_tensor(t_, t_, q2, ALU.mult))
            step(dve.tensor_scalar(t_, t_, 1.0 / k, None, ALU.add))
        step(dve.tensor_tensor(t_, t_, y_, ALU.mult))
        step(dve.tensor_scalar(y_, prm[:, PRM["lam"]:PRM["lam"] + 4], -1.0, 0.0, ALU.mult, ALU.max))
        step(dve.scalar_tensor_tensor(sp_, t_, 2.0, y_, ALU.mult, ALU.add))
        step(dve.tensor_scalar(sp_, sp_, 4.0, None, ALU.mult))
        dve.sem_inc(rgst, 1)
        dve.wait_ge(asm_, HEADS + 1)
        u = gr_[:, :, :]
        step(dve.tensor_scalar(ua, u, 1.0, None, ALU.add))
        step(dve.reciprocal(ua, ua))
        step(dve.tensor_scalar(ub, u, -1.0, 1.0, ALU.mult, ALU.add))
        step(dve.tensor_tensor(ub, ub, ua, ALU.mult))
        dve.sem_inc(headq, 1)
        dve.wait_ge(headd, HEADS + 1)
        step(dve.tensor_tensor(u, u, ua, ALU.mult))
        step(dve.tensor_tensor(u, u, gi_, ALU.mult))
        step(dve.tensor_tensor(u, u, xc, ALU.mult))
        for c in range(RB):
            step(dve.tensor_tensor_scan(hs[:, c, 0:SEQ], ub[:, c, 0:SEQ], u[:, c, 0:SEQ], 0.0, ALU.mult, ALU.add))
        dve.wait_ge(hland, 32)
        step(dve.tensor_tensor(hs[:, :, SEQ:TOK], ub[:, :, SEQ:TOK], h0s[:, :, :], ALU.mult))
        step(dve.tensor_tensor(hs[:, :, SEQ:TOK], hs[:, :, SEQ:TOK], u[:, :, SEQ:TOK], ALU.add))
        dve.sem_inc(rgst, 1)
        step(dve.tensor_tensor(cat[:, HEADS:HEADS + RB, :], hs, gg, ALU.mult))
        dve.sem_inc(mixin, 1)
        add_out()

        def choose(r, wait_places):
            def top16(n, row, best, where):
                first = step.n
                stages = (lambda i: dve.max(best(i)[:, 0:8], row(i)),
                          lambda i: dve.max_index(where(i)[:, 0:8], best(i)[:, 0:8], row(i)),
                          lambda i: dve.match_replace(row(i), best(i)[:, 0:8], row(i), LOW),
                          lambda i: dve.max(best(i)[:, 8:16], row(i)),
                          lambda i: dve.max_index(where(i)[:, 8:16], best(i)[:, 8:16], row(i)))
                for stage in stages:
                    for i in range(n):
                        if step.n >= first + n:
                            dve.wait_ge(dve_s, step.n - n + 1)
                        stage(i).then_inc(dve_s, 1)
                        step.n += 1
                dve.wait_ge(dve_s, step.n)

            top16(HC, lambda i: sc[0:r, i, :], lambda i: v16[0:r, i, :], lambda i: i16[0:r, i, :])
            dve.sem_inc(scfree, 1)
            dve.tensor_copy(i16f[0:r, :, :], i16[0:r, :, :]).then_inc(dve_s, 1)
            for h in range(PH):
                dve.tensor_tensor(cand[0:r, h, :].rearrange("p (a b) -> p a b", a=TOPK),
                                  v16[0:r, 2 * h, :].unsqueeze(2).broadcast_to([r, TOPK, TOPK]),
                                  v16[0:r, 2 * h + 1, :].unsqueeze(1).broadcast_to([r, TOPK, TOPK]), ALU.add)\
                    .then_inc(dve_s, 1)
            step.n += PH + 1
            dve.wait_ge(dve_s, step.n)
            top16(PH, lambda h: cand[0:r, h, :], lambda h: s16[0:r, h, :],
                  lambda h: c16[0:r, h * TOPK:(h + 1) * TOPK])
            step(dve.tensor_copy(gsum[0:r, :], s16[0:r, :, 0]))
            step(dve.tensor_tensor(s16[0:r, :, :], s16[0:r, :, :], gsum[0:r, :].unsqueeze(2).broadcast_to([r, PH, TOPK]),
                                   ALU.subtract))
            dve.sem_inc(dexs, 1)
            step(dve.tensor_scalar(chi[0:r, :], c16[0:r, :], 4, None, ALU.logical_shift_right))
            step(dve.tensor_scalar(clo[0:r, :], c16[0:r, :], 15, None, ALU.bitwise_and))
            step(dve.tensor_copy(hif[0:r, :], chi[0:r, :]))
            step(dve.tensor_copy(lof[0:r, :], clo[0:r, :]))
            wait_places()
            big = cand[0:r, :, :].rearrange("p h (k j) -> p h k j", j=TOPK)
            flat = cand[0:r, :, :].rearrange("p h (k j) -> p (h k) j", j=TOPK)
            for half, (pos, dst) in enumerate(((hif, e1f[0:r, :]), (lof, e2s[0:r, :]))):
                step(dve.tensor_tensor(flat, pos[0:r, :].unsqueeze(2).broadcast_to([r, SEL, TOPK]),
                                       small[0:r, 0:16].unsqueeze(1).broadcast_to([r, SEL, TOPK]), ALU.is_equal))
                idx = i16f[0:r, :, :].rearrange("p (h c) j -> p h c j", c=2)[:, :, half, :]
                step(dve.tensor_tensor(big, big, idx.unsqueeze(2).broadcast_to([r, PH, TOPK, TOPK]), ALU.mult))
                step(dve.tensor_reduce(dst, flat, AX.X, ALU.add))
            step(dve.scalar_tensor_tensor(e2f[0:r, 0, :], e1f[0:r, :], float(NKEY), e2s[0:r, :], ALU.mult, ALU.add))

        def gates(r, dst):
            step(dve.tensor_reduce(gsum[0:r, :], s16[0:r, :, :], AX.X, ALU.add))
            step(dve.reciprocal(gsum[0:r, :], gsum[0:r, :]))
            step(dve.tensor_tensor(dst, s16[0:r, :, :], gsum[0:r, :].unsqueeze(2).broadcast_to([r, PH, TOPK]), ALU.mult))

        def onehots(n, c, r, tok):
            wait_apart(dve, go, gready, n + 1)
            iota = io128[:, r * CH:(r + 1) * CH].unsqueeze(1).broadcast_to([P, OT, CH])
            k = step.n + 1
            dve.tensor_tensor(e1oh[c % 2], iota, eT[:, 0, bass.ds(tok, OT)].unsqueeze(2).broadcast_to([P, OT, CH]),
                              ALU.is_equal).then_inc(dve_s, 1)
            dve.tensor_tensor(e2oh[c % 2], io128[:, :].unsqueeze(1).broadcast_to([P, OT, P]),
                              eT[:, 1, bass.ds(tok, OT)].unsqueeze(2).broadcast_to([P, OT, P]), ALU.is_equal)\
                .then_inc(dve_s, 1)
            step.n += 2
            dve.wait_ge(dve_s, k)
            dve.tensor_tensor(e1oh[c % 2], e1oh[c % 2],
                              eT[:, 2, bass.ds(tok, OT)].unsqueeze(2).broadcast_to([P, OT, CH]), ALU.mult)\
                .then_inc(dve_s, 1)
            step.n += 1
            dve.wait_ge(dve_s, step.n)
            dve.sem_inc(oready, 1)

        def peer(l):
            norm()
            per = TILES + 2
            with dve.Fori(0, DT) as t:
                step.clear()
                wait_apart(dve, go, peerd, t + (l * (TILES + 1) + 1))
                choose(P, lambda: wait_apart(dve, go, efree, t + (l * DT + 1)))
                wait_apart(dve, go, geld, t + (l * (TILES + 1) + 1))
                gates(P, coef.rearrange("p (h k) -> p h k", h=PH))
                dve.sem_inc(chosen, 1)
            dve.wait_ge(efree, (l + 1) * DT + 1)
            with dve.Fori(0, GT) as t:
                step.clear()
                wait_apart(dve, go, peerd, t + (l * (TILES + 1) + DT + 1))
                choose(P, lambda: None)
                wait_apart(dve, go, geld, t + (l * (TILES + 1) + DT + 1))
                gates(P, coef.rearrange("p (h k) -> p h k", h=PH))
                step(dve.tensor_copy(gt[:, bass.ds(t, 1), :].rearrange("p a c -> p (a c)"), coef))
                step(dve.tensor_copy(eix[:, bass.ds(t, 1), :].rearrange("p a c -> p (a c)"), e2f[:, 0, :]))
                dve.sem_inc(chosen, 1)
            step.clear()
            dve.wait_ge(peerd, (l + 1) * (TILES + 1))
            choose(DEC, lambda: None)
            dve.wait_ge(geld, (l + 1) * (TILES + 1))
            gates(DEC, e2f[0:DEC, 1, :].rearrange("p (h k) -> p h k", h=PH))
            dve.sem_inc(chosen, 1)
            b = take()
            step(dve.tensor_tensor(dsel.rearrange("p a h k -> p (a h) k"), b[:, 0:2 * SEL].rearrange("p (a k) -> p a k", k=TOPK),
                                   small[:, 16:32].unsqueeze(1).broadcast_to([P, 2 * PH, TOPK]), ALU.mult))
            dve.sem_inc(vfree, 1)
            step(dve.tensor_reduce(dex, dsel.rearrange("p a h k -> p (a h) k"), AX.X, ALU.add))
            step(dve.tensor_copy(dix[:, :], dex[:, 0:PH]))
            step(dve.memset(cT[:, :, :], 0.0))
            dve.sem_inc(chosen, 1)
            with dve.Fori(0, CH // CB) as j:
                step.clear()
                for c in range(CB):
                    onehots(j * CB + (l * NCH + c), c, 0, j * (CB * OT) + c * OT)
            for r in range(RANGES):
                t, values = DT + r // 2, r % 2 == 1
                acc = (xs[:, t, :], hn[:, t, :])
                if values:
                    dve.wait_ge(acts, HEADS + l * (GT + 1) + r // 2 + 1)
                    step(dve.tensor_tensor(coef[:, :], dots[:, :], gt[:, r // 2, :], ALU.mult))
                    step(dve.memset(acc[1], 0.0))
                dve.wait_ge(gevac, l * NCH + (r + 1) * CH + 2)
                with dve.Fori(0, CH // CB) as j:
                    step.clear()
                    if values:
                        step(dve.tensor_copy(d16[:, :], coef[:, bass.ds(j * GBODY, GBODY)]))
                    for c in range(CB):
                        n = j * CB + (l * NCH + r * CH + c)
                        wait_apart(dve, go, gelud, n + 3)
                        wait_apart(dve, go, vdn, n + 1)
                        dve.tensor_tensor(cT[:, c % 2, :], ga[:, c % 2, :],
                                          G[r % 2][:, bass.ds(j * CB + c, 1), :].rearrange("p a t -> p (a t)"), ALU.mult)\
                            .then_inc(mulr, 1)
                        if r < RANGES - 1:
                            onehots(n + CH, c, r + 1, j * (CB * OT) + c * OT)
                        half = c % 2
                        base = l * (GROUPS // 2) + r * (SEL // GSLOTS)
                        wait_apart(dve, go, rland[half], j * 128 + 64 * (base + c // 2 + 1))
                        for i in range(GRP):
                            row, q = ring[half * GRP + i], c * GRP + i
                            if not values:
                                m = dve.tensor_tensor_reduce(row, row, hn[:, t, :], 1.0, 0.0, ALU.mult, ALU.add,
                                                             d16[:, q:q + 1])
                                if i < GRP - 1:
                                    m.then_inc(dve_s, 1)
                                    step.n += 1
                                else:
                                    step(m)
                            else:
                                step(dve.scalar_tensor_tensor(acc[i % 2], row, d16[:, q:q + 1], acc[i % 2],
                                                              ALU.mult, ALU.add))
                        dve.sem_inc(rfree, 1)
                    if not values:
                        step(dve.tensor_copy(dots[:, bass.ds(j * GBODY, GBODY)], d16[:, :]))
                step.clear()
                if values:
                    step(dve.tensor_tensor(acc[0], acc[0], acc[1], ALU.add))
                else:
                    dve.sem_inc(dotd, 1)
            dve.wait_ge(ydone, l + 1)
            for t in range(DT):
                for h in range(2):
                    x = xs[:, t, h * 512:(h + 1) * 512]
                    step(dve.tensor_tensor(x, x, ps[2 + 2 * t + h][:, :], ALU.add))
            dve.sem_inc(yfree, 1)
            dve.wait_ge(repd, l + 1)
            for h in range(PH):
                if h % GRP == 0:
                    dve.wait_ge(rland[h // GRP], 64 * ((l + 1) * (GROUPS // 2) - 1))
                step(dve.tensor_tensor_reduce(ring[h], ring[h], xrep, 1.0, 0.0, ALU.mult, ALU.add,
                                              ddot[:, h:h + 1]))
                if h % GRP == GRP - 1:
                    dve.sem_inc(rfree, 1)
            dve.sem_inc(dotd, 1)
            dve.wait_ge(acts, HEADS + (l + 1) * (GT + 1))
            step(dve.tensor_tensor(dcf, ddot, dex[:, PH:2 * PH], ALU.mult))
            step(dve.tensor_tensor(dw, small[:, 32:32 + DEC].unsqueeze(1).broadcast_to([P, PH, DEC]),
                                   dcf.unsqueeze(2).broadcast_to([P, PH, DEC]), ALU.mult))
            dve.sem_inc(decs, 1)
            for c in range(2):
                b = take()
                x = xs[0:DEC, TILES, c * 512:(c + 1) * 512]
                dve.tensor_tensor(x, x, b[0:DEC, :], ALU.add).then_inc(vfree, 1)
            dve.wait_ge(vfree, nv[0])
            dve.sem_inc(peerover, 1)

        peer(0)
        norm()
        step(dve.memset(cxp[:, :, 0:SCC - 1], 0.0))
        dve.wait_ge(afree, A_CG)
        for k in range(KD):
            b = take()
            dve.tensor_tensor(cxp[:, k, SCC - 1:SCC - 1 + HALF], b[:, 0:HALF], cgT[:, k, 0:HALF], ALU.mult)\
                .then_inc(vfree, 1)
            b = take()
            step(dve.tensor_tensor(cxp[:, k, SCC - 1 + HALF:SCC - 1 + SEQ], b[:, 0:SEQ - HALF], cgT[:, k, HALF:SEQ], ALU.mult))
            dve.tensor_tensor(cxd[:, k, :, SCC - 1], b[:, SEQ - HALF:HALF], cgT[:, k, SEQ:TOK], ALU.mult)\
                .then_inc(vfree, 1)
        dve.wait_ge(vfree, nv[0])
        dve.wait_ge(sconst, 16 * 9)
        dve.sem_inc(rgst, 1)
        for k in range(KD):
            o = PRM["sconv"] + k * SCC
            for dst, src in ((cvT[:, k, 0:SEQ], lambda i: cxp[:, k, i:i + SEQ]), (cvT[:, k, SEQ:TOK], lambda i: cxd[:, k, :, i])):
                step(dve.tensor_scalar(dst, src(0), prm[:, o:o + 1], None, ALU.mult))
                for i in range(1, SCC):
                    step(dve.scalar_tensor_tensor(dst, src(i), prm[:, o + i:o + i + 1], dst, ALU.mult, ALU.add))
        dve.wait_ge(afree, A_BG)
        step(dve.tensor_tensor(cat[:, :, :], cvT, bgT, ALU.mult))
        dve.sem_inc(mixin, 1)
        add_out()
        peer(1)
        norm()


def blocks(w, first=0, n=None):
    return np.ascontiguousarray(w.reshape(KD, P, -1, BLK).transpose(2, 1, 0, 3))


def chan(a, nb):
    a = a.reshape(*a.shape[:-1], nb, P)
    return np.ascontiguousarray(np.moveaxis(a, (-1, -2), (0, 1)))


def blockdiag(w):
    out = np.zeros((P, RB, P), w.dtype)
    h = P // 2
    for c in range(RB):
        out[:h, c, :h] = w[2 * c]
        out[h:, c, h:] = w[2 * c + 1]
    return out


OUTS = {"y_prompt": [SEQ, D], "y_sample": [DEC, D], "k_prompt": [SEQ, AW], "v_prompt": [SEQ, AW],
        "k_sample": [DEC, AW], "v_sample": [DEC, AW], "hs": [P, RB, DEC + 1], "rgp": [P, RB, RGC - 1],
        "rgs": [P, RB, DEC, RGC - 1], "scp": [P, KD, SCC - 1], "scs": [P, KD, DEC, SCC - 1]}


def kernel(**a):
    import concourse.bacc as bacc
    from concourse.bass_utils import run_bass_kernel_spmd

    a = {k: np.asarray(v) for k, v in a.items()}
    f = {
        "x_prompt": a["x_prompt"][0], "x_sample": a["x_sample"][:, 0],
        "cache_k": a["cache_k"][0].reshape(-1, SUB * AW), "cache_v": a["cache_v"][0].reshape(-1, SUB * AW),
        "page_table": a["page_table"].reshape(DEC * NG, PG).T, "rel_bias": a["rel_bias"],
        "gain0": a["norm_mix"][0:1], "gain1": a["norm_ffn"][0:1], "gain2": a["norm_mix"][1:2],
        "gain3": a["norm_ffn"][1:2], "gain4": a["norm_final"].reshape(1, D),
        "w_in_a": blocks(a["w_in_a"][0]), "w_out_a": blocks(a["w_out_a"][0]), "w_in_c": blocks(a["w_in_c"][0]),
        "w_out_c": blocks(a["w_out_c"][0]), "wq0": blocks(a["peer_wq"][0]), "wq1": blocks(a["peer_wq"][1]),
        "lambda_q1": a["lambda_q1"], "lambda_k1": a["lambda_k1"], "lambda_q2": a["lambda_q2"],
        "lambda_k2": a["lambda_k2"],
        "wa_bd": blockdiag(a["rg_wa"][0]), "wi_bd": blockdiag(a["rg_wi"][0]),
        "h0": chan(a["state_rglru_h"][0], RB),
        "rgbuf": chan(a["state_rglru_conv"][0], RB), "sbuf0": chan(a["state_sconv"][0], KD),
    }
    prm = np.zeros((P, NPRM), np.float32)
    prm[:, 0:16] = chan(a["rg_conv_w"][0], RB).reshape(P, -1)
    prm[:, 16:20] = chan(a["rg_conv_b"][0], RB)
    prm[:, 20:24] = chan(a["rg_ba"][0], RB)
    prm[:, 24:28] = chan(a["rg_bi"][0], RB)
    prm[:, 28:32] = chan(a["rg_lambda"][0], RB)
    prm[:, 32] = a["subln_g"][0]
    prm[:, 33:] = chan(a["sc_conv_w"][0], KD).reshape(P, -1)
    f["prm"] = prm
    for l in range(2):
        f[f"keys{l}"] = a["peer_keys"][l].transpose(3, 0, 1, 2).reshape(P, HC, NKEY)
        f[f"peer_u{l}"] = a["peer_u"][l]
        f[f"peer_ut{l}"] = a["peer_u"][l].reshape(NCH, P, KD, P).transpose(0, 3, 2, 1).reshape(NCH * P, KD, P)
        f[f"peer_v{l}"] = a["peer_v"][l]
    f.update(shape_constants())
    f["c_mask"] = np.full((1, HEADS), MASK, np.float32)

    nc = bacc.Bacc("TRN2", target_bir_lowering=False, num_devices=1)
    arrays, ins, outs = {}, {}, {}
    for name, v in f.items():
        v = np.ascontiguousarray(v)
        arrays[name + "_in"] = v
        ins[name] = nc.dram_tensor(name + "_in", v.shape, mybir.dt.from_np(v.dtype), kind="ExternalInput").ap()
    ins["skew"] = nc.dram_tensor("skew", [HEADS, P, SEQ + P - 1], F32).ap()
    for name, shape in OUTS.items():
        outs[name] = nc.dram_tensor(name, shape, F32, kind="ExternalOutput").ap()
    build(nc, ins, outs)
    r = run_bass_kernel_spmd(nc, [arrays], core_ids=[0]).results[0]

    def back(v):
        v = np.moveaxis(v, (0, 1), (-1, -2))
        return np.ascontiguousarray(v.reshape(*v.shape[:-2], -1))

    kv = lambda v: v.reshape(1, 1, SEQ, HEADS, P)
    kvs = lambda v: v.reshape(1, DEC, 1, HEADS, P)
    h = back(r["hs"])
    return (r["y_prompt"].reshape(1, SEQ, D), r["y_sample"].reshape(DEC, 1, D), kv(r["k_prompt"]), kv(r["v_prompt"]),
            kvs(r["k_sample"]), kvs(r["v_sample"]), h[0:1].reshape(1, 1, AW), h[1:].reshape(1, DEC, AW),
            back(r["rgp"]).reshape(1, 1, RGC - 1, AW), back(r["rgs"]).reshape(1, DEC, RGC - 1, AW),
            back(r["scp"]).reshape(1, 1, SCC - 1, D), back(r["scs"]).reshape(1, DEC, SCC - 1, D))
```

```python
import math
from contextlib import ExitStack

import concourse.bass as bass
import numpy as np
from concourse import mybir

F32 = mybir.dt.float32
I32 = mybir.dt.int32
U32 = mybir.dt.uint32
ALU = mybir.AluOpType
ACT = mybir.ActivationFunctionType
AX = mybir.AxisListType

P = 128
D = 1024
KD = D // P
SEQ = 512
TILES = SEQ // P
DEC = 8
TOK = SEQ + DEC
HALF = TOK // 2
HEADS = 4
HD = 64
AW = 512
PAST = 4096
PAGES = PAST // P
NPHYS = 320
RB = 4
RGC = 4
SCC = 3
BUCKETS = 32
PH = 8
TOPK = 16
NKEY = 128
NEXP = NKEY * NKEY
HC = 2 * PH
SEL = PH * TOPK
EPS = 1e-6
LOW = -3.0e38
MASK = -1.0e30
LAM0 = 0.8 - 0.6 * math.exp(0.0)
BLK = 512
PG = 2
NG = PAGES // PG
GP = PG * P
VALUE_AHEAD = 4
VALUE_LAG = 9
SUB = GP // P
PSLOTS = 4
GSLOTS = 8
GBODY = 2 * GSLOTS
LAST = SEL // GBODY
GRP = 4
DT = 2
GT = TILES - DT
NCH = NEXP // P
RANGES = 4
CH = NCH // RANGES
CB = 4
OT = DT * P // CH
DP = DEC * PH
DK = DEC * SEL // P
DG = 2 * DK // GRP

PRM = dict(conv_w=0, conv_b=16, ba=20, bi=24, lam=28, subln=32, sconv=33)
NPRM = 33 + KD * SCC


def bucket(dist):
    exact = BUCKETS // 2
    n = np.maximum(dist, 0)
    nf = np.maximum(n, 1).astype(np.float32)
    far = exact + (np.log(nf / np.float32(exact)) / np.float32(math.log(128 / exact))
                   * np.float32(BUCKETS - exact)).astype(np.int32)
    return np.where(n < exact, n, np.minimum(far, BUCKETS - 1))


def shape_constants():
    j = np.arange(SEQ + P - 1)
    oh = np.zeros((BUCKETS + 1, SEQ + P - 1), np.float32)
    dist = SEQ - 1 - j
    ok = dist >= 0
    oh[bucket(dist)[ok], j[ok]] = 1.0
    oh[BUCKETS, ~ok] = 1.0
    b = bucket(PAST - np.arange(PAST))
    assert (b[:-GP] == BUCKETS - 1).all()
    ohd = np.zeros((BUCKETS, SUB + 1, P), np.float32)
    ohd[BUCKETS - 1, SUB, :] = 1.0
    for i in range(SUB):
        ohd[b[-GP + i::SUB], i, np.arange(P)] = 1.0
    ident = np.eye(P, dtype=np.float32)
    sel = np.zeros((DEC, DEC, P), np.float32)
    for i in range(DEC):
        sel[i, i] = 1.0
    part = np.arange(P)
    rep = (part[None, :] % DEC == np.arange(DEC)[:, None]).astype(np.float32)
    small = np.zeros((P, 16 + 16 + DEC + P + 1), np.float32)
    small[:, 40 + P] = part % (P // PG)
    small[:, 40:40 + P] = np.arange(P)
    small[:, 0:16] = np.arange(16)
    small[:, 32:32 + DEC] = part[:, None] % DEC == np.arange(DEC)[None, :]
    return {"c_oh": oh, "c_ohd": ohd, "c_ident": ident, "c_sel": sel, "c_rep": rep, "c_small": small}


class Chain:

    def __init__(self, eng, sem):
        self.eng, self.sem, self.n = eng, sem, 0

    def __call__(self, ins):
        self.n += 1
        ins.then_inc(self.sem, 1)
        self.eng.wait_ge(self.sem, self.n)

    def clear(self):
        self.eng.sem_clear(self.sem)
        self.n = 0


def wait_apart(eng, go, sem, value):
    eng.wait_ge(sem, value)
    eng.sem_inc(go, 1)


def rows(t):
    return P if t < TILES else DEC


def cols(t):
    return slice(t * P, t * P + rows(t))


EARLY = DEC // 2 * NG
TICKS = DEC * NG


def keys_by(tick):
    return min(DEC * NG, EARLY + -(-(DEC * NG - EARLY) * (tick + 1) // (TICKS - NG)))


def attention_order():
    order = []
    for turn in range(DEC + 1):
        for tick in range(NG):
            now = turn * NG + tick
            for n in range(keys_by(now - 1) if now else EARLY, keys_by(now)):
                order.append(("keys", n))
            if turn < DEC and tick in (0, 2, 4, 6):
                order.append(({0: "maximum", 2: "spread", 4: "subtract", 6: "sum"}[tick], turn))
            v = now - VALUE_LAG
            if 0 <= v < DEC * NG:
                order.append(("values", v))
                if v % NG == NG - 1:
                    order.append(("keep", v // NG))
            n = 2 * turn
            if turn < DEC:
                if n == 0 and tick == 7:
                    order.append(("logits", 0))
                if tick in (8, 12) and n + tick // 4 - 1 < HEADS * TILES:
                    order.append(("logits", n + tick // 4 - 1))
                if tick in (9, 13):
                    order.append(("weights", n + (tick == 13)))
                if tick in (10, 14):
                    order.append(("outputs", n + (tick == 14)))
            if turn >= 1 and tick == 5 and n % TILES == 0:
                order.append(("headnorm", n // TILES - 1))
    return order


def build(nc, ins, outs):
    with ExitStack() as ctx:
        program(nc, ins, outs, ctx)


def program(nc, ins, outs, ctx):
    def sb(name, shape, dt=F32):
        return ctx.enter_context(nc.sbuf_tensor(name, shape, dt))

    def sem(name):
        return ctx.enter_context(nc.semaphore(name))

    xs = sb("xs", [P, TILES + 1, D])
    hn = sb("hn", [P, TILES + 1, D])
    hT = sb("hT", [P, KD, TOK])
    gain = sb("gain", [P, D])
    ident = sb("ident", [P, P])
    ones = sb("ones", [P, P])
    rep = sb("rep", [DEC, P])
    small = sb("small", [P, 16 + 16 + DEC + P + 1])
    io128 = small[:, 40:40 + P]
    prm = sb("prm", [P, NPRM])
    h0s = sb("h0s", [P, RB, DEC])
    st = sb("st", [P, 64])
    kq = sb("kq", [P, 160])
    AREA = 36860
    area = sb("area", [P, AREA])

    def at(off, *shape):
        n = math.prod(shape)
        assert off + n <= AREA, (off, shape)
        v = area[:, off:off + n]
        if len(shape) == 2:
            v = v.rearrange("p (a b) -> p a b", a=shape[0])
        elif len(shape) == 3:
            v = v.rearrange("p (a b c) -> p a b c", a=shape[0], b=shape[1])
        return v

    cat = hT
    wr = area[:, 26400:26400 + 2 * KD * BLK].rearrange("p (s k c) -> p s k c", s=2, k=KD)
    lamv = at(24000, 4, HD)
    selb = area[0:DEC, 34600:34600 + DEC * P].rearrange("p (b c) -> p b c", b=DEC)
    z = at(0, TILES + 1, 3 * AW)
    qT = at(7680, HEADS, SEQ)
    kT = at(9728, HEADS, SEQ)
    xp = at(11776, RB, SEQ + RGC - 1)
    xd = at(13836, RB, DEC, RGC)
    grT = at(13964, RB, TOK)
    s = at(16044, DEC, PAGES + 1, 8)
    pages = [at(18156 + i * SUB * AW, SUB, AW) for i in range(PSLOTS)]
    vpages = [at(18156 + i * SUB * AW, SUB, AW) for i in range(PSLOTS, 2 * PSLOTS)] + \
             [gain[:, :].rearrange("p (a c) -> p a c", a=SUB)]
    pgi = area[:, 35640:35640 + DEC * NG].bitcast(I32)
    pgf = at(35640 + DEC * NG, DEC * NG)
    qb = hn[:, 0:TILES, :].rearrange("p t c -> p (t c)").rearrange("p (b c) -> p b c", b=DEC)
    obs = hn[0:8, 0:TILES, :].rearrange("p t c -> p (t c)").rearrange("p (b c) -> p b c", b=DEC)
    bias = at(26400, HEADS, SEQ)
    lg = at(28448, 2, 2, SEQ)
    wt = at(30496, 2, SEQ)
    pT = at(31520, SEQ)
    sq = at(32032, SEQ)
    rs = at(32544, SEQ)
    wide = at(33056, SEQ + P - 1)
    ohs = area[0:BUCKETS + 1, 33700:33700 + SEQ + P - 1]
    rbx = area[0:BUCKETS + 1, 34340:34340 + HEADS]
    rbw = area[0:BUCKETS + 1, 34350:34350 + P]
    bd = hn[:, TILES, 0:(SUB + 1) * 8].rearrange("p (a b) -> p a b", a=SUB + 1)
    ohd = area[0:BUCKETS, 35900:35900 + (SUB + 1) * P].rearrange("p (a b) -> p a b", a=SUB + 1)
    rbs = hn[0:BUCKETS, TILES, 400:404]
    rb0 = hn[0:DEC, TILES, 408:412]
    snew = hn[0:DEC, TILES, 512:1024]
    sn8 = hn[0:DEC, TILES, 416:424]
    sdg = hn[0:DEC, TILES, 432:496]
    xc = at(0, RB, TOK)
    gr_ = at(2080, RB, TOK)
    hs = gr_
    gi_ = at(4160, RB, TOK)
    ua = at(6240, RB, TOK)
    ub = at(8320, RB, TOK)
    root4u = at(18156, RB, TOK)
    gg = at(20236, RB, TOK)
    wab = at(22316, 2, RB, P)
    cgT = at(0, KD, TOK)
    cxp = at(4160, KD, SEQ + SCC - 1)
    cxd = at(8272, KD, DEC, SCC)
    bgT = at(8464, KD, TOK)
    cvT = at(12624, KD, TOK)
    wqs = [at(j * KD * BLK, KD, BLK) for j in range(4)]
    keys = at(16384, HC, NKEY)
    pq = at(18432, 2, HC, P)
    sc = at(22528, HC, NKEY)
    v16 = at(24832, HC, TOPK)
    i16 = area[:, 25088:25344].bitcast(U32).rearrange("p (a b) -> p a b", a=HC)
    i16f = at(25344, HC, TOPK)
    cand = at(25600, PH, 256)
    s16 = at(27648, PH, TOPK)
    c16 = area[:, 27776:27904].bitcast(U32)
    chi = area[:, 27904:28032].bitcast(U32)
    clo = area[:, 28032:28160].bitcast(U32)
    hif = at(28160, SEL)
    lof = at(28288, SEL)
    e1f = at(28416, SEL)
    e2f = at(28544, 2, SEL)
    e2s = at(28808, SEL)
    gsum = at(28800, PH)
    scd = area[0:DP, 24576:24576 + 2 * NKEY].rearrange("p (c n) -> p c n", c=2)
    pqd = at(35820, 2, PH, DP)
    e2o0 = [at(8192 + i * OT * P, OT, P) for i in range(2)]
    e1o0 = [at(10240 + i * OT * CH, OT, CH) for i in range(2)]
    eT = at(29000, 3, DT * P)
    eix = area[:, 29768:29768 + GT * SEL].bitcast(I32).rearrange("p (a b) -> p a b", a=GT)
    gt = at(30024, GT, SEL)
    dots = at(30280, SEL)
    coef = at(30408, SEL)
    d16 = at(30536, GBODY)
    ixs = area[:, 30552:30568].bitcast(I32)
    dex = at(30568, 2 * DK)
    dix = area[:, 30584:30592].bitcast(I32)
    ddot = at(30592, PH)
    dcf = at(30600, PH)
    dw = at(30608, PH, DEC)
    G = [at(i * CH * DT * P, CH, DT * P) for i in range(2)]
    us = [at(16384 + i * D, KD, P) for i in range(4)]
    vs = [at(20480 + i * D, D) for i in range(2)]
    e2oh = [at(22528 + i * OT * P, OT, P) for i in range(2)]
    e1oh = [at(24576 + i * OT * CH, OT, CH) for i in range(2)]
    ga = at(25088, 2, DT * P)
    cT = at(25600, 2, DT * P)
    ring = [at(30700 + i * D, D) for i in range(6)] + [hn[:, i, :] for i in range(2)]
    xrep = gain[:, :]

    ps = [ctx.enter_context(nc.psum_tensor(f"ps{i}", [P, 512], F32)) for i in range(8)]

    go = sem("go")
    dve_steps, act_steps, pool_steps = sem("dve_steps"), sem("act_steps"), sem("pool_steps")
    consts = sem("consts")
    x_landed = sem("x_landed")
    gain_landed = sem("gain_landed")
    gain_used = sem("gain_used")
    weights_landed = [sem("weights_landed0"), sem("weights_landed1")]
    weights_used = sem("weights_used")
    wq_landed = sem("wq_landed")
    peer_keys_landed = sem("peer_keys_landed")
    state_landed = sem("state_landed")
    scalar_dmas = sem("scalar_dmas")
    stored = sem("stored")
    outputs_stored = sem("outputs_stored")
    act_bank_full, act_bank_free = sem("act_bank_full"), sem("act_bank_free")
    dve_bank_full, dve_bank_free = sem("dve_bank_full"), sem("dve_bank_free")
    mean_squares_ready, roots_ready = sem("mean_squares_ready"), sem("roots_ready")
    normed = sem("normed")
    lambda_ready, lambda_exps_ready = sem("lambda_ready"), sem("lambda_exps_ready")
    mixer_steps = sem("mixer_steps")
    conv_steps = sem("conv_steps")
    conved = sem("conved")
    act_results = sem("act_results")
    wide_ready = sem("wide_ready")
    bias_landed = sem("bias_landed")
    page_table_landed, page_rows_ready = sem("page_table_landed"), sem("page_rows_ready")
    key_slots_free = sem("key_slots_free")
    keys_landed = [sem(f"keys_landed{i}") for i in range(PSLOTS)]
    value_slots_free = sem("value_slots_free")
    values_landed = [sem(f"values_landed{i}") for i in range(len(vpages))]
    dec_maxima = sem("dec_maxima")
    dec_logits_ready = sem("dec_logits_ready")
    dec_exps_ready = sem("dec_exps_ready")
    dec_sums_done = sem("dec_sums_done")
    dec_sums_kept = sem("dec_sums_kept")
    dec_norm_steps = sem("dec_norm_steps")
    block_logits_ready = sem("block_logits_ready")
    block_exps_ready = sem("block_exps_ready")
    block_weights_ready = sem("block_weights_ready")
    act_parts_ready = sem("act_parts_ready")
    head_squares_ready, head_roots_ready = sem("head_squares_ready"), sem("head_roots_ready")
    zeros_ready = sem("zeros_ready")
    queried = sem("queried")
    scores_ready = sem("scores_ready")
    scores_used = sem("scores_used")
    top_scores_ready = sem("top_scores_ready")
    top_exps_ready = sem("top_exps_ready")
    chosen = sem("chosen")
    indices_turned = sem("indices_turned")
    row_groups_free = sem("row_groups_free")
    rows_landed = [sem(f"rows_landed{i}") for i in range(2)]
    dots_ready = sem("dots_ready")
    dec_rows_spread = sem("dec_rows_spread")
    dec_coefs_ready = sem("dec_coefs_ready")
    u_landed = [sem(f"u_landed{i}") for i in range(4)]
    v_landed = [sem(f"v_landed{i}") for i in range(2)]
    first_done = sem("first_done")
    gelu_done = sem("gelu_done")
    coefs_ready = sem("coefs_ready")
    second_done = sem("second_done")
    onehots_ready = sem("onehots_ready")
    gates_in_psum = sem("gates_in_psum")
    gates_in_sbuf = sem("gates_in_sbuf")
    dense_sums_done, dense_sums_taken = sem("dense_sums_done"), sem("dense_sums_taken")
    peer_done = sem("peer_done")

    BLOCK_STATS = (16, 48)

    block = ctx.enter_context(nc.Block())

    W_ORDER = [("w_in_a", j) for j in range(5)] + [("w_out_a", j) for j in range(2)] + \
              [("w_in_c", j) for j in (2, 3, 4, 5, 0, 1)] + [("w_out_c", j) for j in range(2)]

    A_Q = 2 * (TILES + 1) + TILES + 1 + DEC
    A_QB = 2 * (TILES + 1) + 3 * (TILES + 1) + 2 * 2 * RB + 2 * TILES + DEC + 1
    A_PEER = 2 * (TILES + 1) + PH + 1 + HC // 4 * (2 * TILES - 1) + DT + 2
    A_CG = A_QB + 2 * HEADS + 2 * HEADS * TILES + 4 * RB + A_PEER + 2 * (TILES + 1) + 2 * KD
    A_BG = A_CG + 2 * KD

    GROUPS = GT * 2 * SEL // GRP + 2 * PH // GRP

    n_stores = [0]

    @block.sync
    def _(sp):
        for c, v in (("c_ident", ident[:, :]), ("c_sel", selb[:, :, :]), ("c_rep", rep[:, :]),
                     ("c_small", small[:, :]), ("prm", prm[:, :])):
            sp.dma_start(v, ins[c]).then_inc(consts, 16)
        for i, n in enumerate(("lambda_q1", "lambda_k1", "lambda_q2", "lambda_k2")):
            sp.dma_start(lamv[:, i, :], ins[n].broadcast_to([P, HD])).then_inc(consts, 16)
        sp.dma_start(h0s[:, :, :], ins["h0"]).then_inc(state_landed, 16)
        sp.dma_start(xd[:, :, :, 0:RGC - 1], ins["rgbuf"]).then_inc(state_landed, 16)
        x3 = ins["x_prompt"].rearrange("(t p) d -> p t d", p=P)
        sp.dma_start(xs[:, 0:TILES, :], x3).then_inc(x_landed, 16)
        sp.dma_start(xs[0:DEC, TILES, :], ins["x_sample"]).then_inc(x_landed, 16)

        for i in range(PG):
            sp.dma_start(pgi[i * (P // PG):(i + 1) * (P // PG), :],
                         ins["page_table"][i:i + 1, :].broadcast_to([P // PG, DEC * NG])).then_inc(page_table_landed, 16)

        nblk = [0]

        def weight(k=1):
            for _ in range(k):
                n = nblk[0]
                name, j = W_ORDER[n]
                if n >= 2:
                    sp.wait_ge(weights_used, n - 1)
                sp.dma_start(wr[:, n % 2, :, :], ins[name][j]).then_inc(weights_landed[n % 2], 16)
                nblk[0] += 1

        weight(5)

        for h in range(HEADS):
            sp.wait_ge(wide_ready, h + 1)
            sp.dma_start(ins["skew"][h], wide).then_inc(stored, 16)
            n_stores[0] += 1
            sp.wait_ge(stored, 16 * n_stores[0])
            n = SEQ + P - 1
            src = bass.AP(ins["skew"].tensor, h * P * n + P - 1, [[n - 1, P], [1, SEQ]])
            sp.dma_start(bias[:, h, :], src).then_inc(bias_landed, 16)
            sp.wait_ge(bias_landed, 16 * (h + 1))

        sp.wait_ge(conv_steps, 1)
        weight(2)

        def tables(l):
            sp.wait_ge(mixer_steps, 5 + l)
            sp.wait_ge(outputs_stored, 16 * (7 + l))
            sp.wait_ge(scalar_dmas, 16 * (8 + 2 * l))
            for j in range(4):
                sp.dma_start(wqs[j], ins[f"wq{l}"][j]).then_inc(wq_landed, 16)
            sp.wait_ge(scores_ready, (l + 1) * (TILES + 1))
            with sp.Fori(0, NCH // CB) as j:
                for c in range(CB):
                    wait_apart(sp, go, first_done, j * CB + (l * NCH + c + 1))
                    sp.dma_start(us[c], ins[f"peer_ut{l}"][bass.ds(j * (CB * P) + c * P, P), :, :])\
                        .then_inc(u_landed[c], 16)
                    wait_apart(sp, go, second_done, j * CB + (l * NCH + c + 1))
                    sp.dma_start(vs[c % 2], ins[f"peer_v{l}"][bass.ds(j * (CB * P) + c * P, P), :])\
                        .then_inc(v_landed[c % 2], 16)

        tables(0)
        sp.wait_ge(peer_done, 1)
        weight(6)
        weight(2)
        tables(1)
        assert nblk[0] == len(W_ORDER)
        y3 = outs["y_prompt"].rearrange("(t p) d -> p t d", p=P)
        for t in range(TILES + 1):
            sp.wait_ge(normed, 4 * (TILES + 1) + t + 1)
            dst = y3[:, t, :] if t < TILES else outs["y_sample"]
            sp.dma_start(dst, hn[0:rows(t), t, :]).then_inc(stored, 16)
            n_stores[0] += 1
        sp.wait_ge(stored, 16 * (n_stores[0]))
        sp.wait_ge(scalar_dmas, 16 * 10)

    @block.gpsimd
    def _(pool):
        pool.memset(ones[:, :], 1.0).then_inc(go, 1)
        pool.wait_ge(go, 1)

        def page_gather(cache, slots, n, free, landed):
            pool.wait_ge(free, n + 1)
            pool.indirect_dma_start(slots[n % len(slots)].rearrange("p a c -> p (a c)"), None, ins[cache],
                                    bass.IndirectOffsetOnAxis(ap=pgi[:, n:n + 1], axis=0)).then_inc(landed[n % len(slots)], 16)

        pool.wait_ge(page_rows_ready, 1)
        k = v = 0
        for tick in range(TICKS + VALUE_LAG):
            while k < min(DEC * NG, keys_by(tick) + PSLOTS):
                page_gather("cache_k", pages, k, key_slots_free, keys_landed)
                k += 1
            if v < min(DEC * NG, tick - VALUE_LAG + len(vpages) + VALUE_AHEAD):
                page_gather("cache_v", vpages, v, value_slots_free, values_landed)
                v += 1

        def group(l, what, idx, half):
            for i in range(GRP):
                r = half * GRP + i
                pool.indirect_dma_start(ring[r], None, ins[what + str(l)],
                                        bass.IndirectOffsetOnAxis(ap=idx[:, i:i + 1], axis=0)).then_inc(rows_landed[half], 16)

        def gathers(l, what, tile_ix, g0):
            with pool.Fori(0, LAST) as i:
                pool.sem_clear(pool_steps)
                for n in range(GBODY // GRP):
                    if n % 2 == 0:
                        o = n // 2 * GSLOTS
                        pool.tensor_copy(ixs[:, o:o + GSLOTS], tile_ix[:, bass.ds(i * GBODY + o, GSLOTS)])\
                            .then_inc(pool_steps, 1)
                    wait_apart(pool, go, row_groups_free, i * (GBODY // GRP) + (g0 + n + 1))
                    pool.wait_ge(pool_steps, n // 2 + 1)
                    group(l, what, ixs[:, n * GRP:(n + 1) * GRP], n % 2)

        for l in range(2):
            base = l * GROUPS
            pool.wait_ge(mixer_steps, 5 + l)
            pool.memset(pqd, 0.0).then_inc(zeros_ready, 1)
            pool.wait_ge(chosen, l * (TILES + 2) + 2)
            for n, what in enumerate(("peer_u", "peer_v")):
                for half in range(2):
                    pool.wait_ge(row_groups_free, base + 2 * n + half + 1)
                    group(l, what, dix[:, half * GRP:(half + 1) * GRP], half)
            for t in reversed(range(GT)):
                pool.wait_ge(chosen, l * (TILES + 2) + (3 if t == GT - 1 else 6))
                g0 = base + DG + (GT - 1 - t) * 2 * SEL // GRP
                gathers(l, "peer_u", eix[:, t, :], g0)
                gathers(l, "peer_v", eix[:, t, :], g0 + SEL // GRP)

    @block.tensor
    def _(pe):
        na, nv, nb = [0], [0], [0]
        turns = [4, 0]

        def abank():
            g = na[0]
            na[0] += 1
            if g >= 4:
                pe.wait_ge(act_bank_free, g - 3)
            return ps[g % 4]

        def vbank():
            g = nv[0]
            nv[0] += 1
            k, since = turns
            if g - since >= k:
                pe.wait_ge(dve_bank_free, g - k + 1)
            return ps[4 + (g - since) % k]

        def take_turns(k):
            pe.wait_ge(dve_bank_free, nv[0])
            turns[:] = [k, nv[0]]

        def wblock():
            n = nb[0]
            nb[0] += 1
            pe.wait_ge(weights_landed[n % 2], 16 * (n // 2 + 1))
            return wr[:, n % 2, :, :]

        def transposes(norm):
            for t in range(TILES + 1):
                r = rows(t)
                pe.wait_ge(normed, norm * (TILES + 1) + t + 1)
                for k0 in range(0, KD, 4):
                    b = abank()
                    for k in range(4):
                        m = pe.transpose(b[:, k * P:k * P + r], hn[0:r, t, (k0 + k) * P:(k0 + k + 1) * P],
                                         ident[0:r, 0:r])
                    m.then_inc(act_bank_full, 1)

        def natural(bank_of, ready, lhs):
            w = wblock()
            for t in range(TILES + 1):
                b = bank_of()
                for k in range(KD):
                    m = pe.matmul(b[0:rows(t), :], lhs[:, k, cols(t)], w[:, k, :], start=(k == 0), stop=(k == KD - 1))
                m.then_inc(ready, 1)
            pe.wait_ge(ready, (na if bank_of is abank else nv)[0])
            pe.sem_inc(weights_used, 1)

        def tlayout(bank_of, ready, counter):
            w = wblock()
            for c in range(BLK // P):
                for half in range(2):
                    b = bank_of()
                    for k in range(KD):
                        m = pe.matmul(b[:, 0:HALF], w[:, k, c * P:(c + 1) * P], hT[:, k, half * HALF:(half + 1) * HALF],
                                      start=(k == 0), stop=(k == KD - 1))
                    m.then_inc(ready, 1)
            pe.wait_ge(ready, counter[0])
            pe.sem_inc(weights_used, 1)

        pe.wait_ge(consts, 16 * 9)
        pe.wait_ge(go, 1)
        pe.sem_inc(first_done, 4)
        pe.sem_inc(second_done, 2)
        pe.sem_inc(gates_in_psum, 2)
        transposes(0)
        pe.wait_ge(act_bank_free, na[0])
        natural(abank, act_bank_full, hT)
        pe.wait_ge(act_bank_free, na[0])
        for b_ in range(DEC):
            b = abank()
            pe.matmul(b[:, :], selb[:, b_, :], z[0:DEC, TILES, 0:AW], start=True, stop=True).then_inc(act_bank_full, 1)
        for _ in range(2):
            natural(abank, act_bank_full, hT)
        for _ in range(2):
            tlayout(abank, act_bank_full, na)
        pe.wait_ge(act_bank_free, na[0])
        for t in range(TILES):
            for part in range(2):
                b = abank()
                for h in range(HEADS):
                    m = pe.transpose(b[:, h * P:(h + 1) * P], z[:, t, part * AW + h * P:part * AW + (h + 1) * P],
                                     ident[:, :])
                m.then_inc(act_bank_full, 1)
        pe.wait_ge(scalar_dmas, 16 * 6)
        b = abank()
        for i in range(SUB + 1):
            m = pe.matmul(b[:, i * HEADS:(i + 1) * HEADS], ohd[:, i, :], rbs, start=True, stop=True)
        m.then_inc(act_bank_full, 1)
        for h in range(HEADS):
            pe.wait_ge(act_results, h + 1)
            for c0 in (0, 320):
                b = abank()
                pe.matmul(b[:, 0:min(320, SEQ + P - 1 - c0)], rbw, ohs[:, c0:min(c0 + 320, SEQ + P - 1)],
                          start=True, stop=True).then_inc(act_bank_full, 1)
        take_turns(3)
        o = ps[7]

        def maximum(b_):
            pe.wait_ge(dec_maxima, 2 * b_ + 1)
            b = vbank()
            pe.transpose(b[0:8, 0:P], kq[:, 8 * b_:8 * b_ + 8], ident[:, :]).then_inc(dve_bank_full, 1)

        def spread(b_):
            pe.wait_ge(dec_maxima, 2 * b_ + 2)
            b = vbank()
            pe.matmul(b[:, 0:8], ones[0:8, :], kq[0:8, 64 + 8 * b_:64 + 8 * b_ + 8], start=True, stop=True)\
                .then_inc(dve_bank_full, 1)

        def values(g):
            b_, j = divmod(g, NG)
            if j == 0:
                pe.wait_ge(dec_exps_ready, b_ + 1)
                if b_:
                    pe.wait_ge(dec_sums_kept, b_)
                pe.matmul(o[0:8, :], s[0:DEC, b_, PAGES, :], z[0:DEC, TILES, 2 * AW:3 * AW],
                          start=True, stop=False, skip_group_check=True)
            pe.wait_ge(values_landed[g % len(vpages)], 16 * (g // len(vpages) + 1))
            for i in range(SUB):
                m = pe.matmul(o[0:8, :], s[:, b_, j * SUB + i, :], vpages[g % len(vpages)][:, i, :],
                              start=False, stop=(j == NG - 1 and i == SUB - 1), skip_group_check=True)
            m.then_inc(value_slots_free, 1)
            if j == NG - 1:
                pe.wait_ge(value_slots_free, len(vpages) + g + 1)
                pe.sem_inc(dec_sums_done, 1)

        def logits(n):
            h, i = divmod(n, TILES)
            keys_n = (i + 1) * P
            for c in range(2):
                b = vbank()
                pe.matmul(b[:, 0:keys_n], qT[c * HD:(c + 1) * HD, h, i * P:(i + 1) * P],
                          kT[c * HD:(c + 1) * HD, h, 0:keys_n], start=True, stop=True).then_inc(dve_bank_full, 1)

        def outputs(n):
            h, i = divmod(n, TILES)
            pe.wait_ge(block_weights_ready, n + 1)
            b = abank()
            for kb in range(i + 1):
                m = pe.transpose(b[:, kb * P:(kb + 1) * P], wt[:, n % 2, kb * P:(kb + 1) * P], ident[:, :])
            m.then_inc(act_bank_full, 1)
            pe.wait_ge(act_bank_free, na[0])
            b = abank()
            for kb in range(i + 1):
                m = pe.matmul(b[:, 0:P], z[:, kb, 2 * AW + h * P:2 * AW + (h + 1) * P], pT[:, kb * P:(kb + 1) * P],
                              start=(kb == 0), stop=(kb == i))
            m.then_inc(act_bank_full, 1)

        def headnorm(h):
            pe.wait_ge(act_parts_ready, h + 1)
            b = vbank()
            pe.matmul(b[:, :], ones[:, :], sq, start=True, stop=True).then_inc(dve_bank_full, 1)

        mine = dict(maximum=maximum, spread=spread, values=values, logits=logits, outputs=outputs, headnorm=headnorm)
        for what, k in attention_order():
            if what in mine:
                mine[what](k)
        pe.wait_ge(mixer_steps, 3)
        b = vbank()
        pe.matmul(b[:, 0:64], ones[:, :], kq[:, 0:64], start=True, stop=True).then_inc(dve_bank_full, 1)
        pe.wait_ge(dec_sums_kept, DEC)
        for b_ in range(DEC):
            for h in range(HEADS):
                m = pe.matmul(o[:, b_ * 8 + 2 * h:b_ * 8 + 2 * h + 2], obs[:, b_, h * P:(h + 1) * P],
                              ident[0:8, 2 * h:2 * h + 2], start=True, stop=True, skip_group_check=True)
        m.then_inc(dec_sums_done, 1)
        take_turns(4)
        pe.wait_ge(mixer_steps, 4)
        b = vbank()
        pe.matmul(b[:, 0:32], ones[:, :], kq[:, 32:64], start=True, stop=True).then_inc(dve_bank_full, 1)
        pe.wait_ge(scalar_dmas, 16 * 8)
        for c in range(RB):
            pe.wait_ge(conved, c + 1)
            for m_ in range(2):
                for half in range(2):
                    b = abank()
                    pe.matmul(b[:, 0:HALF], wab[:, m_, c, :], xc[:, c, half * HALF:(half + 1) * HALF],
                              start=True, stop=True).then_inc(act_bank_full, 1)
        pe.wait_ge(mixer_steps, 5)
        for _ in range(2):
            natural(vbank, dve_bank_full, cat)

        def peer(l, norm):
            transposes(norm)
            pe.wait_ge(act_bank_free, na[0])
            pe.wait_ge(wq_landed, 64 * (l + 1))
            pe.wait_ge(peer_keys_landed, 16 * (l + 1))

            def queries(t):
                for g in range(HC // 4):
                    b = abank()
                    for c in range(4):
                        for k in range(KD):
                            m = pe.matmul(b[:, c * P:c * P + P], wqs[g][:, k, c * P:(c + 1) * P], hT[:, k, cols(t)],
                                          start=(k == 0), stop=(k == KD - 1))
                    m.then_inc(act_bank_full, 1)
                return na[0]

            def last_queries():
                for h in range(PH):
                    b = abank()
                    for c in range(2):
                        hc, n = 2 * h + c, P + DEC
                        for k in range(KD):
                            m = pe.matmul(b[:, c * n:(c + 1) * n], wqs[hc // 4][:, k, hc % 4 * P:(hc % 4 + 1) * P],
                                          hT[:, k, SEQ - P:TOK], start=(k == 0), stop=(k == KD - 1))
                    m.then_inc(act_bank_full, 1)

            def scores(slot, got):
                pe.wait_ge(act_bank_free, got)
                for g in range(HC // 4):
                    b = abank()
                    for c in range(4):
                        m = pe.matmul(b[:, c * P:(c + 1) * P], pq[:, slot, 4 * g + c, :],
                                      keys[:, 4 * g + c, :], start=True, stop=True)
                    m.then_inc(act_bank_full, 1)

            def turn(t):
                pe.wait_ge(chosen, l * (TILES + 2) + 4 + t)
                b = abank()
                for i, v in enumerate((e1f, e2s, coef)):
                    m = pe.transpose(b[:, i * P:(i + 1) * P], v, ident[:, :])
                m.then_inc(act_bank_full, 1)

            def gates(n, c, e2, e1):
                wait_apart(pe, go, onehots_ready, n + 1)
                wait_apart(pe, go, gates_in_sbuf, n + 1)
                for i in range(OT):
                    m = pe.matmul(ps[6 + c % 2][:, i * CH:(i + 1) * CH], e2[c % 2][:, i, :], e1[c % 2][:, i, :],
                                  start=True, stop=True)
                m.then_inc(gates_in_psum, 1)

            last_queries()
            got = na[0]
            pe.wait_ge(act_bank_free, got)
            b = abank()
            for c in range(2):
                for h in range(PH):
                    m = pe.matmul(b[0:DP, c * P:(c + 1) * P], pqd[:, c, h, :], keys[:, 2 * h + c, :],
                                  start=(h == 0), stop=(h == PH - 1))
            m.then_inc(act_bank_full, 1)
            scores(0, got)
            pe.wait_ge(chosen, l * (TILES + 2) + 1)
            b = vbank()
            for i, shift in enumerate((ident[0:DP, :], kq[0:DP, 0:P])):
                m = pe.matmul(b[:, 0:2 * DK].rearrange("p (a k) -> p a k", a=2), shift,
                              e2f[0:DP, :, i * DK:(i + 1) * DK], start=(i == 0), stop=(i == 1))
            m.then_inc(dve_bank_full, 1)
            q0 = queries(0)
            for c in range(2):
                b = abank()
                pe.matmul(b[:, :], rep[:, :], hn[0:DEC, TILES, c * 512:(c + 1) * 512], start=True, stop=True)\
                    .then_inc(act_bank_full, 1)
            q1 = queries(1)
            scores(1, q0)
            q2 = queries(2)
            pe.wait_ge(act_bank_full, na[0])
            pe.sem_inc(queried, 1)
            pe.wait_ge(dec_coefs_ready, l + 1)
            b0, b1 = vbank(), vbank()
            for k in range(DK):
                if k % GRP == 0:
                    pe.wait_ge(rows_landed[k // GRP], 64 * (l * (GROUPS // 2) + 2))
                for c, b in enumerate((b0, b1)):
                    m = pe.matmul(b[0:DEC, :], dw[:, k, :], ring[k][:, c * 512:(c + 1) * 512],
                                  start=(k == 0), stop=(k == DK - 1))
                if k % GRP == GRP - 1:
                    m.then_inc(row_groups_free, 1)
            pe.wait_ge(row_groups_free, l * GROUPS + DG + 2)
            pe.sem_inc(dve_bank_full, 2)
            scores(0, q1)
            turn(0)
            pe.wait_ge(dve_bank_free, nv[0])
            for n in range(CH // 2):
                gates(l * NCH + n, n, e2o0, e1o0)
            scores(1, q2)
            turn(1)
            for n in range(CH // 2, CH):
                gates(l * NCH + n, n, e2o0, e1o0)
            def first(n, c):
                wait_apart(pe, go, gelu_done, n + 1)
                wait_apart(pe, go, u_landed[c], (n - c) * 4 + 16)
                for k in range(KD):
                    m = pe.matmul(ps[c % 2][:, 0:DT * P], us[c][:, k, :], hT[:, k, 0:DT * P],
                                  start=(k == 0), stop=(k == KD - 1))
                m.then_inc(first_done, 1)

            def second(n, c):
                wait_apart(pe, go, coefs_ready, n + 3)
                wait_apart(pe, go, v_landed[c % 2], (n - c) * 8 + 16 * (c // 2 + 1))
                for t in range(DT):
                    for h in range(2):
                        m = pe.matmul(ps[2 + 2 * t + h][:, :], cT[:, c % 2, t * P:(t + 1) * P],
                                      vs[c % 2][:, h * 512:(h + 1) * 512], start=False, stop=False, skip_group_check=True)
                m.then_inc(second_done, 1)

            pe.wait_ge(act_bank_free, na[0])
            pe.wait_ge(chosen, (l + 1) * (TILES + 2))
            for i in range(4):
                pe.matmul(ps[2 + i][:, :], ones[:, :], cT[:, :, :], start=True, stop=False, skip_group_check=True)
            first(l * NCH, 0)

            def chunks(j, r, more=True):
                for c in range(CB):
                    n = j * CB + (l * NCH + r * CH + c)
                    if more or c < CB - 1:
                        first(n + 1, (c + 1) % CB)
                    if r < RANGES - 1:
                        gates(n + CH, c, e2oh, e1oh)
                    second(n, c)

            for r in range(RANGES):
                with pe.Fori(0, CH // CB - (r == RANGES - 1)) as j:
                    chunks(j, r)
            chunks(CH // CB - 1, RANGES - 1, more=False)
            pe.wait_ge(second_done, (l + 1) * NCH + 2)
            pe.sem_inc(dense_sums_done, 1)
            pe.wait_ge(dense_sums_taken, l + 1)
        peer(0, 1)
        transposes(2)
        pe.wait_ge(act_bank_free, na[0])
        for _ in range(2):
            tlayout(abank, act_bank_full, na)
        for _ in range(2):
            tlayout(vbank, dve_bank_full, nv)
        for _ in range(2):
            tlayout(abank, act_bank_full, na)
        pe.wait_ge(mixer_steps, 6)
        for _ in range(2):
            natural(vbank, dve_bank_full, cat)
        peer(1, 3)

    @block.scalar
    def _(act):
        na = [0]
        step = Chain(act, act_steps)

        def take():
            g = na[0]
            na[0] += 1
            act.wait_ge(act_bank_full, g + 1)
            return ps[g % 4]

        def roots(n):
            act.wait_ge(mean_squares_ready, n + 1)
            v = st[:, 40:40 + TILES + 1]
            act.activation(v, v, ACT.Sqrt).then_inc(roots_ready, 1)

        def t_out(norm):
            roots(norm)
            for t in range(TILES + 1):
                r = rows(t)
                for k0 in range(0, KD, 4):
                    b = take()
                    act.copy(hT[:, k0:k0 + 4, cols(t)],
                             b[:, :].rearrange("p (k c) -> p k c", k=4)[:, :, 0:r]).then_inc(act_bank_free, 1)

        act.dma_start(gain[:, :], ins["gain0"].broadcast_to([P, D])).then_inc(gain_landed, 16)
        act.sem_inc(gelu_done, 2)
        act.sem_inc(gates_in_sbuf, 2)
        act.wait_ge(lambda_ready, 1)
        step(act.activation(st[:, 8:10], st[:, 8:10], ACT.Exp))
        act.activation(st[:, 24:28], st[:, 24:28], ACT.Exp).then_inc(lambda_exps_ready, 1)
        t_out(0)
        act.wait_ge(normed, TILES + 1)
        act.wait_ge(act_bank_full, na[0])
        for j in range(3):
            for t in range(TILES + 1):
                b = take()
                act.copy(z[0:rows(t), t, j * AW:(j + 1) * AW], b[0:rows(t), :]).then_inc(act_bank_free, 1)
            if j == 0:
                for b_ in range(DEC):
                    b = take()
                    act.mul(qb[:, b_, :], b[:, :], HD ** -0.5).then_inc(act_bank_free, 1)
        for j in range(2):
            for c in range(RB):
                b = take()
                if j == 0:
                    act.copy(xp[:, c, RGC - 1:RGC - 1 + HALF], b[:, 0:HALF]).then_inc(act_bank_free, 1)
                else:
                    act.copy(grT[:, c, 0:HALF], b[:, 0:HALF]).then_inc(act_bank_free, 1)
                b = take()
                if j == 0:
                    step(act.copy(xp[:, c, RGC - 1 + HALF:RGC - 1 + SEQ], b[:, 0:SEQ - HALF]))
                    act.copy(xd[:, c, :, RGC - 1], b[:, SEQ - HALF:HALF]).then_inc(act_bank_free, 1)
                else:
                    act.copy(grT[:, c, HALF:TOK], b[:, 0:HALF]).then_inc(act_bank_free, 1)
        act.wait_ge(act_bank_free, na[0])
        act.dma_start(ohd, ins["c_ohd"]).then_inc(scalar_dmas, 16)
        act.dma_start(rbs, ins["rel_bias"]).then_inc(scalar_dmas, 16)
        act.dma_start(rb0, ins["rel_bias"][0:1, :].broadcast_to([DEC, HEADS])).then_inc(scalar_dmas, 16)
        act.dma_start(ohs, ins["c_oh"]).then_inc(scalar_dmas, 16)
        act.dma_start(rbx[0:BUCKETS, :], ins["rel_bias"]).then_inc(scalar_dmas, 16)
        act.dma_start(rbx[BUCKETS:BUCKETS + 1, :], ins["c_mask"]).then_inc(scalar_dmas, 16)
        k3 = outs["k_prompt"].rearrange("(t p) d -> p t d", p=P)
        v3 = outs["v_prompt"].rearrange("(t p) d -> p t d", p=P)
        act.dma_start(k3, z[:, 0:TILES, AW:2 * AW]).then_inc(outputs_stored, 16)
        act.dma_start(v3, z[:, 0:TILES, 2 * AW:3 * AW]).then_inc(outputs_stored, 16)
        act.dma_start(outs["k_sample"], z[0:DEC, TILES, AW:2 * AW]).then_inc(outputs_stored, 16)
        act.dma_start(outs["v_sample"], z[0:DEC, TILES, 2 * AW:3 * AW]).then_inc(outputs_stored, 16)
        for t in range(TILES):
            for part in range(2):
                b = take()
                dst = (qT if part == 0 else kT)[:, :, cols(t)]
                src = b[:, :].rearrange("p (h c) -> p h c", h=HEADS)
                act.mul(dst, src, HD ** -0.5 if part == 0 else 1.0).then_inc(act_bank_free, 1)
        b = take()
        for c in range(2):
            m = act.copy(bd[:, :, :].rearrange("p a (h c) -> p a h c", c=2)[:, :, :, c],
                         b[:, 0:(SUB + 1) * HEADS].rearrange("p (a h) -> p a h", a=SUB + 1))
            if c == 0:
                step(m)
            else:
                m.then_inc(act_bank_free, 1)
        act.wait_ge(act_bank_free, na[0])
        act.wait_ge(scalar_dmas, 16 * 6)
        for h in range(HEADS):
            if h:
                act.wait_ge(act_bank_full, na[0])
            act.copy(rbw, rbx[:, h:h + 1].broadcast_to([BUCKETS + 1, P])).then_inc(act_results, 1)
            if h:
                act.wait_ge(bias_landed, 16 * h)
            b = take()
            step(act.copy(wide[:, 0:320], b[:, 0:320]))
            act.sem_inc(act_bank_free, 1)
            b = take()
            act.copy(wide[:, 320:SEQ + P - 1], b[:, 0:SEQ + P - 1 - 320]).then_inc(act_bank_free, 1)
            act.wait_ge(act_bank_free, na[0])
            act.sem_inc(wide_ready, 1)
        def subtract(b_):
            act.wait_ge(dec_logits_ready, b_ + 1)
            act.activation(s[:, b_, :, :], s[:, b_, :, :], ACT.Exp).then_inc(dec_exps_ready, 1)

        def keep(b_):
            act.wait_ge(dec_sums_done, b_ + 1)
            act.copy(obs[:, b_, :], ps[7][0:8, :]).then_inc(dec_sums_kept, 1)

        def logits(n):
            w, m = (n % TILES + 1) * P, BLOCK_STATS[n % 2]
            for c in range(2):
                act.wait_ge(block_logits_ready, 2 * n + c + 1)
                act.activation(lg[:, n % 2, c, 0:w], lg[:, n % 2, c, 0:w], ACT.Exp,
                               bias=st[:, m + c:m + c + 1], accum_out=st[:, m + 2 + c:m + 3 + c]).then_inc(block_exps_ready, 1)

        def outputs(n):
            h, i = divmod(n, TILES)
            b = take()
            act.copy(pT[:, 0:(i + 1) * P], b[:, 0:(i + 1) * P]).then_inc(act_bank_free, 1)
            b = take()
            step(act.copy(cat[:, h, i * P:(i + 1) * P], b[:, 0:P]))
            act.sem_inc(act_bank_free, 1)
            if i == TILES - 1:
                act.activation(sq, cat[:, h, 0:SEQ], ACT.Square).then_inc(act_parts_ready, 1)

        def headnorm(h):
            act.wait_ge(head_squares_ready, h + 1)
            act.activation(rs, rs, ACT.Sqrt).then_inc(head_roots_ready, 1)

        mine = dict(subtract=subtract, keep=keep, logits=logits, outputs=outputs, headnorm=headnorm)
        for what, k in attention_order():
            if what in mine:
                mine[what](k)
        act.dma_start(wab[:, 0, :, :], ins["wa_bd"]).then_inc(scalar_dmas, 16)
        act.dma_start(wab[:, 1, :, :], ins["wi_bd"]).then_inc(scalar_dmas, 16)
        act.wait_ge(dec_norm_steps, 1)
        act.activation(kq[:, 64:96], kq[:, 64:96], ACT.Sqrt).then_inc(dec_norm_steps, 1)
        for c in range(RB):
            for m_, dst in enumerate((gr_, gi_)):
                for half in range(2):
                    b = take()
                    o = PRM["ba" if m_ == 0 else "bi"] + c
                    act.activation(dst[:, c, half * HALF:(half + 1) * HALF], b[:, 0:HALF], ACT.Sigmoid,
                                   bias=prm[:, o:o + 1]).then_inc(act_bank_free, 1)
        act.wait_ge(act_bank_free, na[0])
        act.wait_ge(conv_steps, 2)
        for c in range(RB):
            step(act.activation(gr_[:, c, :], gr_[:, c, :], ACT.Tanh, scale=st[:, 4 + c:5 + c]))
        act.sem_inc(head_squares_ready, 1)
        act.activation(root4u[:, :, :], gr_[:, :, :], ACT.Sqrt, scale=4.0).then_inc(head_roots_ready, 1)
        act.activation(gg[:, :, :], grT[:, :, :], ACT.Gelu_apprx_tanh).then_inc(act_parts_ready, 1)
        act.wait_ge(conv_steps, 3)
        act.dma_start(outs["hs"], hs[:, :, SEQ - 1:TOK]).then_inc(outputs_stored, 16)
        act.dma_start(outs["rgp"], xp[:, :, SEQ:SEQ + RGC - 1]).then_inc(outputs_stored, 16)
        act.dma_start(outs["rgs"], xd[:, :, :, 1:RGC]).then_inc(outputs_stored, 16)
        act.wait_ge(outputs_stored, 16 * 7)

        def peer(l, norm):
            act.wait_ge(mixer_steps, 5 + l)
            act.dma_start(keys[:, :, :], ins[f"keys{l}"]).then_inc(peer_keys_landed, 16)
            t_out(norm)

            def queries(slot):
                for g in range(HC // 4):
                    b = take()
                    act.copy(pq[:, slot, 4 * g:4 * g + 4, :], b[:, :].rearrange("p (a c) -> p a c", a=4)).then_inc(act_bank_free, 1)

            def last_queries():
                act.wait_ge(zeros_ready, l + 1)
                for h in range(PH):
                    b = take()[:, 0:2 * (P + DEC)].rearrange("p (a c) -> p a c", a=2)
                    step(act.copy(pq[:, 0, 2 * h:2 * h + 2, :], b[:, :, 0:P]))
                    act.copy(pqd[:, :, h, h * DEC:(h + 1) * DEC], b[:, :, P:P + DEC]).then_inc(act_bank_free, 1)

            def scores(turns):
                if turns:
                    act.wait_ge(scores_used, l * TILES + turns)
                for g in range(HC // 4):
                    b = take()
                    act.copy(sc[:, 4 * g:4 * g + 4, :], b[:, :].rearrange("p (a c) -> p a c", a=4)).then_inc(act_bank_free, 1)
                act.wait_ge(act_bank_free, na[0])
                act.sem_inc(scores_ready, 1)

            def exps(turns, r, nh):
                act.wait_ge(top_scores_ready, l * (TILES + 1) + turns + 1)
                act.activation(s16[0:r, 0:nh, :], s16[0:r, 0:nh, :], ACT.Exp).then_inc(top_exps_ready, 1)

            def turn(t):
                b = take()
                step(act.copy(eT[:, :, t * P:(t + 1) * P], b[:, 0:3 * P].rearrange("p (a c) -> p a c", a=3)))
                act.sem_inc(act_bank_free, 1)
                act.sem_inc(indices_turned, 1)

            def gates(n, c, G, tok):
                wait_apart(act, go, gates_in_psum, n + 3)
                act.copy(G[:, :, bass.ds(tok, OT)],
                         ps[6 + c % 2][:, 0:OT * CH].rearrange("p (t e) -> p e t", t=OT)).then_inc(gates_in_sbuf, 1)

            last_queries()
            b = take()
            step(act.copy(scd, b[0:DP, 0:2 * P].rearrange("p (c n) -> p c n", c=2)))
            act.sem_inc(act_bank_free, 1)
            act.sem_inc(scores_ready, 1)
            scores(0)
            exps(0, DP, 1)
            queries(1)
            for c in range(2):
                b = take()
                act.copy(xrep[:, c * 512:(c + 1) * 512], b[:, :]).then_inc(act_bank_free, 1)
            act.wait_ge(act_bank_free, na[0])
            act.sem_inc(dec_rows_spread, 1)
            exps(1, P, PH)
            queries(0)
            scores(1)
            act.wait_ge(dots_ready, l * (GT + 1) + 1)
            act.activation(ddot[:, :], ddot[:, :], ACT.Gelu_apprx_tanh).then_inc(act_results, 1)
            queries(1)
            scores(2)
            exps(2, P, PH)
            turn(0)
            for n in range(CH // 2):
                gates(l * NCH + n, n, G[0], n * OT)
            scores(3)
            exps(3, P, PH)
            turn(1)
            for n in range(CH // 2, CH):
                gates(l * NCH + n, n, G[0], n * OT)
            exps(4, P, PH)

            def gelu(n, c):
                wait_apart(act, go, first_done, n + 5)
                wait_apart(act, go, coefs_ready, n + 1)
                act.activation(ga[:, c % 2, :], ps[c % 2][:, 0:DT * P], ACT.Gelu_apprx_tanh).then_inc(gelu_done, 1)

            for r in range(RANGES):
                with act.Fori(0, CH // CB) as j:
                    for c in range(CB):
                        n = j * CB + (l * NCH + r * CH + c)
                        gelu(n, c)
                        if r < RANGES - 1:
                            gates(n + CH, c, G[(r + 1) % 2], j * (CB * OT) + c * OT)
                if r % 2 == 0:
                    act.wait_ge(dots_ready, l * (GT + 1) + r // 2 + 2)
                    act.activation(dots[:, :], dots[:, :], ACT.Gelu_apprx_tanh).then_inc(act_results, 1)

        def next_gain(n):
            act.wait_ge(gain_used, n)
            act.dma_start(gain[:, :], ins[f"gain{n}"].broadcast_to([P, D])).then_inc(gain_landed, 16)

        next_gain(1)
        peer(0, 1)
        next_gain(2)
        t_out(2)
        act.wait_ge(act_bank_free, na[0])
        act.dma_start(cxd[:, :, :, 0:SCC - 1], ins["sbuf0"]).then_inc(scalar_dmas, 16)
        for dst in (cgT, bgT):
            for j in range(2):
                for c in range(BLK // P):
                    for half in range(2):
                        b = take()
                        act.copy(dst[:, j * 4 + c, half * HALF:(half + 1) * HALF], b[:, 0:HALF]).then_inc(act_bank_free, 1)
        act.wait_ge(conv_steps, 4)
        act.dma_start(outs["scp"], cxp[:, :, SEQ:SEQ + SCC - 1]).then_inc(scalar_dmas, 16)
        act.wait_ge(scalar_dmas, 160)
        act.dma_start(outs["scs"], cxd[:, :, :, 1:SCC]).then_inc(outputs_stored, 16)
        act.wait_ge(outputs_stored, 16 * 8)
        next_gain(3)
        peer(1, 3)
        next_gain(4)
        roots(4)

    @block.vector
    def _(dve):
        step = Chain(dve, dve_steps)
        nv, nn = [0], [0]
        turns = [4, 0]

        def take():
            g = nv[0]
            nv[0] += 1
            dve.wait_ge(dve_bank_full, g + 1)
            k, since = turns
            return ps[4 + (g - since) % k]

        def squares(t):
            r = rows(t)
            step(dve.tensor_tensor_reduce(hn[0:r, t, :], xs[0:r, t, :], xs[0:r, t, :], 1.0 / D, EPS,
                                          ALU.mult, ALU.add, st[0:r, 40 + t:41 + t]))

        def norm(left):
            n = nn[0]
            nn[0] += 1
            for t in left:
                squares(t)
            dve.sem_inc(mean_squares_ready, 1)
            dve.wait_ge(gain_landed, 16 * (n + 1))
            dve.wait_ge(roots_ready, n + 1)
            step(dve.reciprocal(st[:, 40:40 + TILES + 1], st[:, 40:40 + TILES + 1]))
            for t in range(TILES + 1):
                r = rows(t)
                dve.scalar_tensor_tensor(hn[0:r, t, :], xs[0:r, t, :], st[0:r, 40 + t:41 + t], gain[0:r, :], ALU.mult, ALU.mult)\
                    .then_inc(normed, 1)
                dve.wait_ge(normed, n * (TILES + 1) + t + 1)
            dve.sem_inc(gain_used, 1)

        def add_out():
            for j in range(2):
                for t in range(TILES + 1):
                    r = rows(t)
                    b = take()
                    x = xs[0:r, t, j * BLK:(j + 1) * BLK]
                    dve.tensor_tensor(x, x, b[0:r, :], ALU.add).then_inc(dve_bank_free, 1)
                    if j == 1:
                        dve.wait_ge(dve_bank_free, nv[0])
                        squares(t)

        step(dve.memset(st[:, :], 1.0))
        dve.wait_ge(consts, 16 * 9)
        for i in range(2):
            step(dve.tensor_tensor_reduce(lamv[:, 2 * i, :], lamv[:, 2 * i, :], lamv[:, 2 * i + 1, :], 1.0, 0.0,
                                          ALU.mult, ALU.add, st[:, 8 + i:9 + i]))
        lam_ = prm[:, PRM["lam"]:PRM["lam"] + RB]
        step(dve.scalar_tensor_tensor(st[:, 24:28], lam_, -1.0, lam_, ALU.mult, ALU.min))
        dve.sem_inc(lambda_ready, 1)
        dve.sem_inc(key_slots_free, PSLOTS)
        dve.sem_inc(value_slots_free, len(vpages) - 1)
        dve.sem_inc(row_groups_free, 2)
        dve.sem_inc(coefs_ready, 2)
        dve.sem_inc(indices_turned, 1)
        dve.wait_ge(page_table_landed, 16 * PG)
        step(dve.tensor_copy(pgf, pgi))
        step(dve.tensor_scalar(pgf, pgf, float(P // SUB), small[:, 40 + P:41 + P], ALU.mult, ALU.add))
        step(dve.tensor_copy(pgi, pgf))
        dve.sem_inc(page_rows_ready, 1)
        dve.wait_ge(x_landed, 32)
        norm(range(TILES + 1))
        step(dve.memset(xp[:, :, 0:RGC - 1], 0.0))
        sp_ = st[:, 4:8]
        y_, t_, q2 = st[:, 24:28], st[:, 28:32], st[:, 32:36]
        dve.wait_ge(lambda_exps_ready, 1)
        step(dve.tensor_scalar(t_, y_, 2.0, None, ALU.add))
        step(dve.reciprocal(t_, t_))
        step(dve.tensor_tensor(y_, y_, t_, ALU.mult))
        step(dve.tensor_tensor(q2, y_, y_, ALU.mult))
        step(dve.memset(t_, 1.0 / 19))
        for k in range(17, 0, -2):
            step(dve.tensor_tensor(t_, t_, q2, ALU.mult))
            step(dve.tensor_scalar(t_, t_, 1.0 / k, None, ALU.add))
        step(dve.tensor_tensor(t_, t_, y_, ALU.mult))
        step(dve.tensor_scalar(y_, prm[:, PRM["lam"]:PRM["lam"] + 4], -1.0, 0.0, ALU.mult, ALU.max))
        step(dve.scalar_tensor_tensor(sp_, t_, 2.0, y_, ALU.mult, ALU.add))
        step(dve.tensor_scalar(sp_, sp_, 4.0, None, ALU.mult))
        dve.wait_ge(act_bank_free, A_Q)
        product = {}

        def key_sums(n):
            b_, g = divmod(n, NG)
            dve.wait_ge(dve_steps, product[n])
            dve.tensor_reduce(s[:, b_, g * SUB:(g + 1) * SUB, :].rearrange("p j c -> p (j c)"),
                              pages[n % PSLOTS].rearrange("p g c -> p (g c)").rearrange("p (a d) -> p a d", d=HD),
                              AX.X, ALU.add).then_inc(key_slots_free, 1)

        def keys_(n):
            kp = pages[n % PSLOTS]
            dve.wait_ge(keys_landed[n % PSLOTS], 16 * (n // PSLOTS + 1))
            dve.tensor_tensor(kp, kp, qb[:, n // NG:n // NG + 1, :].broadcast_to([P, SUB, AW]), ALU.mult)\
                .then_inc(dve_steps, 1)
            step.n += 1
            product[n] = step.n
            if n:
                key_sums(n - 1)

        for n in range(EARLY):
            keys_(n)
        dve.wait_ge(scalar_dmas, 16 * 6)
        q_, k_ = z[0:DEC, TILES, 0:AW], z[0:DEC, TILES, AW:2 * AW]
        step(dve.tensor_tensor(snew, q_, k_, ALU.mult))
        step(dve.tensor_reduce(sn8, snew.rearrange("p (a d) -> p a d", d=HD), AX.X, ALU.add))
        step(dve.scalar_tensor_tensor(sn8.rearrange("p (h c) -> p h c", c=2), sn8.rearrange("p (h c) -> p h c", c=2),
                                      HD ** -0.5, rb0.unsqueeze(2).broadcast_to([DEC, HEADS, 2]), ALU.mult, ALU.add))
        step(dve.memset(s[:, :, PAGES, :], MASK))
        eye = ident[0:DEC, 0:DEC].unsqueeze(2).broadcast_to([DEC, DEC, 8])
        sd = sdg.rearrange("p (b c) -> p b c", b=DEC)
        step(dve.tensor_scalar(sd, eye, -MASK, MASK, ALU.mult, ALU.add))
        step(dve.tensor_tensor(s[0:DEC, :, PAGES, :], sn8.unsqueeze(1).broadcast_to([DEC, DEC, 8]), eye, ALU.mult))
        step(dve.tensor_tensor(s[0:DEC, :, PAGES, :], s[0:DEC, :, PAGES, :], sd, ALU.add))
        dve.wait_ge(act_bank_free, A_QB)
        dve.wait_ge(lambda_exps_ready, 1)
        step(dve.tensor_tensor(st[:, 10:11], st[:, 8:9], st[:, 9:10], ALU.subtract))
        step(dve.tensor_scalar(st[:, 11:12], st[:, 10:11], LAM0, -1.0, ALU.add, ALU.mult))
        step(dve.tensor_scalar(st[:, 12:13], prm[:, PRM["subln"]:PRM["subln"] + 1], 1.0 - LAM0, None, ALU.mult))
        turns[:] = [3, nv[0]]
        dve.sem_inc(value_slots_free, 1)
        def maximum(b_):
            if b_ == DEC - 1:
                key_sums(DEC * NG - 1)
            dve.wait_ge(key_slots_free, PSLOTS + NG * (b_ + 1))
            last, far = s[:, b_, PAGES - SUB:PAGES, :], s[:, b_, 0:PAGES - SUB, :]
            dve.tensor_tensor(last, last, bd[:, 0:SUB, :], ALU.add).then_inc(dve_steps, 1)
            dve.tensor_tensor(far, far, bd[:, SUB, :].unsqueeze(1).broadcast_to([P, PAGES - SUB, 8]), ALU.add)\
                .then_inc(dve_steps, 1)
            step.n += 2
            dve.wait_ge(dve_steps, step.n)
            dve.tensor_reduce(kq[:, 8 * b_:8 * b_ + 8], s[:, b_, :, :].rearrange("p j c -> p c j"), AX.X, ALU.max)\
                .then_inc(dec_maxima, 1)

        def spread(b_):
            b = take()
            step(dve.tensor_reduce(st[0:8, 2:3], b[0:8, 0:P], AX.X, ALU.max))
            dve.sem_inc(dve_bank_free, 1)
            dve.tensor_scalar(kq[0:8, 64 + 8 * b_:64 + 8 * b_ + 8], ident[0:8, 0:8], st[0:8, 2:3], None, ALU.mult)\
                .then_inc(dec_maxima, 1)

        def subtract(b_):
            b = take()
            v = s[:, b_, :, :]
            step(dve.tensor_tensor(v, v, b[:, 0:8].unsqueeze(1).broadcast_to([P, PAGES + 1, 8]), ALU.subtract))
            dve.sem_inc(dve_bank_free, 1)
            dve.sem_inc(dec_logits_ready, 1)

        def sum_(b_):
            dve.wait_ge(dec_exps_ready, b_ + 1)
            step(dve.tensor_reduce(kq[:, 8 * b_:8 * b_ + 8], s[:, b_, :, :].rearrange("p j c -> p c j"), AX.X, ALU.add))

        def logits(n):
            h, i = divmod(n, TILES)
            w, m = (i + 1) * P, BLOCK_STATS[n % 2]
            if n == 0:
                dve.wait_ge(bias_landed, 16 * HEADS)
            for c in range(2):
                b = take()
                dve.tensor_tensor(lg[:, n % 2, c, 0:w], b[:, 0:w], bias[:, h, (TILES - 1 - i) * P:SEQ], ALU.add)\
                    .then_inc(dve_bank_free, 1)
            for c in range(2):
                dve.wait_ge(dve_bank_free, nv[0] - 1 + c)
                dve.tensor_reduce(st[:, m + c:m + c + 1], lg[:, n % 2, c, 0:w], AX.X, ALU.max, negate=True)\
                    .then_inc(block_logits_ready, 1)

        def weights(n):
            w, m = (n % TILES + 1) * P, BLOCK_STATS[n % 2]
            l0 = lg[:, n % 2, 0, 0:w]
            dve.wait_ge(block_exps_ready, 2 * n + 2)
            step(dve.reciprocal(st[:, m + 4:m + 6], st[:, m + 2:m + 4]))
            step(dve.tensor_scalar(l0, l0, st[:, m + 4:m + 5], None, ALU.mult))
            step(dve.tensor_tensor(st[:, m + 5:m + 6], st[:, m + 5:m + 6], st[:, 11:12], ALU.mult))
            dve.scalar_tensor_tensor(wt[:, n % 2, 0:w], lg[:, n % 2, 1, 0:w], st[:, m + 5:m + 6], l0, ALU.mult, ALU.add)\
                .then_inc(block_weights_ready, 1)
            dve.wait_ge(block_weights_ready, n + 1)

        def headnorm(h):
            b = take()
            step(dve.tensor_scalar(rs, b[:, :], 1.0 / P, EPS, ALU.mult, ALU.add))
            dve.sem_inc(dve_bank_free, 1)
            dve.sem_inc(head_squares_ready, 1)
            dve.wait_ge(head_roots_ready, h + 1)
            step(dve.reciprocal(rs, rs))
            step(dve.scalar_tensor_tensor(cat[:, h, 0:SEQ], cat[:, h, 0:SEQ], st[:, 12:13], rs, ALU.mult, ALU.mult))

        mine = dict(keys=keys_, maximum=maximum, spread=spread, subtract=subtract, sum=sum_, logits=logits,
                    weights=weights, headnorm=headnorm)
        for what, k in attention_order():
            if what in mine:
                mine[what](k)
        dve.sem_inc(mixer_steps, 3)
        b = take()
        step(dve.reciprocal(kq[:, 128:160], b[:, 0:64].rearrange("p (a c) -> p a c", c=2)[:, :, 0]))
        step(dve.reciprocal(kq[:, 0:32], b[:, 0:64].rearrange("p (a c) -> p a c", c=2)[:, :, 1]))
        dve.sem_inc(dve_bank_free, 1)
        dve.wait_ge(dec_sums_done, DEC + 1)
        o2 = ps[7][:, 0:64].rearrange("p (a c) -> p a c", c=2)
        step(dve.scalar_tensor_tensor(kq[:, 0:32], o2[:, :, 1], st[:, 11:12], kq[:, 0:32], ALU.mult, ALU.mult))
        step(dve.tensor_tensor(kq[:, 128:160], o2[:, :, 0], kq[:, 128:160], ALU.mult))
        turns[:] = [4, nv[0]]
        step(dve.tensor_tensor(kq[:, 0:32], kq[:, 0:32], kq[:, 128:160], ALU.add))
        dve.tensor_tensor(kq[:, 32:64], kq[:, 0:32], kq[:, 0:32], ALU.mult).then_inc(mixer_steps, 1)
        b = take()
        step(dve.tensor_scalar(kq[:, 64:96], b[:, 0:32], 1.0 / P, EPS, ALU.mult, ALU.add))
        dve.sem_inc(dve_bank_free, 1)
        dve.sem_inc(dec_norm_steps, 1)
        dve.wait_ge(dec_norm_steps, 2)
        step(dve.reciprocal(kq[:, 64:96], kq[:, 64:96]))
        step(dve.scalar_tensor_tensor(cat[:, 0:HEADS, SEQ:TOK], kq[:, 0:32].rearrange("p (b h) -> p h b", h=HEADS),
                                      st[:, 12:13], kq[:, 64:96].rearrange("p (b h) -> p h b", h=HEADS),
                                      ALU.mult, ALU.mult))
        step(dve.memset(kq[0:DP, 0:DP], 0.0))
        step(dve.tensor_copy(kq[0:DP, DP:P], ident[0:DP, 0:DP]))
        dve.wait_ge(outputs_stored, 16 * 4)
        dve.wait_ge(state_landed, 32)
        for c in range(RB):
            for dst, src in ((xc[:, c, 0:SEQ], lambda i: xp[:, c, i:i + SEQ]), (xc[:, c, SEQ:TOK], lambda i: xd[:, c, :, i])):
                o = PRM["conv_w"] + c * RGC
                bb = PRM["conv_b"] + c
                step(dve.tensor_scalar(dst, src(0), prm[:, o:o + 1], prm[:, bb:bb + 1], ALU.mult, ALU.add))
                for i in range(1, RGC):
                    step(dve.scalar_tensor_tensor(dst, src(i), prm[:, o + i:o + i + 1], dst, ALU.mult, ALU.add))
            dve.sem_inc(conved, 1)
        dve.sem_inc(conv_steps, 2)
        dve.wait_ge(head_squares_ready, HEADS + 1)
        u = gr_[:, :, :]
        step(dve.tensor_scalar(ua, u, 1.0, None, ALU.add))
        step(dve.reciprocal(ua, ua))
        step(dve.tensor_scalar(ub, u, -1.0, 1.0, ALU.mult, ALU.add))
        step(dve.tensor_tensor(ub, ub, ua, ALU.mult))
        dve.wait_ge(head_roots_ready, HEADS + 1)
        u = root4u
        step(dve.tensor_tensor(u, u, ua, ALU.mult))
        step(dve.tensor_tensor(u, u, gi_, ALU.mult))
        step(dve.tensor_tensor(u, u, xc, ALU.mult))
        for c in range(RB):
            step(dve.tensor_tensor_scan(hs[:, c, 0:SEQ], ub[:, c, 0:SEQ], u[:, c, 0:SEQ], 0.0, ALU.mult, ALU.add))
        dve.wait_ge(state_landed, 32)
        step(dve.tensor_tensor(hs[:, :, SEQ:TOK], ub[:, :, SEQ:TOK], h0s[:, :, :], ALU.mult))
        step(dve.tensor_tensor(hs[:, :, SEQ:TOK], hs[:, :, SEQ:TOK], u[:, :, SEQ:TOK], ALU.add))
        dve.sem_inc(conv_steps, 1)
        dve.wait_ge(act_parts_ready, HEADS + 1)
        step(dve.tensor_tensor(cat[:, HEADS:HEADS + RB, :], hs, gg, ALU.mult))
        dve.sem_inc(mixer_steps, 1)
        add_out()

        def choose(r, nh, sc, wait_places, beside=()):
            beside = list(beside)
            every = (5 * 3 * nh) // (len(beside) + 1)
            count = [0]

            def top16(n, row, best, where):
                done = [0] * n
                stages = (lambda i: dve.max(best(i)[:, 0:8], row(i)),
                          lambda i: dve.max_index(where(i)[:, 0:8], best(i)[:, 0:8], row(i)),
                          lambda i: dve.match_replace(row(i), best(i)[:, 0:8], row(i), LOW),
                          lambda i: dve.max(best(i)[:, 8:16], row(i)),
                          lambda i: dve.max_index(where(i)[:, 8:16], best(i)[:, 8:16], row(i)))
                for stage in stages:
                    for i in range(n):
                        if done[i]:
                            dve.wait_ge(dve_steps, done[i])
                        stage(i).then_inc(dve_steps, 1)
                        step.n += 1
                        done[i] = step.n
                        count[0] += 1
                        if beside and count[0] % every == 0:
                            beside.pop(0)()
                dve.wait_ge(dve_steps, step.n)

            top16(2 * nh, lambda i: sc[0:r, i, :], lambda i: v16[0:r, i, :], lambda i: i16[0:r, i, :])
            if nh == PH:
                dve.sem_inc(scores_used, 1)
            dve.tensor_copy(i16f[0:r, 0:2 * nh, :], i16[0:r, 0:2 * nh, :]).then_inc(dve_steps, 1)
            for h in range(nh):
                dve.tensor_tensor(cand[0:r, h, :].rearrange("p (a b) -> p a b", a=TOPK),
                                  v16[0:r, 2 * h, :].unsqueeze(2).broadcast_to([r, TOPK, TOPK]),
                                  v16[0:r, 2 * h + 1, :].unsqueeze(1).broadcast_to([r, TOPK, TOPK]), ALU.add)\
                    .then_inc(dve_steps, 1)
            step.n += nh + 1
            dve.wait_ge(dve_steps, step.n)
            top16(nh, lambda h: cand[0:r, h, :], lambda h: s16[0:r, h, :],
                  lambda h: c16[0:r, h * TOPK:(h + 1) * TOPK])
            for work in beside:
                work()
            n = nh * TOPK
            chosen_s = s16[0:r, 0:nh, :]
            step(dve.tensor_copy(gsum[0:r, 0:nh], s16[0:r, 0:nh, 0]))
            step(dve.tensor_tensor(chosen_s, chosen_s, gsum[0:r, 0:nh].unsqueeze(2).broadcast_to([r, nh, TOPK]),
                                   ALU.subtract))
            dve.sem_inc(top_scores_ready, 1)
            dve.tensor_scalar(chi[0:r, 0:n], c16[0:r, 0:n], 4, None, ALU.logical_shift_right).then_inc(dve_steps, 1)
            dve.tensor_scalar(clo[0:r, 0:n], c16[0:r, 0:n], 15, None, ALU.bitwise_and).then_inc(dve_steps, 1)
            step.n += 2
            dve.wait_ge(dve_steps, step.n)
            dve.tensor_copy(hif[0:r, 0:n], chi[0:r, 0:n]).then_inc(dve_steps, 1)
            dve.tensor_copy(lof[0:r, 0:n], clo[0:r, 0:n]).then_inc(dve_steps, 1)
            step.n += 2
            dve.wait_ge(dve_steps, step.n)
            wait_places()
            big = cand[0:r, 0:nh, :].rearrange("p h (k j) -> p h k j", j=TOPK)
            flat = cand[0:r, 0:nh, :].rearrange("p h (k j) -> p (h k) j", j=TOPK)
            for half, (pos, dst) in enumerate(((hif, e1f[0:r, 0:n]), (lof, e2s[0:r, 0:n]))):
                step(dve.tensor_tensor(flat, pos[0:r, 0:n].unsqueeze(2).broadcast_to([r, n, TOPK]),
                                       small[0:r, 0:16].unsqueeze(1).broadcast_to([r, n, TOPK]), ALU.is_equal))
                idx = i16f[0:r, 0:2 * nh, :].rearrange("p (h c) j -> p h c j", c=2)[:, :, half, :]
                step(dve.tensor_tensor(big, big, idx.unsqueeze(2).broadcast_to([r, nh, TOPK, TOPK]), ALU.mult))
                step(dve.tensor_reduce(dst, flat, AX.X, ALU.add))
            step(dve.scalar_tensor_tensor(e2f[0:r, 0, 0:n], e1f[0:r, 0:n], float(NKEY), e2s[0:r, 0:n], ALU.mult, ALU.add))

        def gates(r, nh, dst):
            v, g = s16[0:r, 0:nh, :], gsum[0:r, 0:nh]
            step(dve.tensor_reduce(g, v, AX.X, ALU.add))
            step(dve.reciprocal(g, g))
            step(dve.tensor_tensor(dst, v, g.unsqueeze(2).broadcast_to([r, nh, TOPK]), ALU.mult))

        def onehots(n, c, e2, e1, r, tok):
            wait_apart(dve, go, gates_in_psum, n + 1)
            iota = io128[:, r * CH:(r + 1) * CH].unsqueeze(1).broadcast_to([P, OT, CH])
            dve.tensor_tensor(e2[c % 2], io128[:, :].unsqueeze(1).broadcast_to([P, OT, P]),
                              eT[:, 1, bass.ds(tok, OT)].unsqueeze(2).broadcast_to([P, OT, P]), ALU.is_equal)\
                .then_inc(dve_steps, 1)
            dve.tensor_tensor(e1[c % 2], iota, eT[:, 0, bass.ds(tok, OT)].unsqueeze(2).broadcast_to([P, OT, CH]),
                              ALU.is_equal).then_inc(dve_steps, 1)
            step.n += 2
            dve.wait_ge(dve_steps, step.n)
            dve.tensor_tensor(e1[c % 2], e1[c % 2],
                              eT[:, 2, bass.ds(tok, OT)].unsqueeze(2).broadcast_to([P, OT, CH]), ALU.mult)\
                .then_inc(onehots_ready, 1)

        def peer(l):
            norm(())
            step.clear()
            dve.wait_ge(scores_ready, l * (TILES + 1) + 1)
            choose(DP, 1, scd, lambda: None)
            dve.wait_ge(top_exps_ready, l * (TILES + 1) + 1)
            gates(DP, 1, e2f[0:DP, 1, 0:TOPK].unsqueeze(1))
            dve.sem_inc(chosen, 1)
            b = take()
            step(dve.tensor_copy(dex[:, :], b[:, 0:2 * DK]))
            dve.sem_inc(dve_bank_free, 1)
            step(dve.tensor_copy(dix[:, :], dex[:, 0:DK]))
            dve.sem_inc(chosen, 1)

            def tile(turns, beside=()):
                step.clear()
                dve.wait_ge(scores_ready, l * (TILES + 1) + turns + 1)
                choose(P, PH, sc, lambda: dve.wait_ge(indices_turned, 1 + l * DT + (turns > 2) + (turns > 3)), beside)
                dve.wait_ge(top_exps_ready, l * (TILES + 1) + turns + 1)
                gates(P, PH, coef.rearrange("p (h k) -> p h k", h=PH))

            def keep(t):
                step(dve.tensor_copy(gt[:, t, :], coef))
                step(dve.tensor_copy(eix[:, t, :], e2f[:, 0, :]))

            tile(1)
            keep(1)
            dve.sem_inc(chosen, 1)
            dve.wait_ge(dec_rows_spread, l + 1)
            for k in range(DK):
                if k % GRP == 0:
                    dve.wait_ge(rows_landed[k // GRP], 64 * (l * (GROUPS // 2) + 1))
                step(dve.tensor_tensor_reduce(ring[k], ring[k], xrep, 1.0, 0.0, ALU.mult, ALU.add, ddot[:, k:k + 1]))
                if k % GRP == GRP - 1:
                    dve.sem_inc(row_groups_free, 1)
            dve.sem_inc(dots_ready, 1)
            dve.wait_ge(act_results, HEADS + l * (GT + 1) + 1)
            step(dve.tensor_tensor(dcf, ddot, dex[:, DK:2 * DK], ALU.mult))
            step(dve.tensor_tensor(dw, small[:, 32:32 + DEC].unsqueeze(1).broadcast_to([P, DK, DEC]),
                                   dcf.unsqueeze(2).broadcast_to([P, DK, DEC]), ALU.mult))
            dve.sem_inc(dec_coefs_ready, 1)
            tile(2)
            dve.sem_inc(chosen, 1)
            for c in range(2):
                b = take()
                x = xs[0:DEC, TILES, c * 512:(c + 1) * 512]
                dve.tensor_tensor(x, x, b[0:DEC, :], ALU.add).then_inc(dve_bank_free, 1)
            dve.wait_ge(dve_bank_free, nv[0])

            def group(n, wait):
                def work():
                    if wait:
                        dve.wait_ge(indices_turned, 1 + l * DT + n * OT // P + 1)
                        dve.wait_ge(queried, l + 1)
                    onehots(l * NCH + n, n, e2o0, e1o0, 0, n * OT)
                return work

            half = CH // 2
            tile(3, [group(n, n == 0) for n in range(half)])
            dve.sem_inc(chosen, 1)
            tile(4, [group(n, n == half) for n in range(half, CH)])
            keep(0)
            step(dve.memset(cT[:, :, :], 0.0))
            dve.sem_inc(chosen, 1)
            for r in range(RANGES):
                t, values = TILES - 1 - r // 2, r % 2 == 1
                acc = (xs[:, t, :], hn[:, t, :])
                if values:
                    dve.wait_ge(act_results, HEADS + l * (GT + 1) + r // 2 + 2)
                    step(dve.tensor_tensor(coef[:, :], dots[:, :], gt[:, t - DT, :], ALU.mult))
                    step(dve.memset(acc[1], 0.0))
                dve.wait_ge(gates_in_sbuf, l * NCH + (r + 1) * CH + 2)
                with dve.Fori(0, CH // CB) as j:
                    step.clear()
                    if values:
                        step(dve.tensor_copy(d16[:, :], coef[:, bass.ds(j * GBODY, GBODY)]))
                    for c in range(CB):
                        n = j * CB + (l * NCH + r * CH + c)
                        wait_apart(dve, go, gelu_done, n + 3)
                        wait_apart(dve, go, second_done, n + 1)
                        dve.tensor_tensor(cT[:, c % 2, :], ga[:, c % 2, :],
                                          G[r % 2][:, bass.ds(j * CB + c, 1), :].rearrange("p a t -> p (a t)"), ALU.mult)\
                            .then_inc(coefs_ready, 1)
                        if r < RANGES - 1:
                            onehots(n + CH, c, e2oh, e1oh, r + 1, j * (CB * OT) + c * OT)
                        half = c % 2
                        base = l * (GROUPS // 2) + DG // 2 + r * (SEL // GSLOTS)
                        wait_apart(dve, go, rows_landed[half], j * 128 + 64 * (base + c // 2 + 1))
                        for i in range(GRP):
                            row, q = ring[half * GRP + i], c * GRP + i
                            if not values:
                                m = dve.tensor_tensor_reduce(row, row, hn[:, t, :], 1.0, 0.0, ALU.mult, ALU.add,
                                                             d16[:, q:q + 1])
                                if i < GRP - 1:
                                    m.then_inc(dve_steps, 1)
                                    step.n += 1
                                else:
                                    step(m)
                            else:
                                step(dve.scalar_tensor_tensor(acc[i % 2], row, d16[:, q:q + 1], acc[i % 2],
                                                              ALU.mult, ALU.add))
                        dve.sem_inc(row_groups_free, 1)
                    if not values:
                        step(dve.tensor_copy(dots[:, bass.ds(j * GBODY, GBODY)], d16[:, :]))
                step.clear()
                if values:
                    step(dve.tensor_tensor(acc[0], acc[0], acc[1], ALU.add))
                    squares(t)
                    if r == 1:
                        squares(TILES)
                else:
                    dve.sem_inc(dots_ready, 1)
            dve.wait_ge(dense_sums_done, l + 1)
            for t in range(DT):
                for h in range(2):
                    x = xs[:, t, h * 512:(h + 1) * 512]
                    step(dve.tensor_tensor(x, x, ps[2 + 2 * t + h][:, :], ALU.add))
            dve.sem_inc(dense_sums_taken, 1)
            dve.sem_inc(peer_done, 1)

        peer(0)
        norm(range(DT))
        step(dve.memset(cxp[:, :, 0:SCC - 1], 0.0))
        dve.wait_ge(act_bank_free, A_CG)
        for k in range(KD):
            b = take()
            dve.tensor_tensor(cxp[:, k, SCC - 1:SCC - 1 + HALF], b[:, 0:HALF], cgT[:, k, 0:HALF], ALU.mult)\
                .then_inc(dve_bank_free, 1)
            b = take()
            step(dve.tensor_tensor(cxp[:, k, SCC - 1 + HALF:SCC - 1 + SEQ], b[:, 0:SEQ - HALF], cgT[:, k, HALF:SEQ], ALU.mult))
            dve.tensor_tensor(cxd[:, k, :, SCC - 1], b[:, SEQ - HALF:HALF], cgT[:, k, SEQ:TOK], ALU.mult)\
                .then_inc(dve_bank_free, 1)
        dve.wait_ge(dve_bank_free, nv[0])
        dve.wait_ge(scalar_dmas, 16 * 9)
        dve.sem_inc(conv_steps, 1)
        for k in range(KD):
            o = PRM["sconv"] + k * SCC
            for dst, src in ((cvT[:, k, 0:SEQ], lambda i: cxp[:, k, i:i + SEQ]), (cvT[:, k, SEQ:TOK], lambda i: cxd[:, k, :, i])):
                step(dve.tensor_scalar(dst, src(0), prm[:, o:o + 1], None, ALU.mult))
                for i in range(1, SCC):
                    step(dve.scalar_tensor_tensor(dst, src(i), prm[:, o + i:o + i + 1], dst, ALU.mult, ALU.add))
        dve.wait_ge(act_bank_free, A_BG)
        step(dve.tensor_tensor(cat[:, :, :], cvT, bgT, ALU.mult))
        dve.sem_inc(mixer_steps, 1)
        add_out()
        peer(1)
        norm(range(DT))


def blocks(w, first=0, n=None):
    return np.ascontiguousarray(w.reshape(KD, P, -1, BLK).transpose(2, 1, 0, 3))


def chan(a, nb):
    a = a.reshape(*a.shape[:-1], nb, P)
    return np.ascontiguousarray(np.moveaxis(a, (-1, -2), (0, 1)))


def blockdiag(w):
    out = np.zeros((P, RB, P), w.dtype)
    h = P // 2
    for c in range(RB):
        out[:h, c, :h] = w[2 * c]
        out[h:, c, h:] = w[2 * c + 1]
    return out


OUTS = {"y_prompt": [SEQ, D], "y_sample": [DEC, D], "k_prompt": [SEQ, AW], "v_prompt": [SEQ, AW],
        "k_sample": [DEC, AW], "v_sample": [DEC, AW], "hs": [P, RB, DEC + 1], "rgp": [P, RB, RGC - 1],
        "rgs": [P, RB, DEC, RGC - 1], "scp": [P, KD, SCC - 1], "scs": [P, KD, DEC, SCC - 1]}


def kernel(**a):
    import concourse.bacc as bacc
    from concourse.bass_utils import run_bass_kernel_spmd

    a = {k: np.asarray(v) for k, v in a.items()}
    f = {
        "x_prompt": a["x_prompt"][0], "x_sample": a["x_sample"][:, 0],
        "cache_k": a["cache_k"][0].reshape(-1, SUB * AW), "cache_v": a["cache_v"][0].reshape(-1, SUB * AW),
        "page_table": a["page_table"].reshape(DEC * NG, PG).T, "rel_bias": a["rel_bias"],
        "gain0": a["norm_mix"][0:1], "gain1": a["norm_ffn"][0:1], "gain2": a["norm_mix"][1:2],
        "gain3": a["norm_ffn"][1:2], "gain4": a["norm_final"].reshape(1, D),
        "w_in_a": blocks(a["w_in_a"][0]), "w_out_a": blocks(a["w_out_a"][0]), "w_in_c": blocks(a["w_in_c"][0]),
        "w_out_c": blocks(a["w_out_c"][0]), "wq0": blocks(a["peer_wq"][0]), "wq1": blocks(a["peer_wq"][1]),
        "lambda_q1": a["lambda_q1"], "lambda_k1": a["lambda_k1"], "lambda_q2": a["lambda_q2"],
        "lambda_k2": a["lambda_k2"],
        "wa_bd": blockdiag(a["rg_wa"][0]), "wi_bd": blockdiag(a["rg_wi"][0]),
        "h0": chan(a["state_rglru_h"][0], RB),
        "rgbuf": chan(a["state_rglru_conv"][0], RB), "sbuf0": chan(a["state_sconv"][0], KD),
    }
    prm = np.zeros((P, NPRM), np.float32)
    prm[:, 0:16] = chan(a["rg_conv_w"][0], RB).reshape(P, -1)
    prm[:, 16:20] = chan(a["rg_conv_b"][0], RB)
    prm[:, 20:24] = chan(a["rg_ba"][0], RB)
    prm[:, 24:28] = chan(a["rg_bi"][0], RB)
    prm[:, 28:32] = chan(a["rg_lambda"][0], RB)
    prm[:, 32] = a["subln_g"][0]
    prm[:, 33:] = chan(a["sc_conv_w"][0], KD).reshape(P, -1)
    f["prm"] = prm
    for l in range(2):
        f[f"keys{l}"] = a["peer_keys"][l].transpose(3, 0, 1, 2).reshape(P, HC, NKEY)
        f[f"peer_u{l}"] = a["peer_u"][l]
        f[f"peer_ut{l}"] = a["peer_u"][l].reshape(NCH, P, KD, P).transpose(0, 3, 2, 1).reshape(NCH * P, KD, P)
        f[f"peer_v{l}"] = a["peer_v"][l]
    f.update(shape_constants())
    f["c_mask"] = np.full((1, HEADS), MASK, np.float32)

    nc = bacc.Bacc("TRN2", target_bir_lowering=False, num_devices=1)
    arrays, ins, outs = {}, {}, {}
    for name, v in f.items():
        v = np.ascontiguousarray(v)
        arrays[name + "_in"] = v
        ins[name] = nc.dram_tensor(name + "_in", v.shape, mybir.dt.from_np(v.dtype), kind="ExternalInput").ap()
    ins["skew"] = nc.dram_tensor("skew", [HEADS, P, SEQ + P - 1], F32).ap()
    for name, shape in OUTS.items():
        outs[name] = nc.dram_tensor(name, shape, F32, kind="ExternalOutput").ap()
    build(nc, ins, outs)
    r = run_bass_kernel_spmd(nc, [arrays], core_ids=[0]).results[0]

    def back(v):
        v = np.moveaxis(v, (0, 1), (-1, -2))
        return np.ascontiguousarray(v.reshape(*v.shape[:-2], -1))

    kv = lambda v: v.reshape(1, 1, SEQ, HEADS, P)
    kvs = lambda v: v.reshape(1, DEC, 1, HEADS, P)
    h = back(r["hs"])
    return (r["y_prompt"].reshape(1, SEQ, D), r["y_sample"].reshape(DEC, 1, D), kv(r["k_prompt"]), kv(r["v_prompt"]),
            kvs(r["k_sample"]), kvs(r["v_sample"]), h[0:1].reshape(1, 1, AW), h[1:].reshape(1, DEC, AW),
            back(r["rgp"]).reshape(1, 1, RGC - 1, AW), back(r["rgs"]).reshape(1, DEC, RGC - 1, AW),
            back(r["scp"]).reshape(1, 1, SCC - 1, D), back(r["scs"]).reshape(1, DEC, SCC - 1, D))
```
